# Optimizing a Trainium2 kernel written in Bass

```python
import jax, jax.numpy as jnp
from jax import lax
import numpy as np

D_MODEL = 1024
BATCH = 1
SEQ = 128
DEPTH = 2
DEC_BATCH = 1
DEC_SEQ = 128
PAST_LEN = 128

GRID_W = 64
ROPE_BASE = 10000.0
HEAD_DIM = 64
A_HEADS = 6
A_KV_HEADS = 2
A_GROUP = A_HEADS // A_KV_HEADS
WINDOW = 128
WBLK = 128
B_HEADS = 4
NA_KH = 8
NA_KW = 16
C_HEADS = 6
C_Q_RANK = 256
C_KV_RANK = 128
C_NOPE = 64
C_ROPE = 32
C_V = 64
MIX_W = (A_HEADS + B_HEADS + C_HEADS) * HEAD_DIM
IN_WIDTHS = (A_HEADS * HEAD_DIM, A_KV_HEADS * HEAD_DIM, A_KV_HEADS * HEAD_DIM,
             B_HEADS * HEAD_DIM, B_HEADS * HEAD_DIM, B_HEADS * HEAD_DIM,
             C_Q_RANK, C_KV_RANK, C_ROPE)
IN_COLS = sum(IN_WIDTHS)
HEAD_SCALE = HEAD_DIM ** -0.5
C_SCALE = (C_NOPE + C_ROPE) ** -0.5
QBLK = 128
N_EXPERTS = 64
TOP_K = 6
MOE_GROUPS = 8
MOE_TOPK_GROUPS = 4
D_EXPERT = 256
D_SHARED = 256
ROUTED_SCALE = 2.5
MOE_BLK = 128
NEG = -1e30
EPS = 1e-6

kernel_name = "hybrid_dit_prefix_step"

def rms_norm(x, g):
    xf = x.astype(jnp.float32)
    y = xf * lax.rsqrt(jnp.mean(xf * xf, axis=-1, keepdims=True) + EPS)
    return (y * g.astype(jnp.float32)).astype(x.dtype)

def modulation(cvec, w_ada, b_ada):
    m = jax.nn.silu(cvec) @ w_ada + b_ada
    return jnp.split(m[..., None, :], 6, axis=-1)

def split_projection(z):
    B, N, _ = z.shape
    offs = list(np.cumsum(IN_WIDTHS)[:-1])
    qa, ka, va, qb, kb, vb, cq, ckv, kr = jnp.split(z, offs, axis=-1)
    qa = qa.reshape(B, N, A_HEADS, HEAD_DIM)
    ka = ka.reshape(B, N, A_KV_HEADS, HEAD_DIM)
    va = va.reshape(B, N, A_KV_HEADS, HEAD_DIM)
    qb = qb.reshape(B, N, B_HEADS, HEAD_DIM)
    kb = kb.reshape(B, N, B_HEADS, HEAD_DIM)
    vb = vb.reshape(B, N, B_HEADS, HEAD_DIM)
    return qa, ka, va, qb, kb, vb, cq, ckv, kr

def axial_rope_tables(n_tokens, rot_dim):
    t = jnp.arange(n_tokens)
    row = (t // GRID_W).astype(jnp.float32)
    col = (t % GRID_W).astype(jnp.float32)
    n_freq = rot_dim // 4
    inv = ROPE_BASE ** (-jnp.arange(n_freq, dtype=jnp.float32) / n_freq)
    ang = jnp.concatenate([row[:, None] * inv, col[:, None] * inv], axis=-1)
    return jnp.cos(ang), jnp.sin(ang)

def apply_rope(x, cos, sin):
    xf = x.astype(jnp.float32)
    x1, x2 = jnp.split(xf, 2, axis=-1)
    c = cos[None, :, None, :]
    s = sin[None, :, None, :]
    return jnp.concatenate([x1 * c - x2 * s, x2 * c + x1 * s], axis=-1).astype(x.dtype)

def repeat_kv(k):
    return jnp.repeat(k, A_GROUP, axis=2)

def softmax_f32(s):
    return jax.nn.softmax(s, axis=-1)

def dense_attention(q, k, v, scale, sink=None):
    B, Nq, H, dq = q.shape
    dv = v.shape[-1]
    nb = Nq // QBLK
    qb = jnp.moveaxis(q.reshape(B, nb, QBLK, H, dq), 1, 0)

    def one_block(qi):
        s = jnp.einsum('bqhd,bkhd->bhqk', qi, k, preferred_element_type=jnp.float32) * scale
        if sink is None:
            p = softmax_f32(s)
        else:
            s_sink = jnp.broadcast_to(sink.astype(jnp.float32)[None, :, None, None], s.shape[:-1] + (1,))
            p = softmax_f32(jnp.concatenate([s, s_sink], axis=-1))[..., :-1]
        return jnp.einsum('bhqk,bkhd->bqhd', p.astype(v.dtype), v)

    o = lax.map(one_block, qb)
    return jnp.moveaxis(o, 0, 1).reshape(B, Nq, H, dv)

def window_attention(q, k, v, kc, vc, sink):
    B, N, H, d = q.shape
    L = kc.shape[1]
    nb = N // WBLK
    pad = ((0, 0), (WBLK, WBLK), (0, 0), (0, 0))
    kp = jnp.pad(k, pad)
    vp = jnp.pad(v, pad)
    idx = jnp.arange(nb)[:, None] * WBLK + jnp.arange(3 * WBLK)[None, :]
    kb = kp[:, idx]
    vb = vp[:, idx]
    qb = q.reshape(B, nb, WBLK, H, d)
    qpos = jnp.arange(nb)[:, None] * WBLK + jnp.arange(WBLK)[None, :]
    kpos = idx - WBLK
    kp3 = kpos[:, None, :]
    valid = (jnp.abs(kp3 - qpos[:, :, None]) <= WINDOW) & (kp3 >= 0) & (kp3 < N)
    s_loc = jnp.einsum('bnqhd,bnkhd->bnhqk', qb, kb, preferred_element_type=jnp.float32) * HEAD_SCALE
    s_loc = jnp.where(valid[None, :, None], s_loc, NEG)
    s_ctx = jnp.einsum('bnqhd,blhd->bnhql', qb, kc, preferred_element_type=jnp.float32) * HEAD_SCALE
    s_sink = jnp.broadcast_to(sink.astype(jnp.float32)[None, None, :, None, None], s_loc.shape[:-1] + (1,))
    p = softmax_f32(jnp.concatenate([s_loc, s_ctx, s_sink], axis=-1)).astype(v.dtype)
    p_loc = p[..., :3 * WBLK]
    p_ctx = p[..., 3 * WBLK:3 * WBLK + L]
    o = (jnp.einsum('bnhqk,bnkhd->bnqhd', p_loc, vb)
         + jnp.einsum('bnhql,blhd->bnqhd', p_ctx, vc))
    return o.reshape(B, N, H, d)

def neighborhood_attention(q, k, v, kc, vc, rpb):
    B, N, H, d = q.shape
    rows = N // GRID_W
    kh = min(NA_KH, rows)
    r = jnp.arange(rows)
    rs = jnp.clip(r - kh // 2, 0, rows - kh)
    row_idx = rs[:, None] + jnp.arange(kh)[None, :]
    K = kh * GRID_W
    kg = k.reshape(B, rows, GRID_W, H, d)[:, row_idx].reshape(B, rows, K, H, d)
    vg = v.reshape(B, rows, GRID_W, H, d)[:, row_idx].reshape(B, rows, K, H, d)
    qg = q.reshape(B, rows, GRID_W, H, d)
    col = jnp.arange(GRID_W)
    cs = jnp.clip(col - NA_KW // 2, 0, GRID_W - NA_KW)
    key_col = jnp.tile(col, kh)
    key_row = jnp.repeat(row_idx, GRID_W, axis=1)
    col_ok = (key_col[None, :] >= cs[:, None]) & (key_col[None, :] < cs[:, None] + NA_KW)
    dr = key_row - r[:, None] + (NA_KH - 1)
    dc = jnp.clip(key_col[None, :] - col[:, None], -(NA_KW - 1), NA_KW - 1) + (NA_KW - 1)
    bias = rpb[:, dr[:, None, :], dc[None, :, :]]
    bias = jnp.moveaxis(bias, 0, 1)[None].astype(jnp.float32)
    s_loc = jnp.einsum('brqhd,brkhd->brhqk', qg, kg, preferred_element_type=jnp.float32) * HEAD_SCALE + bias
    s_loc = jnp.where(col_ok[None, None, None], s_loc, NEG)
    s_ctx = jnp.einsum('brqhd,blhd->brhql', qg, kc, preferred_element_type=jnp.float32) * HEAD_SCALE
    p = softmax_f32(jnp.concatenate([s_loc, s_ctx], axis=-1)).astype(v.dtype)
    o = (jnp.einsum('brhqk,brkhd->brqhd', p[..., :K], vg)
         + jnp.einsum('brhql,blhd->brqhd', p[..., K:], vc))
    return o.reshape(B, N, H, d)

def mla_query(cq, p):
    B, N, _ = cq.shape
    return (rms_norm(cq, p['c_q_norm_g']) @ p['c_w_uq']).reshape(B, N, C_HEADS, C_NOPE + C_ROPE)

def mla_keys(ckv_n, kr, p):
    B, N, _ = ckv_n.shape
    kv = (ckv_n @ p['c_w_ukv']).reshape(B, N, C_HEADS, C_NOPE + C_V)
    k_nope, v = kv[..., :C_NOPE], kv[..., C_NOPE:]
    k = jnp.concatenate([k_nope, jnp.broadcast_to(kr[:, :, None, :], (B, N, C_HEADS, C_ROPE))], axis=-1)
    return k, v

def swiglu(x, wg, wu, wd):
    return (jax.nn.silu(x @ wg) * (x @ wu)) @ wd

def route(xf, router_w, router_bias):
    T = xf.shape[0]
    scores = jax.nn.sigmoid((xf @ router_w).astype(jnp.float32))
    sel = scores + router_bias.astype(jnp.float32)
    per = N_EXPERTS // MOE_GROUPS
    grp_score = lax.top_k(sel.reshape(T, MOE_GROUPS, per), 2)[0].sum(-1)
    _, gidx = lax.top_k(grp_score, MOE_TOPK_GROUPS)
    gmask = jnp.any(gidx[:, :, None] == jnp.arange(MOE_GROUPS)[None, None, :], axis=1)
    sel = jnp.where(jnp.repeat(gmask, per, axis=1), sel, NEG)
    _, top_idx = lax.top_k(sel, TOP_K)
    w = jnp.take_along_axis(scores, top_idx, axis=-1)
    w = w / jnp.sum(w, axis=-1, keepdims=True) * ROUTED_SCALE
    return top_idx, w

def moe_ffn(h, p):
    B, N, D = h.shape
    T = B * N
    xf = h.reshape(T, D)
    top_idx, top_w = route(xf, p['router_w'], p['router_bias'])
    M = T * TOP_K
    flat_e = top_idx.reshape(M)
    flat_tok = jnp.arange(M, dtype=jnp.int32) // TOP_K
    order = jnp.argsort(flat_e)
    e_s = flat_e[order]
    tok_s = flat_tok[order]
    w_s = top_w.reshape(M)[order].astype(h.dtype)
    counts = jnp.zeros((N_EXPERTS,), jnp.int32).at[flat_e].add(1)
    padded = (counts + MOE_BLK - 1) // MOE_BLK * MOE_BLK
    pad_end = jnp.cumsum(padded)
    pad_start = pad_end - padded
    start = jnp.cumsum(counts) - counts
    dest = pad_start[e_s] + jnp.arange(M, dtype=jnp.int32) - start[e_s]
    n_blocks = -(-M // MOE_BLK) + N_EXPERTS
    row_tok = jnp.zeros((n_blocks * MOE_BLK,), jnp.int32).at[dest].set(tok_s)
    block_e = jnp.minimum(
        jnp.searchsorted(pad_end, jnp.arange(n_blocks, dtype=jnp.int32) * MOE_BLK, side='right'),
        N_EXPERTS - 1)
    xb = xf[row_tok].reshape(n_blocks, MOE_BLK, D)

    def expert_block(args):
        xi, e = args
        return swiglu(xi, p['exp_w_gate'][e], p['exp_w_up'][e], p['exp_w_down'][e])

    yb = lax.map(expert_block, (xb, block_e)).reshape(n_blocks * MOE_BLK, D)
    routed = jax.ops.segment_sum(yb[dest] * w_s[:, None], tok_s, num_segments=T)
    shared = swiglu(xf, p['sh_w_gate'], p['sh_w_up'], p['sh_w_down'])
    return (routed + shared).reshape(B, N, D)

def ffn_sublayer(x, sh2, sc2, g2, p):
    h2 = rms_norm(x, p['norm2_g']) * (1 + sc2) + sh2
    return x + g2 * moe_ffn(h2, p)

def context_layer(x, c_ctx, p):
    B, L, _ = x.shape
    sh1, sc1, g1, sh2, sc2, g2 = modulation(c_ctx, p['w_ada'], p['b_ada'])
    h = rms_norm(x, p['norm1_g']) * (1 + sc1) + sh1
    qa, ka, va, qb, kb, vb, cq, ckv, kr = split_projection(h @ p['w_in'])
    oa = dense_attention(qa, repeat_kv(ka), repeat_kv(va), HEAD_SCALE, sink=p['a_sink'])
    ob = dense_attention(qb, kb, vb, HEAD_SCALE)
    qc = mla_query(cq, p)
    ckv_n = rms_norm(ckv, p['c_kv_norm_g'])
    kc, vc = mla_keys(ckv_n, kr, p)
    oc = dense_attention(qc, kc, vc, C_SCALE)
    o = jnp.concatenate([oa.reshape(B, L, -1), ob.reshape(B, L, -1), oc.reshape(B, L, -1)], axis=-1)
    x = x + g1 * (o @ p['w_out'])
    x = ffn_sublayer(x, sh2, sc2, g2, p)
    return x, ka, va, kb, vb, ckv_n, kr

def latent_layer(x, cvec, ctx_ak, ctx_av, ctx_bk, ctx_bv, ctx_ckv, ctx_kr, p, rope64, rope32):
    B, N, _ = x.shape
    sh1, sc1, g1, sh2, sc2, g2 = modulation(cvec, p['w_ada'], p['b_ada'])
    h = rms_norm(x, p['norm1_g']) * (1 + sc1) + sh1
    qa, ka, va, qb, kb, vb, cq, ckv, kr = split_projection(h @ p['w_in'])
    qa = apply_rope(qa, *rope64)
    ka = apply_rope(ka, *rope64)
    oa = window_attention(qa, repeat_kv(ka), repeat_kv(va), repeat_kv(ctx_ak), repeat_kv(ctx_av), p['a_sink'])
    ob = neighborhood_attention(qb, kb, vb, ctx_bk, ctx_bv, p['b_rpb'])
    qc = mla_query(cq, p)
    qc = jnp.concatenate([qc[..., :C_NOPE], apply_rope(qc[..., C_NOPE:], *rope32)], axis=-1)
    kr_rot = apply_rope(kr[:, :, None, :], *rope32)[:, :, 0, :]
    k_lat, v_lat = mla_keys(rms_norm(ckv, p['c_kv_norm_g']), kr_rot, p)
    k_ctx, v_ctx = mla_keys(ctx_ckv, ctx_kr, p)
    oc = dense_attention(qc, jnp.concatenate([k_lat, k_ctx], axis=1),
                         jnp.concatenate([v_lat, v_ctx], axis=1), C_SCALE)
    o = jnp.concatenate([oa.reshape(B, N, -1), ob.reshape(B, N, -1), oc.reshape(B, N, -1)], axis=-1)
    x = x + g1 * (o @ p['w_out'])
    return ffn_sublayer(x, sh2, sc2, g2, p)

def setup_inputs(seed: int = 0) -> dict:
    key = jax.random.key(seed)
    ks = jax.random.split(key, 31)
    D = D_MODEL

    def nrm(k, shape, s):
        return jax.random.normal(k, shape, jnp.float32) * s

    return {
        "x_prompt": nrm(ks[0], (BATCH, SEQ, D), 1.0),
        "x_sample": nrm(ks[1], (DEC_BATCH, DEC_SEQ, D), 1.0),
        "cache_a_k": nrm(ks[2], (DEC_BATCH, DEPTH, PAST_LEN, A_KV_HEADS, HEAD_DIM), 1.0),
        "cache_a_v": nrm(ks[3], (DEC_BATCH, DEPTH, PAST_LEN, A_KV_HEADS, HEAD_DIM), 1.0),
        "cache_b_k": nrm(ks[4], (DEC_BATCH, DEPTH, PAST_LEN, B_HEADS, HEAD_DIM), 1.0),
        "cache_b_v": nrm(ks[5], (DEC_BATCH, DEPTH, PAST_LEN, B_HEADS, HEAD_DIM), 1.0),
        "cache_c_kv": nrm(ks[6], (DEC_BATCH, DEPTH, PAST_LEN, C_KV_RANK), 1.0),
        "cache_c_krope": nrm(ks[7], (DEC_BATCH, DEPTH, PAST_LEN, C_ROPE), 1.0),
        "c": nrm(ks[8], (DEC_BATCH, D), 1.0),
        "c_ctx": nrm(ks[9], (D,), 1.0),
        "norm1_g": 1.0 + nrm(ks[10], (DEPTH, D), 0.05),
        "norm2_g": 1.0 + nrm(ks[11], (DEPTH, D), 0.05),
        "w_ada": nrm(ks[12], (DEPTH, D, 6 * D), 0.5 * D ** -0.5),
        "b_ada": nrm(ks[13], (DEPTH, 6 * D), 0.02),
        "w_in": nrm(ks[14], (DEPTH, D, IN_COLS), D ** -0.5),
        "a_sink": nrm(ks[15], (DEPTH, A_HEADS), 0.5),
        "b_rpb": nrm(ks[16], (DEPTH, B_HEADS, 2 * NA_KH - 1, 2 * NA_KW - 1), 0.2),
        "c_q_norm_g": 1.0 + nrm(ks[17], (DEPTH, C_Q_RANK), 0.05),
        "c_w_uq": nrm(ks[18], (DEPTH, C_Q_RANK, C_HEADS * (C_NOPE + C_ROPE)), C_Q_RANK ** -0.5),
        "c_kv_norm_g": 1.0 + nrm(ks[19], (DEPTH, C_KV_RANK), 0.05),
        "c_w_ukv": nrm(ks[20], (DEPTH, C_KV_RANK, C_HEADS * (C_NOPE + C_V)), C_KV_RANK ** -0.5),
        "w_out": nrm(ks[21], (DEPTH, MIX_W, D), MIX_W ** -0.5),
        "router_w": nrm(ks[22], (DEPTH, D, N_EXPERTS), D ** -0.5),
        "router_bias": nrm(ks[23], (DEPTH, N_EXPERTS), 0.01),
        "exp_w_gate": nrm(ks[24], (DEPTH, N_EXPERTS, D, D_EXPERT), D ** -0.5),
        "exp_w_up": nrm(ks[25], (DEPTH, N_EXPERTS, D, D_EXPERT), D ** -0.5),
        "exp_w_down": nrm(ks[26], (DEPTH, N_EXPERTS, D_EXPERT, D), D_EXPERT ** -0.5),
        "sh_w_gate": nrm(ks[27], (DEPTH, D, D_SHARED), D ** -0.5),
        "sh_w_up": nrm(ks[28], (DEPTH, D, D_SHARED), D ** -0.5),
        "sh_w_down": nrm(ks[29], (DEPTH, D_SHARED, D), D_SHARED ** -0.5),
        "final_norm_g": 1.0 + nrm(ks[30], (D,), 0.05),
    }

def reference(x_prompt, x_sample, cache_a_k, cache_a_v, cache_b_k, cache_b_v, cache_c_kv, cache_c_krope,
              c, c_ctx, norm1_g, norm2_g, w_ada, b_ada, w_in, a_sink, b_rpb, c_q_norm_g, c_w_uq,
              c_kv_norm_g, c_w_ukv, w_out, router_w, router_bias, exp_w_gate, exp_w_up, exp_w_down,
              sh_w_gate, sh_w_up, sh_w_down, final_norm_g):
    n_lat = x_sample.shape[1]
    rope64 = axial_rope_tables(n_lat, HEAD_DIM)
    rope32 = axial_rope_tables(n_lat, C_ROPE)
    xp = x_prompt
    xs = x_sample
    ak, av, bk, bv, ckv_l, kr_l = [], [], [], [], [], []
    for l in range(DEPTH):
        p = {
            'norm1_g': norm1_g[l], 'norm2_g': norm2_g[l], 'w_ada': w_ada[l], 'b_ada': b_ada[l],
            'w_in': w_in[l], 'a_sink': a_sink[l], 'b_rpb': b_rpb[l],
            'c_q_norm_g': c_q_norm_g[l], 'c_w_uq': c_w_uq[l],
            'c_kv_norm_g': c_kv_norm_g[l], 'c_w_ukv': c_w_ukv[l], 'w_out': w_out[l],
            'router_w': router_w[l], 'router_bias': router_bias[l],
            'exp_w_gate': exp_w_gate[l], 'exp_w_up': exp_w_up[l], 'exp_w_down': exp_w_down[l],
            'sh_w_gate': sh_w_gate[l], 'sh_w_up': sh_w_up[l], 'sh_w_down': sh_w_down[l],
        }
        xp, ka, va, kb, vb, ckv_n, kr = context_layer(xp, c_ctx, p)
        ak.append(ka); av.append(va); bk.append(kb); bv.append(vb); ckv_l.append(ckv_n); kr_l.append(kr)
        xs = latent_layer(xs, c, cache_a_k[:, l], cache_a_v[:, l], cache_b_k[:, l], cache_b_v[:, l],
                          cache_c_kv[:, l], cache_c_krope[:, l], p, rope64, rope32)
    y_prompt = rms_norm(xp, final_norm_g)
    y_sample = rms_norm(xs, final_norm_g)
    new_a_k = jnp.stack(ak, axis=1)
    new_a_v = jnp.stack(av, axis=1)
    new_b_k = jnp.stack(bk, axis=1)
    new_b_v = jnp.stack(bv, axis=1)
    new_c_kv = jnp.stack(ckv_l, axis=1)
    new_c_krope = jnp.stack(kr_l, axis=1)
    return (y_prompt, y_sample, new_a_k, new_a_v, new_b_k, new_b_v, new_c_kv, new_c_krope)


_drawn_inputs = setup_inputs


def setup_inputs(seed=0):
    import zlib

    import numpy as np

    out = dict(_drawn_inputs(seed))
    spreads = {}
    factors = {'a_sink': 8.0, 'b_rpb': 3.05, 'c_q_norm_g': 3.826}
    for name, (base, spread) in spreads.items():
        noise = np.random.default_rng([zlib.crc32(name.encode()), seed]).standard_normal(out[name].shape)
        drawn = base * np.exp(spread * noise) if base else spread * noise
        out[name] = __import__('jax').numpy.asarray(drawn.astype(out[name].dtype))
    for name, factor in factors.items():
        out[name] = (out[name] * factor).astype(out[name].dtype)
    return out
```

```python
from contextlib import ExitStack

import numpy as np
import concourse.bass as bass
from concourse import mybir

F32 = mybir.dt.float32
I32 = mybir.dt.int32
ALU = mybir.AluOpType
ACT = mybir.ActivationFunctionType
AX = mybir.AxisListType

P = 128
DEPTH, D, T = 2, 1024, 128
KD = D // P
NG = 2
HD, NH = 64, 16
A_H, A_KV, B_H, C_H = 6, 2, 4, 6
A_GROUP = A_H // A_KV
CQ, CKV, CR, CN = 256, 128, 32, 64
CD = CN + CR
WIDTHS = (A_H * HD, A_KV * HD, A_KV * HD, B_H * HD, B_H * HD, B_H * HD, CQ, CKV, CR)
OFF = [sum(WIDTHS[:i]) for i in range(len(WIDTHS) + 1)]
O_QA, O_KA, O_VA, O_QB, O_KB, O_VB, O_CQ, O_CKV, O_KR, IN_COLS = OFF
NZ = IN_COLS // 4
HEAD_SCALE = HD ** -0.5
C_SCALE = CD ** -0.5
GRID_W, NA_KH, NA_KW = 64, 8, 16
ROWS = T // GRID_W
EPS = 1e-6
NEG = -1e30
E, TOP_K, GROUPS, TOP_G, DE = 64, 6, 8, 4, 256
PER = E // GROUPS
ROUTED_SCALE = 2.5
CAP = 64
PAIRS = E // 2
XU = 32
XP_MAX = 12
NU = E + XU
SLOT = 6144
NSLOT = 4
KEYT = 3
KH = A_KV + B_H + C_H
BW = GRID_W + 2 * (NA_KW - 1)
BB = 6144
RPB_R, RPB_C = 2 * NA_KH - 1, 2 * NA_KW - 1

V_B, V_N1, V_N2, V_QG, V_C, V_F, V_ROWS = 0, 48, 56, 64, 66, 82, 90

C_ROT64, C_ROT32, C_MASK, C_ID, C_UP = 0, 64, 96, 224, 352
C_CUM, C_TIE, C_SLOT, C_PART, C_EVEN, C_COLS = 480, 608, 672, 736, 737, 753


def constants():
    t = np.arange(T)
    row, col = (t // GRID_W).astype(np.float32), (t % GRID_W).astype(np.float32)
    k = np.zeros((P, C_COLS), np.float32)
    for at, dim in ((C_ROT64, HD), (C_ROT32, CR)):
        n = dim // 4
        inv = (np.float32(10000.0) ** (-np.arange(n, dtype=np.float32) / np.float32(n))).astype(np.float32)
        ang = np.concatenate([row[:, None] * inv, col[:, None] * inv], axis=-1).astype(np.float32)
        k[:, at:at + dim // 2] = np.cos(ang)
        k[:, at + dim // 2:at + dim] = np.sin(ang)
    start = np.clip(np.arange(GRID_W) - NA_KW // 2, 0, GRID_W - NA_KW)
    c = t % GRID_W
    inside = (c[None, :] >= start[c][:, None]) & (c[None, :] < start[c][:, None] + NA_KW)
    k[:, C_MASK:C_MASK + T] = np.where(inside, 0.0, NEG)
    k[:, C_ID:C_ID + P] = np.eye(P)
    k[:, C_UP:C_UP + P] = np.triu(np.ones((P, P)), 1)
    k[:E, C_CUM:C_CUM + E] = np.triu(np.ones((E, E)))
    k[:E, C_CUM + E:C_CUM + 2 * E] = np.triu(np.ones((E, E)), 1)
    k[:, C_TIE:C_TIE + 64] = np.tril(np.ones((GROUPS, GROUPS)), -1).reshape(1, 64)
    k[:, C_SLOT:C_SLOT + CAP] = np.arange(1, CAP + 1)
    k[:, C_PART] = np.arange(P)
    k[:, C_EVEN:C_EVEN + 16] = 2 * np.arange(16)
    return k


def backbone(nc, I, consts, skew, O):
    y_prompt, y_sample, new_ak, new_av, new_bk, new_bv, new_ckv, new_kr = O
    ctx = ExitStack()
    with ctx:
        def sb(name, shape, dt=F32):
            return ctx.enter_context(nc.sbuf_tensor(name, shape, dt))

        def carve(buf):
            at = [0]

            def view(shape, parts=P):
                n = int(np.prod(shape))
                v = buf[0:parts, at[0]:at[0] + n]
                at[0] += n
                assert at[0] <= buf.shape[1]
                if len(shape) == 1:
                    return v
                names = "abcd"[:len(shape)]
                return v.rearrange(f"p ({' '.join(names)}) -> p {' '.join(names)}", **dict(zip(names, shape)))
            return view

        def sem(name):
            return ctx.enter_context(nc.semaphore(name))

        ring = sb("ring", [P, NSLOT, SLOT])
        xt = sb("xt", [P, KD, NG * T])
        ht = sb("ht", [P, KD, NG * T])
        wide = sb("wide", [P, NG, D])
        z = sb("z", [P, NG, IN_COLS])
        h2 = z[:, :, 0:D]
        tbl = sb("tbl", [P, C_COLS])
        ones = sb("ones", [P, P])
        mhalf = sb("mhalf", [P, NG * T])
        vec_rows = sb("vec_rows", [V_ROWS, P])
        cols = sb("cols", [P, V_ROWS])
        csilu = sb("csilu", [P, KD, NG])
        ctanh = sb("ctanh", [P, NG, KD])
        mod = sb("mod", [P, 48, NG])
        gs1 = sb("gs1", [P, KD, NG])
        gs2 = sb("gs2", [P, KD, NG])
        ms = sb("ms", [P, NG * T])
        rs = sb("rs", [P, NG * T])
        w_uq = sb("w_uq", [P, 2, C_H * CD])
        w_ukv = sb("w_ukv", [P, C_H * 2 * HD])
        w_router = sb("w_router", [P, KD, E])
        rbias = sb("rbias", [P, E])
        kvg = sb("kvg", [P, CKV])
        sink = sb("sink", [P, NH])
        nsink = sb("nsink", [P, NH])
        cache = sb("cache", [P, 2 * A_KV * HD + 2 * B_H * HD + CKV + CR])
        bias_b = sb("bias_b", [P, B_H, T])
        st = sb("st", [P, 4])
        rst = sb("rst", [P, 4])
        kc_buf = sb("kc_buf", [P, KEYT * C_H * CD])
        vc_buf = sb("vc_buf", [P, KEYT * C_H * HD])
        qt_buf = sb("qt_buf", [P, NH * T])
        kt_buf = sb("kt_buf", [P, KEYT * KH * T])
        pr_buf = sb("pr_buf", [P, 2 * 512])
        kc = carve(kc_buf)([KEYT, C_H, CD])
        vc = carve(vc_buf)([KEYT, C_H, HD])
        qt = carve(qt_buf)([NH, T])
        kt = carve(kt_buf)([KEYT, KH, T])
        pr = carve(pr_buf)([2, 512])
        rtmp = carve(pr_buf)([4, 256])
        lat = carve(ht[:].rearrange("p a b -> p (a b)"))
        cqt = lat([2, NG, T])
        ckvt = lat([KEYT, T])
        qc = lat([NG, C_H, CD])
        pt = sb("pt", [P, 2, 512])
        nmax = sb("nmax", [P, NH])
        sums = sb("sums", [P, NH])
        esink = sb("esink", [P, NH])
        rden = sb("rden", [P, NH])
        route_view, plan_view = carve(kc_buf), carve(vc_buf)
        score = route_view([NG, E])
        selv = route_view([NG, E])
        repl = route_view([NG, E])
        mask = route_view([NG, E])
        top8 = route_view([NG, GROUPS, 8])
        gsc = route_view([NG, GROUPS])
        cmp1 = route_view([NG, GROUPS, GROUPS])
        cmp2 = route_view([NG, GROUPS, GROUPS])
        rank = route_view([NG, GROUPS])
        t8 = route_view([NG, 8])
        wsum = route_view([NG])
        pos1 = route_view([NG, NU])
        wu = route_view([NG, NU])
        cnt = plan_view([4], E)
        nbb = plan_view([P], E)
        cum = plan_view([2 * E], XU)
        fin = plan_view([E], XU)
        inr = plan_view([E], XU)
        ns = plan_view([E], XU)
        uv = plan_view([4], XU)
        oneh = plan_view([XU], E)
        diag = plan_view([2 * XU], XU)
        urow = plan_view([2 * XU])
        xexp = sb("xexp", [1, XU], I32)
        xcount = sb("xcount", [1, 2])
        xpairs = sb("xpairs", [1, 1], I32)
        moe_view = carve(kt_buf)
        pick = moe_view([NG, 2 * CAP])
        pickw = moe_view([NG, 2 * CAP])
        xg = moe_view([KD, 2 * CAP])
        th = moe_view([DE])
        a1 = moe_view([DE])
        act_ = moe_view([NG, DE])
        sa = moe_view([512])
        ysb = moe_view([D])
        sht = moe_view([2, NG * T])

        ps = ctx.enter_context(nc.psum_tensor("ps", [P, 8, 512], F32))
        ident = tbl[:, C_ID:C_ID + P]
        xview = ps[:, 0:4, :].rearrange("p b (c n) -> p (b c) n", c=2)

        cache_ak, cache_av = cache[:, 0:128], cache[:, 128:256]
        cache_bk, cache_bv = cache[:, 256:512], cache[:, 512:768]
        cache_ckv, cache_kr = cache[:, 768:896], cache[:, 896:928]

        MISC = 14
        slot_of = [(2 + i) % NSLOT for i in range(MISC)]
        ADA, WIN, WOUT, SHARED = range(0, 8), range(8, 11), range(11, 13), 13

        s_const = sem("s_const")
        s_x = sem("s_x")
        s_vec = sem("s_vec")
        s_small = sem("s_small")
        s_skew0, s_skew1, s_bias = sem("s_skew0"), sem("s_skew1"), sem("s_bias")
        s_zero = sem("s_zero")
        s_misc = [sem(f"s_misc{i}") for i in range(MISC)]
        s_exp = [sem(f"s_exp{q}") for q in range(NSLOT)]
        s_xw = sem("s_xw")
        s_out = sem("s_out")
        s_sp = sem("s_sp")
        s_set = sem("s_set")
        s_dve, s_act, s_pool = sem("s_dve"), sem("s_act"), sem("s_pool")
        names = ("xt_t", "xt_c", "vec_t", "cols_c", "ctanh", "csilu", "mod_mm", "mod", "sq", "ssq", "ms", "rs",
                 "hn", "ht_d", "ht_a", "z_mm", "z_d", "z_a", "stat_d", "stat_a", "stat_r", "lat_d", "kcq_t",
                 "kcq_c", "qkv_mm", "qkv_c", "rope", "qk_t", "qk_d", "qk_a", "s_mm", "nmax", "prob", "p_t", "pt_c",
                 "pv", "esum", "esink", "o", "o_t", "ot_c", "y_mm", "x1", "h2_t", "h2_d", "h2_a", "logit", "rtanh",
                 "mask", "pos_mm", "cnt_mm", "nb", "cum_mm", "inr", "one_t", "oneh", "ext_mm", "plan", "sh_mm",
                 "sh_th", "sh_a", "sh_t", "sht_c", "sh_acc", "sel", "sw", "ga", "gb", "xga", "xgb", "gu", "th", "a",
                 "tt", "sa", "y0", "y1", "ya", "yb", "low_read", "x2",
                 "fin", "fin_t", "fin_c", "cval")
        S = {n: sem("s_" + n) for n in names}

        block = ctx.enter_context(nc.Block())

        def gu_of(slot, k):
            return ring[:, slot, 0:4096].rearrange("p (g k f) -> p g k f", g=2, k=KD)[:, :, k, :]

        def down_of(slot):
            return ring[:, slot, 4096:6144].rearrange("p (k d) -> p k d", k=2)

        score_groups = [(0, h, 4) for h in range(0, NH, 4)] + [(1, h, 2) for h in range(0, NH, 2)]
        NSG = len(score_groups)

        def key_head(h):
            return h // A_GROUP if h < A_H else h - A_H + A_KV

        def value_of(h, key_tile):
            if h < A_H:
                o = HD * (h // A_GROUP)
                return cache_av[:, o:o + HD] if key_tile == 2 else z[:, key_tile, O_VA + o:O_VA + o + HD]
            if h < A_H + B_H:
                o = HD * (h - A_H)
                return cache_bv[:, o:o + HD] if key_tile == 2 else z[:, key_tile, O_VB + o:O_VB + o + HD]
            return vc[:, key_tile, h - A_H - B_H, :]

        def query_of(h, t):
            if h < A_H:
                return z[:, t, O_QA + h * HD:O_QA + (h + 1) * HD]
            if h < A_H + B_H:
                o = O_QB + (h - A_H) * HD
                return z[:, t, o:o + HD]
            return qc[:, t, h - A_H - B_H, :]

        def key_of(kh, key_tile):
            if kh < A_KV:
                return cache_ak[:, kh * HD:(kh + 1) * HD] if key_tile == 2 else \
                    z[:, key_tile, O_KA + kh * HD:O_KA + (kh + 1) * HD]
            if kh < A_KV + B_H:
                o = (kh - A_KV) * HD
                return cache_bk[:, o:o + HD] if key_tile == 2 else z[:, key_tile, O_KB + o:O_KB + o + HD]
            return kc[:, key_tile, kh - A_KV - B_H, :]

        def dim_of(h):
            return HD if h < A_H + B_H else CD

        q_sets = [[("q", t, h) for h in range(0, NH, 4)] for t in range(NG)]
        k_sets = [("k", kt_, h) for kt_ in range(KEYT) for h in range(0, KH, 4)]
        NKQ = len(k_sets) + 4
        QK_T = NKQ + 4
        QK_D0, QK_A0 = (NKQ + 1) // 2, NKQ // 2
        QK_D, QK_A = QK_D0 + 2, QK_A0 + 2

        def copy_heads(eng, sets, n, bank, on_act):
            kind, i, h0 = sets[n]
            first_c = A_H + B_H if kind == "q" else A_KV + B_H
            runs = [(a, b) for a, b in ((h0, min(h0 + 4, first_c)), (max(h0, first_c), h0 + 4)) if a < b]
            for a, b in runs:
                wide_head = a >= first_c
                d = CD if wide_head else HD
                src = ps[0:d, bank, (a - h0) * T:(b - h0) * T].rearrange("p (h n) -> p h n", n=T)
                dst = qt[0:d, a:b, :] if kind == "q" else kt[0:d, i, a:b, :]
                scale = 1.0 if kind == "k" else (C_SCALE if wide_head else HEAD_SCALE)
                if on_act:
                    last = eng.activation(dst, src, ACT.Copy, scale=scale)
                else:
                    last = eng.tensor_scalar(dst, src, scale, None, ALU.mult)
            last.then_inc(S["qk_a" if on_act else "qk_d"], 1)

        def move_tokens(eng, t, on_act):
            src = ps[:, 2 * t:2 * t + 2, :].rearrange("p h (m b) -> p h m b", b=8)
            dst = h2[:, t, :].rearrange("p (b h m) -> p h m b", b=8, h=2)
            if on_act:
                eng.activation(dst, src, ACT.Copy).then_inc(S["h2_a"], 1)
            else:
                eng.tensor_copy(dst, src).then_inc(S["h2_d"], 1)

        @block.sync
        def _(sp):
            sp.dma_start(tbl[:], consts).then_inc(s_const, 16)
            sp.dma_start(wide[:, 0, :], I["x_prompt"][0]).then_inc(s_x, 16)
            sp.dma_start(wide[:, 1, :], I["x_sample"][0]).then_inc(s_x, 16)
            done = xdone = 0
            for l in range(DEPTH):
                w_ada, w_in, w_out = I["w_ada"][l], I["w_in"][l], I["w_out"][l]
                for i in range(MISC):
                    q = slot_of[i]
                    dst = ring[:, q, :]
                    if i in (0, 1) and l:
                        sp.wait_ge(S["y1"], first_done)
                    if i in (2, 3) and l:
                        sp.wait_ge(S["y1"], done)
                    if 4 <= i < 12:
                        sp.wait_ge(S["mod_mm"], l * KD + i - 3)
                    if i >= 12:
                        sp.wait_ge(S["z_mm"], 2 * l + 2)
                    if i in ADA:
                        sp.dma_start(dst, w_ada[i * P:(i + 1) * P, :]).then_inc(s_misc[i], 16)
                    elif i in WIN:
                        k0 = 3 * (i - WIN[0])
                        nk = min(3, KD - k0)
                        sp.dma_start(dst[:, 0:nk * IN_COLS].rearrange("p (k n) -> p k n", k=nk),
                                     w_in[k0 * P:(k0 + nk) * P, :].rearrange("(k p) n -> p k n", p=P)
                                     ).then_inc(s_misc[i], 16)
                    elif i in WOUT:
                        k0 = 4 * (i - WOUT[0])
                        sp.dma_start(dst[:, 0:4 * D].rearrange("p (k n) -> p k n", k=4),
                                     w_out[k0 * P:(k0 + 4) * P, :].rearrange("(k p) n -> p k n", p=P)
                                     ).then_inc(s_misc[i], 16)
                    else:
                        for g, name in enumerate(("sh_w_gate", "sh_w_up")):
                            sp.dma_start(dst[:, g * 2048:(g + 1) * 2048].rearrange("p (k f) -> p k f", k=KD),
                                         I[name][l].rearrange("(k p) f -> p k f", p=P)).then_inc(s_misc[i], 16)
                        sp.dma_start(down_of(q), I["sh_w_down"][l].rearrange("(k p) d -> p k d", p=P)
                                     ).then_inc(s_misc[i], 16)

                def settle():
                    sp.sem_inc(s_sp, 1)

                def load_expert(e, q, landed):
                    sp.dma_start(ring[:, q, 0:2048],
                                 I["exp_w_gate"][l, e, :, :].rearrange("(p k) f -> p (k f)", k=KD)).then_inc(landed, 16)
                    sp.dma_start(ring[:, q, 2048:4096],
                                 I["exp_w_up"][l, e, :, :].rearrange("(p k) f -> p (k f)", k=KD)).then_inc(landed, 16)
                    sp.dma_start(down_of(q),
                                 I["exp_w_down"][l, e, :, :].rearrange("(k p) d -> p k d", p=P)).then_inc(landed, 16)

                sp.wait_ge(S["z_mm"], 2 * l + 2)
                load_expert(0, 0, s_exp[0])
                sp.wait_ge(S["y_mm"], 2 * l + 2)
                load_expert(1, 1, s_exp[1])
                load_expert(2, 2, s_exp[2])
                sp.wait_ge(S["sh_acc"], l + 1)
                load_expert(3, 3, s_exp[3])
                with sp.Fori(0, E // NSLOT - 1) as r:
                    for q in range(NSLOT):
                        if q % 2 == 0:
                            sp.wait_ge(S["y1"], 2 * r + (done + q // 2 + 1))
                            settle()
                        load_expert(4 * r + (NSLOT + q), q, s_exp[q])
                first_done = done + PAIRS
                sp.wait_ge(S["plan"], 2 * l + 2)
                extra = sp.value_load(xpairs[0:1, 0:1], min_val=1, max_val=XP_MAX)
                with sp.Fori(0, extra) as x:
                    e = [sp.value_load(xexp[0:1, bass.ds(2 * x + q, 1)], min_val=0, max_val=E - 1) for q in range(2)]
                    sp.wait_ge(S["low_read"], x + (xdone + PAIRS // 2 * (l + 1)))
                    settle()
                    for q in range(2):
                        load_expert(e[q], q, s_xw)
                done, xdone = extra + (done + PAIRS), extra + xdone

        @block.gpsimd
        def _(pool):
            def small_loads(l):
                for lo, src in ((V_B, I["b_ada"][l].rearrange("(r p) -> r p", p=P)),
                                (V_N1, I["norm1_g"][l].rearrange("(r p) -> r p", p=P)),
                                (V_N2, I["norm2_g"][l].rearrange("(r p) -> r p", p=P)),
                                (V_QG, I["c_q_norm_g"][l].rearrange("(r p) -> r p", p=P)),
                                (V_C, I["c_ctx"].rearrange("(r p) -> r p", p=P)),
                                (V_C + KD, I["c"][0].rearrange("(r p) -> r p", p=P)),
                                (V_F, I["final_norm_g"].rearrange("(r p) -> r p", p=P))):
                    pool.dma_start(vec_rows[lo:lo + src.shape[0], :], src).then_inc(s_vec, 16)
                for dst, src in ((w_uq[:], I["c_w_uq"][l].rearrange("(k p) n -> p k n", p=P)),
                                 (w_ukv[:], I["c_w_ukv"][l]),
                                 (w_router[:], I["router_w"][l].rearrange("(k p) n -> p k n", p=P)),
                                 (rbias[:], I["router_bias"][l:l + 1, :].to_broadcast([P, E])),
                                 (kvg[:], I["c_kv_norm_g"][l:l + 1, :].to_broadcast([P, CKV])),
                                 (sink[:, 0:A_H], I["a_sink"][l:l + 1, :].to_broadcast([P, A_H])),
                                 (cache_ak, I["cache_a_k"][0, l].rearrange("t h d -> t (h d)")),
                                 (cache_av, I["cache_a_v"][0, l].rearrange("t h d -> t (h d)")),
                                 (cache_bk, I["cache_b_k"][0, l].rearrange("t h d -> t (h d)")),
                                 (cache_bv, I["cache_b_v"][0, l].rearrange("t h d -> t (h d)")),
                                 (cache_ckv, I["cache_c_kv"][0, l]),
                                 (cache_kr, I["cache_c_krope"][0, l])):
                    pool.dma_start(dst, src).then_inc(s_small, 16)

            def bias_table(l):
                for h in range(B_H):
                    for r in range(3):
                        out = bass.AP(skew.tensor, skew.offset + (h * 3 + r) * BB,
                                      [[BW + 1, GRID_W], [1, RPB_C]])
                        rr = NA_KH - ROWS + r
                        src = I["b_rpb"][l, h, rr:rr + 1, :].to_broadcast([GRID_W, RPB_C])
                        pool.dma_start(out, src).then_inc(s_skew1, 16)

            pool.memset(ones[:], 1.0).then_inc(s_set, 1)
            pool.memset(mhalf[:], -0.5).then_inc(s_set, 1)
            pool.memset(sink[:], NEG).then_inc(s_set, 1)
            pool.memset(xg[:], 0.0).then_inc(s_set, 1)
            pool.wait_ge(s_set, 4)
            sz = B_H * 3 * BB
            pool.dma_start(bass.AP(skew.tensor, skew.offset, [[sz // P, P], [1, sz // P]]),
                           xg[:, :, :].rearrange("p a b -> p (a b)")[:, 0:sz // P]).then_inc(s_skew0, 16)
            small_loads(0)
            pool.wait_ge(s_skew0, 16)
            bias_table(0)
            for l in range(DEPTH):
                pool.wait_ge(s_skew1, 16 * 12 * (l + 1))
                if l:
                    pool.wait_ge(S["o"], 2 * l)
                for r in range(ROWS):
                    for c in range(ROWS):
                        rr = c - r + ROWS - 1
                        src = bass.AP(skew.tensor, skew.offset + rr * BB + NA_KW - 1,
                                      [[BW, GRID_W], [3 * BB, B_H], [1, GRID_W]])
                        pool.dma_start(bias_b[r * GRID_W:(r + 1) * GRID_W, :, c * GRID_W:(c + 1) * GRID_W],
                                       src).then_inc(s_bias, 16)
                pool.wait_ge(s_set, 4)
                pool.wait_ge(S["ms"], 2 * l + 1)
                pool.tensor_tensor(rs[:], ms[:], mhalf[:], ALU.pow).then_inc(S["rs"], 1)
                pool.wait_ge(S["z_d"], 4 * l + 2)
                pool.wait_ge(S["z_a"], 4 * l + 2)
                for out, o, w in ((new_ak, O_KA, A_KV * HD), (new_av, O_VA, A_KV * HD),
                                  (new_bk, O_KB, B_H * HD), (new_bv, O_VB, B_H * HD)):
                    pool.dma_start(out[0, l].rearrange("t h d -> t (h d)"), z[:, 0, o:o + w]).then_inc(s_out, 16)
                pool.dma_start(new_kr[0, l], z[:, 0, O_KR:IN_COLS]).then_inc(s_out, 16)
                pool.wait_ge(S["stat_d"], l + 1)
                pool.tensor_tensor(rst[:], st[:], mhalf[:, 0:4], ALU.pow).then_inc(S["stat_r"], 1)
                pool.wait_ge(S["lat_d"], l + 1)
                pool.dma_start(new_ckv[0, l], z[:, 0, O_CKV:O_KR]).then_inc(s_out, 16)
                pool.wait_ge(S["ms"], 2 * l + 2)
                pool.tensor_tensor(rs[:], ms[:], mhalf[:], ALU.pow).then_inc(S["rs"], 1)
                if l + 1 < DEPTH:
                    pool.wait_ge(S["nb"], l + 1)
                    small_loads(l + 1)
                    bias_table(l + 1)
            pool.wait_ge(S["ms"], 2 * DEPTH + 1)
            pool.tensor_tensor(rs[:], ms[:], mhalf[:], ALU.pow).then_inc(S["rs"], 1)
            pool.wait_ge(S["fin_c"], 2)
            pool.dma_start(y_prompt[0], wide[:, 0, :]).then_inc(s_out, 16)
            pool.dma_start(y_sample[0], wide[:, 1, :]).then_inc(s_out, 16)
            pool.wait_ge(s_out, 16 * (6 * DEPTH + 2))

        @block.tensor
        def _(pe):
            pe.wait_ge(s_const, 16)
            pe.wait_ge(s_set, 4)
            pe.wait_ge(s_x, 32)
            for c in range(KD):
                for t in range(NG):
                    last = pe.transpose(xview[:, c, t * T:(t + 1) * T], wide[:, t, c * P:(c + 1) * P], ident)
            last.then_inc(S["xt_t"], 1)

            def sum_squares(n):
                pe.wait_ge(S["sq"], n)
                for k in range(KD):
                    last = pe.matmul(ps[:, 5, 0:NG * T], ones[:], wide[:, k // 4, (k % 4) * 256:(k % 4) * 256 + 256],
                                     start=(k == 0), stop=(k == KD - 1))
                last.then_inc(S["ssq"], 1)

            done = xdone = 0
            for l in range(DEPTH):
                pe.wait_ge(s_vec, 16 * 7 * (l + 1))
                pe.transpose(ps[:, 4, 0:V_ROWS], vec_rows[:], ident[0:V_ROWS, 0:V_ROWS]).then_inc(S["vec_t"], 1)
                pe.wait_ge(S["csilu"], l + 1)
                modp = ps[:, 7, 0:96].rearrange("p (j g) -> p j g", g=NG)
                for k in ADA:
                    pe.wait_ge(s_misc[k], 16 * (l + 1))
                    for j in range(48):
                        last = pe.matmul(modp[:, j, :], ring[:, slot_of[k], j * P:(j + 1) * P], csilu[:, k, :],
                                         start=(k == 0 and j == 0), stop=(k == KD - 1), skip_group_check=True)
                    last.then_inc(S["mod_mm"], 1)
                sum_squares(2 * l + 1)
                for t in range(NG):
                    if t == 0:
                        pe.wait_ge(S["ht_d"], 2 * l + 1)
                        pe.wait_ge(S["ht_a"], 2 * l + 1)
                    for k in range(KD):
                        if t == 0 and k % 3 == 0:
                            pe.wait_ge(s_misc[WIN[k // 3]], 16 * (l + 1))
                        for n in range(4):
                            o = (k % 3) * IN_COLS + n * NZ
                            last = pe.matmul(ps[:, 4 * t + n, 0:NZ], ht[:, k, t * T:(t + 1) * T],
                                             ring[:, slot_of[WIN[k // 3]], o:o + NZ],
                                             start=(k == 0), stop=(k == KD - 1))
                    last.then_inc(S["z_mm"], 1)
                pe.wait_ge(S["lat_d"], l + 1)
                for t in range(NG):
                    for c in range(2):
                        last = pe.transpose(ps[:, 0, (2 * c + t) * T:(2 * c + t + 1) * T],
                                            z[:, t, O_CQ + c * P:O_CQ + (c + 1) * P], ident)
                last.then_inc(S["kcq_t"], 1)
                pe.wait_ge(s_small, 16 * 12 * (l + 1))
                for i in range(KEYT):
                    src = cache_ckv if i == 2 else z[:, i, O_CKV:O_KR]
                    last = pe.transpose(ps[:, 1, i * T:(i + 1) * T], src, ident)
                last.then_inc(S["kcq_t"], 1)
                pe.wait_ge(S["kcq_c"], 2 * l + 2)
                half = C_H * CD // 2
                for t in range(NG):
                    for n in range(2):
                        for c in range(2):
                            last = pe.matmul(ps[:, 2 + 2 * t + n, 0:half], cqt[:, c, t, :],
                                             w_uq[:, c, n * half:(n + 1) * half], start=(c == 0), stop=(c == 1))
                    last.then_inc(S["qkv_mm"], 1)
                for i in range(KEYT):
                    b = (6, 0, 2)[i]
                    if i == 2:
                        pe.wait_ge(S["qkv_c"], 5 * l + 1)
                    for n in range(2):
                        last = pe.matmul(ps[:, b + n, 0:384], ckvt[:, i, :], w_ukv[:, n * 384:(n + 1) * 384],
                                         start=True, stop=True)
                    last.then_inc(S["qkv_mm"], 1)
                sets = k_sets + q_sets[0] + q_sets[1]
                pe.wait_ge(S["rope"], l + 1)
                pe.wait_ge(S["qkv_c"], 5 * l + 5)

                def head_set(n):
                    kind, i, h0 = sets[n]
                    if n >= 8:
                        if n % 2 == 0:
                            pe.wait_ge(S["qk_d"], QK_D * l + (n - 8) // 2 + 1)
                        else:
                            pe.wait_ge(S["qk_a"], QK_A * l + (n - 8) // 2 + 1)
                    for j in range(4):
                        if kind == "q":
                            src, d = query_of(h0 + j, i), dim_of(h0 + j)
                        else:
                            src = key_of(h0 + j, i)
                            d = HD if h0 + j < A_KV + B_H else CD
                        last = pe.transpose(ps[0:d, n % 8, j * T:(j + 1) * T], src, ident)
                    last.then_inc(S["qk_t"], 1)

                for n in range(NKQ):
                    head_set(n)
                pe.wait_ge(S["qk_d"], QK_D * l + QK_D0)
                pe.wait_ge(S["qk_a"], QK_A * l + QK_A0)

                def scores(n):
                    t, h0, nh = score_groups[n]
                    b = n % 2
                    tiles = (0,) if t == 0 else (1, 2)
                    if n >= 2:
                        pe.wait_ge(S["prob"], NSG * l + n - 1)
                    for j in range(nh):
                        h = h0 + j
                        d = dim_of(h)
                        for m, i in enumerate(tiles):
                            o = (j * len(tiles) + m) * T
                            last = pe.matmul(ps[:, b, o:o + T], qt[0:d, h, :], kt[0:d, i, key_head(h), :],
                                             start=True, stop=True)
                    last.then_inc(S["s_mm"], 1)

                def probs_by_key(n):
                    pe.wait_ge(S["prob"], NSG * l + n + 1)
                    for j in range(4):
                        last = pe.transpose(ps[:, 2 + n % 2, j * T:(j + 1) * T], pr[:, n % 2, j * T:(j + 1) * T], ident)
                    last.then_inc(S["p_t"], 1)

                def weighted_values(n):
                    t, h0, nh = score_groups[n]
                    tiles = (0,) if t == 0 else (1, 2)
                    pe.wait_ge(S["pt_c"], NSG * l + n + 1)
                    for j in range(nh):
                        h = h0 + j
                        for m, i in enumerate(tiles):
                            o = (j * len(tiles) + m) * T
                            last = pe.matmul(ps[:, 4 + 2 * t + h // 8, (h % 8) * HD:(h % 8 + 1) * HD],
                                             pt[:, n % 2, o:o + T], value_of(h, i),
                                             start=(m == 0), stop=(m == len(tiles) - 1))
                    last.then_inc(S["pv"], 1)

                scores(0)
                scores(1)
                for n in range(NSG):
                    probs_by_key(n)
                    if n + 2 < 4:
                        scores(n + 2)
                    if n >= 1 and n != 4:
                        weighted_values(n - 1)
                    if n == 3:
                        weighted_values(3)
                        for m in range(4):
                            kind, i, h0 = q_sets[1][m]
                            if m >= 2:
                                pe.wait_ge(S["qk_d"], QK_D * l + QK_D0 + 1)
                                pe.wait_ge(S["qk_a"], QK_A * l + QK_A0 + 1)
                            for j in range(4):
                                last = pe.transpose(ps[0:dim_of(h0 + j), 6 + m % 2, j * T:(j + 1) * T],
                                                    query_of(h0 + j, i), ident)
                            last.then_inc(S["qk_t"], 1)
                        pe.wait_ge(S["qk_d"], QK_D * (l + 1))
                        pe.wait_ge(S["qk_a"], QK_A * (l + 1))
                        scores(4)
                        scores(5)
                    if n >= 4 and n + 2 < NSG:
                        scores(n + 2)
                weighted_values(NSG - 1)
                for t in range(NG):
                    pe.wait_ge(S["o"], 2 * l + t + 1)
                    for c in range(KD):
                        last = pe.transpose(xview[:, c, t * T:(t + 1) * T], wide[:, t, c * P:(c + 1) * P], ident)
                last.then_inc(S["o_t"], 1)
                pe.wait_ge(S["ot_c"], 2 * l + 2)
                for i in WOUT:
                    pe.wait_ge(s_misc[i], 16 * (l + 1))
                for c in range(KD):
                    for k in range(KD):
                        w = ring[:, slot_of[WOUT[k // 4]], (k % 4) * D + c * P:(k % 4) * D + (c + 1) * P]
                        last = pe.matmul(ps[:, 4 + c // 2, (c % 2) * 256:(c % 2) * 256 + 256], w, ht[:, k, :],
                                         start=(k == 0), stop=(k == KD - 1))
                    if c % 4 == 3:
                        last.then_inc(S["y_mm"], 1)
                pe.wait_ge(S["x1"], 2 * l + 2)
                sum_squares(2 * l + 2)
                pe.wait_ge(S["ht_d"], 2 * l + 2)
                pe.wait_ge(S["ht_a"], 2 * l + 2)
                for t in range(NG):
                    for k in range(KD):
                        last = pe.matmul(ps[:, 4, t * E:(t + 1) * E], ht[:, k, t * T:(t + 1) * T], w_router[:, k, :],
                                         start=(k == 0), stop=(k == KD - 1))
                last.then_inc(S["logit"], 1)
                for t in range(NG):
                    for c in range(KD):
                        last = pe.transpose(ps[:, 2 * t + c // 4, (c % 4) * P:(c % 4 + 1) * P],
                                            ht[:, c, t * T:(t + 1) * T], ident)
                    last.then_inc(S["h2_t"], 1)
                pe.wait_ge(s_misc[SHARED], 48 * (l + 1))
                q = slot_of[SHARED]
                for t in range(NG):
                    for k in range(KD):
                        last = pe.matmul(ps[:, 6 + t, :], ht[:, k, t * T:(t + 1) * T], gu_of(q, k),
                                         start=(k == 0), stop=(k == KD - 1))
                    last.then_inc(S["sh_mm"], 1)
                pe.wait_ge(S["mask"], l + 1)
                pe.matmul(ps[:, 4, 0:E], tbl[:, C_UP:C_UP + P], mask[:, 0, :], start=True, stop=True)
                pe.matmul(ps[:, 4, E:2 * E], tbl[:, C_UP:C_UP + P], mask[:, 1, :], start=True, stop=False)
                pe.matmul(ps[:, 4, E:2 * E], ones[:], mask[:, 0, :], start=False, stop=True).then_inc(S["pos_mm"], 1)
                for t in range(NG):
                    last = pe.matmul(ps[0:E, 5, 0:2], mask[:, t, :], ones[:, 0:2], start=(t == 0), stop=(t == 1))
                last.then_inc(S["cnt_mm"], 1)
                pe.wait_ge(S["sh_a"], 2 * l + 2)
                for t in range(NG):
                    for c in range(2):
                        last = pe.transpose(ps[:, 7, c * 256 + t * T:c * 256 + (t + 1) * T],
                                            act_[:, t, c * P:(c + 1) * P], ident)
                last.then_inc(S["sh_t"], 1)
                pe.wait_ge(S["nb"], l + 1)
                pe.matmul(ps[0:XU, 5, 128:128 + 2 * E], nbb[:, 0:XU], tbl[0:E, C_CUM:C_CUM + 2 * E],
                          start=True, stop=True).then_inc(S["cum_mm"], 1)
                pe.wait_ge(S["sht_c"], l + 1)
                pe.wait_ge(S["h2_d"], l + 1)
                pe.wait_ge(S["h2_a"], l + 1)
                for c in range(KD):
                    for k in range(2):
                        last = pe.matmul(xview[:, c, :], down_of(q)[:, k, c * P:(c + 1) * P], sht[:, k, :],
                                         start=(c % 2 == 0 and k == 0), stop=(k == 1), skip_group_check=True)
                last.then_inc(S["sh_acc"], 1)
                pe.wait_ge(S["inr"], l + 1)
                pe.transpose(ps[0:E, 5, 0:XU], inr[:], ident[0:XU, 0:XU]).then_inc(S["one_t"], 1)
                pe.matmul(ps[:, 5, 64:64 + 2 * XU], ones[0:XU, :], diag[:], start=True, stop=True)\
                    .then_inc(S["one_t"], 1)
                for i in range(4):
                    src = (pos1 if i < 2 else wu)[:, i % 2, 0:E]
                    last = pe.transpose(ps[0:E, 6, i * T:(i + 1) * T], src, ident)
                last.then_inc(S["ext_mm"], 1)
                pe.wait_ge(S["oneh"], l + 1)
                for i in range(4):
                    last = pe.matmul(ps[:, 7, i * XU:(i + 1) * XU], sa[0:E, i * T:(i + 1) * T], oneh[:],
                                     start=True, stop=True)
                last.then_inc(S["ext_mm"], 1)

                def gather(G):
                    pe.wait_ge(S["sel"], G + 1)
                    yield
                    for b in range(2):
                        for c in range(4 * b, 4 * b + 4):
                            for t in range(NG):
                                last = pe.matmul(ps[:, 4 + b, (c % 4) * P:(c % 4 + 1) * P],
                                                 h2[:, t, c * P:(c + 1) * P], pick[:, t, :],
                                                 start=(t == 0), stop=(t == 1))
                        last.then_inc(S["ga" if b == 0 else "gb"], 1)
                        yield

                def pair(J, slots, landed, count):
                    G = J + l
                    pe.wait_ge(S["xga"], G + 1)
                    pe.wait_ge(S["xgb"], G + 1)
                    for s in landed:
                        pe.wait_ge(s, count)
                    for k in range(KD):
                        for e in range(2):
                            last = pe.matmul(ps[CAP * e:CAP * (e + 1), 6, :], xg[:, k, CAP * e:CAP * (e + 1)],
                                             gu_of(slots[e], k), start=(k == 0), stop=(k == KD - 1))
                    last.then_inc(S["gu"], 1)
                    g = gather(G + 1)
                    next(g)
                    next(g)
                    pe.wait_ge(S["sw"], G + 1)
                    pe.wait_ge(S["a"], J + 1)
                    for t in range(NG):
                        pe.transpose(ps[:, 7, t * T:(t + 1) * T], pickw[:, t, :], ident)
                    for c in range(2):
                        last = pe.transpose(ps[:, 7, 256 + c * P:256 + (c + 1) * P], act_[:, 0, c * P:(c + 1) * P], ident)
                    last.then_inc(S["tt"], 1)
                    next(g)
                    pe.wait_ge(S["sa"], J + 1)
                    for b in range(2):
                        pe.wait_ge(S["xga" if b == 0 else "xgb"], G + 2)
                        for k in range(2):
                            for e in range(2):
                                last = pe.matmul(ps[CAP * e:CAP * (e + 1), 4 + b, :],
                                                 sa[:, 256 + k * P + CAP * e:256 + k * P + CAP * (e + 1)],
                                                 down_of(slots[e])[:, k, b * 512:(b + 1) * 512],
                                                 start=(k == 0), stop=(k == 1))
                        last.then_inc(S["y0" if b == 0 else "y1"], 1)
                    for c in range(KD):
                        if c % 4 == 0:
                            pe.wait_ge(S["ya" if c == 0 else "yb"], J + 1)
                        last = pe.matmul(xview[:, c, :], ysb[:, c * P:(c + 1) * P], sa[:, 0:NG * T],
                                         start=False, stop=True, skip_group_check=True)
                    if slots[0] == 0:
                        last.then_inc(S["low_read"], 1)

                pe.wait_ge(S["plan"], 2 * l + 2)
                for _ in gather(done + l):
                    pass
                with pe.Fori(0, PAIRS // 2) as r:
                    for b in range(2):
                        pair(2 * r + (done + b), (2 * b, 2 * b + 1), s_exp[2 * b:2 * b + 2],
                             48 * r + 48 * (l * PAIRS // 2 + 1))
                extra = pe.value_load(xpairs[0:1, 0:1], min_val=1, max_val=XP_MAX)
                with pe.Fori(0, extra) as x:
                    pair(x + (done + PAIRS), (0, 1), [s_xw], (x + (xdone + 1)) * 96)
                done, xdone = extra + (done + PAIRS), extra + xdone
                pe.wait_ge(S["xga"], done + l + 1)
                pe.wait_ge(S["xgb"], done + l + 1)
            sum_squares(2 * DEPTH + 1)
            pe.wait_ge(S["fin"], 1)
            for t in range(NG):
                for c in range(KD):
                    last = pe.transpose(ps[:, 2 * t + c // 4, (c % 4) * P:(c % 4 + 1) * P],
                                        ht[:, c, t * T:(t + 1) * T], ident)
                last.then_inc(S["fin_t"], 1)

        @block.scalar
        def _(act):
            own = [0]

            def then(ins):
                own[0] += 1
                ins.then_inc(s_act, 1)
                act.wait_ge(s_act, own[0])

            def squares():
                act.activation(wide[:].rearrange("p a b -> p (a b)"), xt[:].rearrange("p a b -> p (a b)"),
                               ACT.Square).then_inc(S["sq"], 1)

            act.wait_ge(S["xt_t"], 1)
            act.activation(xt[:, 4:8, :], xview[:, 4:8, :], ACT.Copy).then_inc(S["xt_c"], 1)
            done = xdone = 0
            for l in range(DEPTH):
                act.wait_ge(S["cols_c"], l + 1)
                act.activation(ctanh[:].rearrange("p a b -> p (a b)"), cols[:, V_C:V_C + 2 * KD], ACT.Tanh,
                               scale=0.5).then_inc(S["ctanh"], 1)
                act.wait_ge(S["xt_c"], 2)
                if l:
                    act.wait_ge(S["x2"], l)
                squares()
                act.wait_ge(S["hn"], 2 * l + 1)
                act.wait_ge(S["mod"], l + 1)
                for c in range(4, KD):
                    for g in range(NG):
                        last = act.activation(ht[:, c, g * T:(g + 1) * T], ht[:, c, g * T:(g + 1) * T], ACT.Identity,
                                              scale=gs1[:, c, g:g + 1], bias=mod[:, c, g:g + 1])
                last.then_inc(S["ht_a"], 1)
                for t in range(NG):
                    act.wait_ge(S["z_mm"], 2 * l + t + 1)
                    for n in (1, 3):
                        act.activation(z[:, t, n * NZ:(n + 1) * NZ], ps[:, 4 * t + n, 0:NZ], ACT.Copy)\
                            .then_inc(S["z_a"], 1)
                act.wait_ge(S["z_d"], 4 * l + 4)
                act.wait_ge(S["z_a"], 4 * l + 4)
                for t in range(NG):
                    act.activation(wide[:, t, 0:CQ], z[:, t, O_CQ:O_CKV], ACT.Square, accum_out=st[:, t:t + 1])
                    last = act.activation(wide[:, t, CQ:CQ + CKV], z[:, t, O_CKV:O_KR], ACT.Square,
                                          accum_out=st[:, 2 + t:3 + t])
                last.then_inc(S["stat_a"], 1)
                act.wait_ge(S["kcq_t"], 2 * l + 2)
                act.activation(ckvt[:].rearrange("p a b -> p (a b)"), ps[:, 1, 0:KEYT * T], ACT.Copy)\
                    .then_inc(S["kcq_c"], 1)
                sets = k_sets + q_sets[0] + q_sets[1]
                for n in range(1, NKQ, 2):
                    act.wait_ge(S["qk_t"], QK_T * l + n + 1)
                    copy_heads(act, sets, n, n % 8, True)
                def probs(n):
                    t, h0, nh = score_groups[n]
                    w = 512 // nh
                    act.wait_ge(S["nmax"], NSG * l + n + 1)
                    if n >= 2:
                        act.wait_ge(S["p_t"], NSG * l + n - 1)
                    for j in range(nh):
                        last = act.activation(pr[:, n % 2, j * w:(j + 1) * w], ps[:, n % 2, j * w:(j + 1) * w], ACT.Exp,
                                              bias=nmax[:, h0 + j:h0 + j + 1], accum_out=sums[:, h0 + j:h0 + j + 1])
                    last.then_inc(S["prob"], 1)

                def key_copy(n):
                    act.wait_ge(S["p_t"], NSG * l + n + 1)
                    if n >= 2:
                        act.wait_ge(S["pv"], NSG * l + n - 1)
                    act.activation(pt[:, n % 2, :], ps[:, 2 + n % 2, :], ACT.Copy).then_inc(S["pt_c"], 1)

                for n in range(NSG):
                    if n == 4:
                        key_copy(3)
                        act.wait_ge(S["esum"], 2 * l + 1)
                        act.activation(esink[:], esink[:], ACT.Exp).then_inc(S["esink"], 1)
                        for m in range(1, 4, 2):
                            act.wait_ge(S["qk_t"], QK_T * l + NKQ + m + 1)
                            copy_heads(act, sets, NKQ + m, 6 + m % 2, True)
                    probs(n)
                    if n >= 1 and n != 4:
                        key_copy(n - 1)
                key_copy(NSG - 1)
                act.wait_ge(S["esum"], 2 * l + 2)
                act.activation(esink[:], esink[:], ACT.Exp).then_inc(S["esink"], 1)
                act.wait_ge(S["o_t"], l + 1)
                act.activation(ht[:, 4:8, :], xview[:, 4:8, :], ACT.Copy).then_inc(S["ot_c"], 1)
                act.wait_ge(S["x1"], 2 * l + 2)
                squares()
                act.wait_ge(S["hn"], 2 * l + 2)
                for c in range(4, KD):
                    for g in range(NG):
                        last = act.activation(ht[:, c, g * T:(g + 1) * T], ht[:, c, g * T:(g + 1) * T], ACT.Identity,
                                              scale=gs2[:, c, g:g + 1], bias=mod[:, 24 + c, g:g + 1])
                last.then_inc(S["ht_a"], 1)
                act.wait_ge(S["logit"], l + 1)
                act.activation(score[:].rearrange("p a b -> p (a b)"), ps[:, 4, 0:NG * E], ACT.Tanh, scale=0.5)\
                    .then_inc(S["rtanh"], 1)
                act.wait_ge(S["h2_t"], 2 * l + 2)
                act.wait_ge(s_out, 96 * (l + 1))
                move_tokens(act, 1, True)
                for t in range(NG):
                    act.wait_ge(S["sh_mm"], 2 * l + t + 1)
                    if t:
                        act.wait_ge(S["sh_a"], 2 * l + 1)
                    act.activation(th[:], ps[:, 6 + t, 0:DE], ACT.Tanh, scale=0.5).then_inc(S["sh_th"], 1)
                act.wait_ge(S["sh_t"], l + 1)
                act.activation(sht[:].rearrange("p a b -> p (a b)"), ps[:, 7, :], ACT.Copy).then_inc(S["sht_c"], 1)

                def copy_second(G):
                    act.wait_ge(S["gb"], G + 1)
                    act.activation(xg[:, 4:8, :].rearrange("p a b -> p (a b)"), ps[:, 5, :], ACT.Copy)\
                        .then_inc(S["xgb"], 1)

                def pair(J):
                    act.wait_ge(S["gu"], J + 1)
                    act.activation(th[:], ps[:, 6, 0:DE], ACT.Tanh, scale=0.5).then_inc(S["th"], 1)
                    act.wait_ge(S["tt"], J + 1)
                    act.activation(sa[:], ps[:, 7, :], ACT.Copy).then_inc(S["sa"], 1)
                    copy_second(J + (l + 1))
                    act.wait_ge(S["y1"], J + 1)
                    act.activation(ysb[:, 512:1024], ps[:, 5, :], ACT.Copy).then_inc(S["yb"], 1)

                act.wait_ge(S["plan"], 2 * l + 2)
                copy_second(done + l)
                with act.Fori(0, PAIRS) as r:
                    pair(r + done)
                extra = act.value_load(xpairs[0:1, 0:1], min_val=1, max_val=XP_MAX)
                with act.Fori(0, extra) as x:
                    pair(x + (done + PAIRS))
                done, xdone = extra + (done + PAIRS), extra + xdone
            act.wait_ge(S["x2"], DEPTH)
            squares()
            act.wait_ge(S["fin_t"], 2)
            act.activation(wide[:, 1, :].rearrange("p (a b) -> p a b", a=2), ps[:, 2:4, :], ACT.Copy)\
                .then_inc(S["fin_c"], 1)

        @block.vector
        def _(dve):
            own = [0]

            def then(ins):
                own[0] += 1
                ins.then_inc(s_dve, 1)
                dve.wait_ge(s_dve, own[0])

            def norm(n, gs=None, shift=None):
                dve.wait_ge(S["ssq"], n)
                dve.tensor_scalar(ms[:], ps[:, 5, 0:NG * T], 1.0 / D, EPS, ALU.mult, ALU.add).then_inc(S["ms"], 1)
                dve.wait_ge(S["rs"], n)
                dve.tensor_tensor(ht[:, 4:8, :], xt[:, 4:8, :], rs[:].unsqueeze(1).to_broadcast([P, 4, NG * T]),
                                  ALU.mult).then_inc(S["hn"], 1)
                then(dve.tensor_tensor(ht[:, 0:4, :], xt[:, 0:4, :], rs[:].unsqueeze(1).to_broadcast([P, 4, NG * T]),
                                       ALU.mult))
                if gs is not None:
                    for c in range(4):
                        for g in range(NG):
                            last = dve.tensor_scalar(ht[:, c, g * T:(g + 1) * T], ht[:, c, g * T:(g + 1) * T],
                                                     gs[:, c, g:g + 1], mod[:, shift + c, g:g + 1], ALU.mult, ALU.add)
                    last.then_inc(S["ht_d"], 1)

            dve.wait_ge(S["xt_t"], 1)
            dve.tensor_copy(xt[:, 0:4, :], xview[:, 0:4, :]).then_inc(S["xt_c"], 1)
            done = xdone = 0
            for l in range(DEPTH):
                dve.wait_ge(S["vec_t"], l + 1)
                dve.tensor_copy(cols[:], ps[:, 4, 0:V_ROWS]).then_inc(S["cols_c"], 1)
                dve.wait_ge(S["ctanh"], l + 1)
                then(dve.scalar_tensor_tensor(ctanh[:].rearrange("p a b -> p (a b)"),
                                              ctanh[:].rearrange("p a b -> p (a b)"), 1.0,
                                              cols[:, V_C:V_C + 2 * KD], ALU.add, ALU.mult))
                dve.tensor_scalar(csilu[:].rearrange("p k g -> p g k"), ctanh[:], 0.5, None, ALU.mult)\
                    .then_inc(S["csilu"], 1)
                dve.wait_ge(S["mod_mm"], KD * (l + 1))
                then(dve.tensor_tensor(mod[:], ps[:, 7, 0:96].rearrange("p (j g) -> p j g", g=NG),
                                       cols[:, V_B:V_B + 48].unsqueeze(2).to_broadcast([P, 48, NG]), ALU.add))
                dve.scalar_tensor_tensor(gs1[:], mod[:, 8:16, :], 1.0,
                                         cols[:, V_N1:V_N1 + KD].unsqueeze(2).to_broadcast([P, KD, NG]),
                                         ALU.add, ALU.mult)
                dve.scalar_tensor_tensor(gs2[:], mod[:, 32:40, :], 1.0,
                                         cols[:, V_N2:V_N2 + KD].unsqueeze(2).to_broadcast([P, KD, NG]),
                                         ALU.add, ALU.mult).then_inc(S["mod"], 1)
                dve.wait_ge(S["mod"], l + 1)
                norm(2 * l + 1, gs1, 0)
                for t in range(NG):
                    dve.wait_ge(S["z_mm"], 2 * l + t + 1)
                    for n in (0, 2):
                        dve.tensor_copy(z[:, t, n * NZ:(n + 1) * NZ], ps[:, 4 * t + n, 0:NZ]).then_inc(S["z_d"], 1)
                dve.wait_ge(S["stat_a"], l + 1)
                dve.tensor_scalar(st[:, 0:2], st[:, 0:2], 1.0 / CQ, EPS, ALU.mult, ALU.add)
                dve.tensor_scalar(st[:, 2:4], st[:, 2:4], 1.0 / CKV, EPS, ALU.mult, ALU.add).then_inc(S["stat_d"], 1)
                dve.wait_ge(s_small, 16 * 12 * (l + 1))
                dve.wait_ge(s_bias, 64 * (l + 1))
                dve.wait_ge(s_const, 16)
                dve.tensor_tensor(bias_b[:], bias_b[:],
                                  tbl[:, C_MASK:C_MASK + T].unsqueeze(1).to_broadcast([P, B_H, T]), ALU.add)
                dve.tensor_scalar(nsink[:], sink[:], -1.0, None, ALU.mult)
                dve.wait_ge(S["stat_r"], l + 1)
                for t in range(NG):
                    dve.tensor_scalar(z[:, t, O_CQ:O_CKV], z[:, t, O_CQ:O_CKV], rst[:, t:t + 1], None, ALU.mult)
                    last = dve.scalar_tensor_tensor(z[:, t, O_CKV:O_KR], z[:, t, O_CKV:O_KR], rst[:, 2 + t:3 + t],
                                                    kvg[:], ALU.mult, ALU.mult)
                last.then_inc(S["lat_d"], 1)

                def rotate(x, at, width, heads, signal=None):
                    cos = tbl[:, at:at + width].unsqueeze(1).to_broadcast([P, heads, width])
                    sin = tbl[:, at + width:at + 2 * width].unsqueeze(1).to_broadcast([P, heads, width])
                    tmp = [rtmp[:, i, 0:heads * width].rearrange("p (h w) -> p h w", h=heads) for i in range(4)]
                    dve.tensor_tensor(tmp[0], x[:, :, 0, :], cos, ALU.mult)
                    dve.tensor_tensor(tmp[1], x[:, :, 1, :], sin, ALU.mult)
                    dve.tensor_tensor(tmp[2], x[:, :, 1, :], cos, ALU.mult)
                    then(dve.tensor_tensor(tmp[3], x[:, :, 0, :], sin, ALU.mult))
                    dve.tensor_tensor(x[:, :, 0, :], tmp[0], tmp[1], ALU.subtract)
                    last = dve.tensor_tensor(x[:, :, 1, :], tmp[2], tmp[3], ALU.add)
                    if signal is None:
                        then(last)
                    else:
                        last.then_inc(signal, 1)

                rotate(z[:, 1, 0:O_VA].rearrange("p (h s w) -> p h s w", s=2, w=32), C_ROT64, 32, A_H + A_KV)
                rotate(z[:, 1, O_KR:IN_COLS].rearrange("p (h s w) -> p h s w", s=2, w=16), C_ROT32, 16, 1)
                dve.wait_ge(S["kcq_t"], 2 * l + 1)
                for c in range(2):
                    last = dve.tensor_scalar(cqt[:, c, :, :], ps[:, 0, c * 256:(c + 1) * 256]
                                             .rearrange("p (t n) -> p t n", t=NG),
                                             cols[:, V_QG + c:V_QG + c + 1], None, ALU.mult)
                last.then_inc(S["kcq_c"], 1)
                half = C_H * CD // 2
                for t in range(NG):
                    dve.wait_ge(S["qkv_mm"], 5 * l + t + 1)
                    dve.tensor_copy(qc[:, t, :, :].rearrange("p (a h) d -> p a (h d)", a=2),
                                    ps[:, 2 + 2 * t:4 + 2 * t, 0:half]).then_inc(S["qkv_c"], 1)
                for i in range(KEYT):
                    b = (6, 0, 2)[i]
                    dve.wait_ge(S["qkv_mm"], 5 * l + i + 3)
                    for n in range(2):
                        src = ps[:, b + n, 0:384].rearrange("p (h d) -> p h d", d=2 * HD)
                        dve.tensor_copy(kc[:, i, 3 * n:3 * n + 3, 0:CN], src[:, :, 0:CN])
                        dve.tensor_copy(vc[:, i, 3 * n:3 * n + 3, :], src[:, :, CN:])
                    kr = cache_kr if i == 2 else z[:, i, O_KR:IN_COLS]
                    dve.tensor_copy(kc[:, i, :, CN:CD], kr.unsqueeze(1).to_broadcast([P, C_H, CR]))\
                        .then_inc(S["qkv_c"], 1)
                dve.wait_ge(S["qkv_c"], 5 * l + 2)
                rotate(qc[:, 1, :, CN:CD].rearrange("p h (s w) -> p h s w", s=2), C_ROT32, 16, C_H,
                       S["rope"])
                sets = k_sets + q_sets[0] + q_sets[1]
                for n in range(0, NKQ, 2):
                    dve.wait_ge(S["qk_t"], QK_T * l + n + 1)
                    copy_heads(dve, sets, n, n % 8, False)

                def maxima(n):
                    t, h0, nh = score_groups[n]
                    w = 512 // nh
                    dve.wait_ge(S["s_mm"], NSG * l + n + 1)
                    b = ps[:, n % 2, :].rearrange("p (h w) -> p h w", h=nh)
                    if t == 1 and A_H <= h0 < A_H + B_H:
                        then(dve.tensor_tensor(b[:, :, 0:T], b[:, :, 0:T], bias_b[:, h0 - A_H:h0 - A_H + nh, :], ALU.add))
                    then(dve.tensor_reduce(nmax[:, h0:h0 + nh], b, AX.X, ALU.max, negate=True))
                    dve.tensor_tensor(nmax[:, h0:h0 + nh], nmax[:, h0:h0 + nh], nsink[:, h0:h0 + nh], ALU.min)\
                        .then_inc(S["nmax"], 1)

                def finish(t):
                    dve.wait_ge(S["prob"], NSG * l + (4 if t == 0 else NSG))
                    dve.wait_ge(S["nmax"], NSG * l + (4 if t == 0 else NSG))
                    dve.tensor_tensor(esink[:], sink[:], nmax[:], ALU.add).then_inc(S["esum"], 1)
                    dve.wait_ge(S["esink"], 2 * l + t + 1)
                    then(dve.tensor_tensor(sums[:], sums[:], esink[:], ALU.add))
                    then(dve.reciprocal(rden[:], sums[:]))
                    dve.wait_ge(S["pv"], NSG * l + (4 if t == 0 else NSG))
                    dve.tensor_tensor(wide[:, t, :].rearrange("p (b h d) -> p b h d", b=2, d=HD),
                                      ps[:, 4 + 2 * t:6 + 2 * t, :].rearrange("p b (h d) -> p b h d", d=HD),
                                      rden[:].rearrange("p (b h) -> p b h", b=2).unsqueeze(3)
                                      .to_broadcast([P, 2, 8, HD]), ALU.mult).then_inc(S["o"], 1)

                for n in range(NSG):
                    if n == 4:
                        finish(0)
                        for m in range(0, 4, 2):
                            dve.wait_ge(S["qk_t"], QK_T * l + NKQ + m + 1)
                            copy_heads(dve, sets, NKQ + m, 6 + m % 2, False)
                    maxima(n)
                finish(1)
                dve.wait_ge(S["o_t"], l + 1)
                dve.tensor_copy(ht[:, 0:4, :], xview[:, 0:4, :]).then_inc(S["ot_c"], 1)
                for c in range(KD):
                    if c % 4 == 0:
                        dve.wait_ge(S["y_mm"], 2 * l + c // 4 + 1)
                    for g in range(NG):
                        o = (c % 2) * 256 + g * T
                        last = dve.scalar_tensor_tensor(xt[:, c, g * T:(g + 1) * T], ps[:, 4 + c // 2, o:o + T],
                                                        mod[:, 16 + c, g:g + 1], xt[:, c, g * T:(g + 1) * T],
                                                        ALU.mult, ALU.add)
                    if c % 4 == 3:
                        last.then_inc(S["x1"], 1)
                dve.wait_ge(S["x1"], 2 * l + 2)
                norm(2 * l + 2, gs2, 24)
                dve.wait_ge(S["rtanh"], l + 1)
                then(dve.tensor_scalar(score[:], score[:], 0.5, 0.5, ALU.mult, ALU.add))
                then(dve.tensor_tensor(selv[:], score[:], rbias[:].unsqueeze(1).to_broadcast([P, NG, E]), ALU.add))
                for t in range(NG):
                    for g in range(GROUPS):
                        last = dve.max(top8[:, t, g, :], selv[:, t, g * PER:(g + 1) * PER])
                then(last)
                then(dve.tensor_tensor(gsc[:], top8[:, :, :, 0], top8[:, :, :, 1], ALU.add))
                for t in range(NG):
                    other = gsc[:, t, :].unsqueeze(1).to_broadcast([P, GROUPS, GROUPS])
                    this = gsc[:, t, :].unsqueeze(2).to_broadcast([P, GROUPS, GROUPS])
                    dve.tensor_tensor(cmp1[:, t], other, this, ALU.is_gt)
                    then(dve.tensor_tensor(cmp2[:, t], other, this, ALU.is_equal))
                    then(dve.tensor_tensor(cmp2[:, t], cmp2[:, t],
                                           tbl[:, C_TIE:C_TIE + 64].rearrange("p (i j) -> p i j", i=GROUPS), ALU.mult))
                    then(dve.tensor_tensor(cmp1[:, t], cmp1[:, t], cmp2[:, t], ALU.add))
                then(dve.tensor_reduce(rank[:], cmp1[:], AX.X, ALU.add))
                then(dve.tensor_scalar(rank[:], rank[:], float(TOP_G), None, ALU.is_lt))
                for t in range(NG):
                    keep_t = rank[:, t, :].unsqueeze(2).to_broadcast([P, GROUPS, PER])
                    sel_t = selv[:, t, :].rearrange("p (g e) -> p g e", g=GROUPS)
                    rep_t = repl[:, t, :].rearrange("p (g e) -> p g e", g=GROUPS)
                    dve.tensor_tensor(sel_t, sel_t, keep_t, ALU.mult)
                    then(dve.tensor_scalar(rep_t, keep_t, -NEG, NEG, ALU.mult, ALU.add))
                then(dve.tensor_tensor(selv[:], selv[:], repl[:], ALU.add))
                for t in range(NG):
                    last = dve.max(t8[:, t, :], selv[:, t, :])
                then(last)
                then(dve.memset(t8[:, :, TOP_K:8], NEG))
                for t in range(NG):
                    last = dve.match_replace(repl[:, t, :], t8[:, t, :], selv[:, t, :], 3.0 * NEG)
                then(last)
                then(dve.tensor_scalar(mask[:], repl[:], 2.0 * NEG, None, ALU.is_lt))
                then(dve.tensor_scalar(repl[:], selv[:], 0.5 * NEG, None, ALU.is_gt))
                dve.tensor_tensor(mask[:], mask[:], repl[:], ALU.mult).then_inc(S["mask"], 1)
                dve.wait_ge(S["mask"], l + 1)
                then(dve.tensor_tensor(repl[:], score[:], mask[:], ALU.mult))
                then(dve.tensor_reduce(wsum[:], repl[:], AX.X, ALU.add))
                then(dve.reciprocal(wsum[:], wsum[:]))
                for t in range(NG):
                    last = dve.tensor_scalar(wu[:, t, 0:E], repl[:, t, :], wsum[:, t:t + 1], 0.5 * ROUTED_SCALE,
                                             ALU.mult, ALU.mult)
                then(last)
                dve.wait_ge(S["pos_mm"], l + 1)
                for t in range(NG):
                    last = dve.scalar_tensor_tensor(pos1[:, t, 0:E], ps[:, 4, t * E:(t + 1) * E], 1.0, mask[:, t, :],
                                                    ALU.add, ALU.mult)
                then(last)
                dve.wait_ge(S["cnt_mm"], l + 1)
                for i in range(1, NG * T // CAP):
                    last = dve.tensor_scalar(cnt[:, i - 1:i], ps[0:E, 5, 0:1], i * CAP + 0.5, None, ALU.is_gt)
                then(last)
                then(dve.tensor_tensor(cnt[:, 0:1], cnt[:, 0:1], cnt[:, 1:2], ALU.add))
                then(dve.tensor_tensor(cnt[:, 0:1], cnt[:, 0:1], cnt[:, 2:3], ALU.add))
                dve.tensor_scalar(nbb[:], ones[0:E, :], cnt[:, 0:1], None, ALU.mult).then_inc(S["nb"], 1)
                dve.wait_ge(S["h2_t"], 2 * l + 2)
                dve.wait_ge(s_out, 96 * (l + 1))
                move_tokens(dve, 0, False)
                for t in range(NG):
                    dve.wait_ge(S["sh_th"], 2 * l + t + 1)
                    then(dve.scalar_tensor_tensor(a1[:], th[:], 1.0, ps[:, 6 + t, 0:DE], ALU.add, ALU.mult))
                    dve.scalar_tensor_tensor(act_[:, t, :], a1[:], 0.5, ps[:, 6 + t, DE:2 * DE], ALU.mult, ALU.mult)\
                        .then_inc(S["sh_a"], 1)
                dve.wait_ge(S["cum_mm"], l + 1)
                then(dve.tensor_copy(cum[:], ps[0:XU, 5, 128:128 + 2 * E]))
                number = tbl[0:XU, C_PART:C_PART + 1]
                dve.tensor_scalar(fin[:], cum[:, 0:E], number, None, ALU.is_le)
                dve.tensor_scalar(inr[:], cum[:, E:2 * E], number, None, ALU.is_le)
                then(dve.tensor_scalar(ns[:], cum[:, E:2 * E], -1.0, number, ALU.mult, ALU.add))
                then(dve.tensor_tensor(inr[:], inr[:], fin[:], ALU.subtract))
                then(dve.tensor_tensor(ns[:], ns[:], inr[:], ALU.mult))
                dve.tensor_reduce(uv[:, 0:1], ns[:], AX.X, ALU.add)
                then(dve.tensor_reduce(uv[:, 1:2], fin[:], AX.X, ALU.add))
                dve.tensor_scalar(uv[:, 2:3], uv[:, 0:1], float(CAP), float(CAP), ALU.mult, ALU.add)
                then(dve.tensor_scalar(uv[:, 3:4], uv[:, 1:2], float(E - 1), None, ALU.min))
                dve.tensor_scalar(diag[:, 0:XU], ident[0:XU, 0:XU], uv[:, 2:3], None, ALU.mult)
                dve.tensor_scalar(diag[:, XU:2 * XU], ident[0:XU, 0:XU], uv[:, 3:4], None, ALU.mult)\
                    .then_inc(S["inr"], 1)
                then(dve.tensor_scalar(fin[0:1, 0:16], tbl[0:1, C_EVEN:C_EVEN + 16], cum[0:1, E - 1:E], None,
                                       ALU.is_lt))
                then(dve.tensor_reduce(xcount[:, 0:1], fin[0:1, 0:16], AX.X, ALU.add))
                dve.tensor_scalar(xpairs[:], xcount[:, 0:1], 1.0, None, ALU.max).then_inc(S["plan"], 1)
                dve.wait_ge(S["one_t"], 2 * l + 2)
                dve.wait_ge(S["ext_mm"], 2 * l + 1)
                dve.tensor_copy(urow[:], ps[:, 5, 64:64 + 2 * XU])
                dve.tensor_copy(sa[0:E, :], ps[0:E, 6, :])
                dve.tensor_copy(oneh[:], ps[0:E, 5, 0:XU]).then_inc(S["oneh"], 1)
                dve.wait_ge(S["ext_mm"], 2 * l + 2)
                dve.wait_ge(S["oneh"], l + 1)
                for t in range(NG):
                    dve.tensor_tensor(pos1[:, t, E:NU], ps[:, 7, t * XU:(t + 1) * XU], urow[:, 0:XU], ALU.subtract)
                    dve.tensor_copy(wu[:, t, E:NU], ps[:, 7, (2 + t) * XU:(3 + t) * XU])
                dve.tensor_copy(xexp[:], urow[0:1, XU:2 * XU]).then_inc(S["plan"], 1)
                dve.wait_ge(S["plan"], 2 * l + 2)

                def choose(u):
                    at = pos1[:, :, bass.ds(u, 2)] if not isinstance(u, int) else pos1[:, :, u:u + 2]
                    dve.tensor_tensor(pick[:].rearrange("p t (e s) -> p t e s", e=2),
                                      tbl[:, C_SLOT:C_SLOT + CAP].unsqueeze(1).unsqueeze(1)
                                      .to_broadcast([P, NG, 2, CAP]),
                                      at.unsqueeze(3).to_broadcast([P, NG, 2, CAP]), ALU.is_equal)\
                        .then_inc(S["sel"], 1)

                def weigh(u, G):
                    at = wu[:, :, bass.ds(u, 2)] if not isinstance(u, int) else wu[:, :, u:u + 2]
                    dve.wait_ge(S["sel"], G + 1)
                    dve.tensor_tensor(pickw[:].rearrange("p t (e s) -> p t e s", e=2),
                                      pick[:].rearrange("p t (e s) -> p t e s", e=2),
                                      at.unsqueeze(3).to_broadcast([P, NG, 2, CAP]), ALU.mult).then_inc(S["sw"], 1)

                def copy_first(G):
                    dve.wait_ge(S["ga"], G + 1)
                    dve.tensor_copy(xg[:, 0:4, :].rearrange("p a b -> p (a b)"), ps[:, 4, :]).then_inc(S["xga"], 1)

                def pair(j, J):
                    G = J + l
                    dve.wait_ge(S["gb"], G + 1)
                    dve.wait_ge(S["sw"], G + 1)
                    choose(2 * j + 2)
                    dve.wait_ge(S["th"], J + 1)
                    dve.scalar_tensor_tensor(a1[:], th[:], 1.0, ps[:, 6, 0:DE], ALU.add, ALU.mult).then_inc(S["cval"], 1)
                    dve.wait_ge(S["cval"], J + 1)
                    dve.tensor_tensor(act_[:, 0, :], a1[:], ps[:, 6, DE:2 * DE], ALU.mult).then_inc(S["a"], 1)
                    copy_first(G + 1)
                    dve.wait_ge(S["tt"], J + 1)
                    weigh(2 * j + 2, G + 1)
                    dve.wait_ge(S["y0"], J + 1)
                    dve.tensor_copy(ysb[:, 0:512], ps[:, 4, :]).then_inc(S["ya"], 1)

                choose(0)
                weigh(0, done + l)
                copy_first(done + l)
                with dve.Fori(0, PAIRS) as r:
                    pair(r, r + done)
                extra = dve.value_load(xpairs[0:1, 0:1], min_val=1, max_val=XP_MAX)
                with dve.Fori(0, extra) as x:
                    pair(x + PAIRS, x + (done + PAIRS))
                done, xdone = extra + (done + PAIRS), extra + xdone
                dve.wait_ge(S["low_read"], xdone + PAIRS // 2 * (l + 1))
                for c in range(KD):
                    for g in range(NG):
                        last = dve.scalar_tensor_tensor(xt[:, c, g * T:(g + 1) * T], xview[:, c, g * T:(g + 1) * T],
                                                        mod[:, 40 + c, g:g + 1], xt[:, c, g * T:(g + 1) * T],
                                                        ALU.mult, ALU.add)
                last.then_inc(S["x2"], 1)
            dve.wait_ge(S["x2"], DEPTH)
            norm(2 * DEPTH + 1)
            dve.wait_ge(S["hn"], 2 * DEPTH + 1)
            for c in range(KD):
                last = dve.tensor_scalar(ht[:, c, :], ht[:, c, :], cols[:, V_F + c:V_F + c + 1], None, ALU.mult)
            last.then_inc(S["fin"], 1)
            dve.wait_ge(S["fin_t"], 2)
            dve.tensor_copy(wide[:, 0, :].rearrange("p (a b) -> p a b", a=2), ps[:, 0:2, :]).then_inc(S["fin_c"], 1)


_INS = ["x_prompt", "x_sample", "cache_a_k", "cache_a_v", "cache_b_k", "cache_b_v", "cache_c_kv", "cache_c_krope",
        "c", "c_ctx", "norm1_g", "norm2_g", "w_ada", "b_ada", "w_in", "a_sink", "b_rpb", "c_q_norm_g", "c_w_uq",
        "c_kv_norm_g", "c_w_ukv", "w_out", "router_w", "router_bias", "exp_w_gate", "exp_w_up", "exp_w_down",
        "sh_w_gate", "sh_w_up", "sh_w_down", "final_norm_g"]
_OUTS = [(1, T, D), (1, T, D), (1, DEPTH, T, A_KV, HD), (1, DEPTH, T, A_KV, HD), (1, DEPTH, T, B_H, HD),
         (1, DEPTH, T, B_H, HD), (1, DEPTH, T, CKV), (1, DEPTH, T, CR)]


def kernel(**inputs):
    import concourse.bacc as bacc
    from concourse.bass_utils import run_bass_kernel_spmd

    nc = bacc.Bacc("TRN2", target_bir_lowering=False, num_devices=1)
    arrays, aps = {}, {}
    for name in _INS:
        a = np.ascontiguousarray(inputs[name])
        arrays[f"in_{name}"] = a
        aps[name] = nc.dram_tensor(f"in_{name}", a.shape, mybir.dt.from_np(a.dtype), kind="ExternalInput").ap()
    arrays["consts"] = constants()
    consts = nc.dram_tensor("consts", (P, C_COLS), F32, kind="ExternalInput").ap()
    skew = nc.dram_tensor("skew", (B_H, 3, BB), F32, kind="Internal").ap()
    outs = [nc.dram_tensor(f"out_{i}", s, F32, kind="ExternalOutput").ap() for i, s in enumerate(_OUTS)]
    backbone(nc, aps, consts, skew, outs)
    r = run_bass_kernel_spmd(nc, [arrays], core_ids=[0])
    return tuple(r.results[0][f"out_{i}"] for i in range(len(_OUTS)))
```

```python
from contextlib import ExitStack

import numpy as np
import concourse.bass as bass
from concourse import mybir

F32 = mybir.dt.float32
I32 = mybir.dt.int32
ALU = mybir.AluOpType
ACT = mybir.ActivationFunctionType
AX = mybir.AxisListType

P = 128
DEPTH, D, T = 2, 1024, 128
KD = D // P
NG = 2
HD, NH = 64, 16
A_H, A_KV, B_H, C_H = 6, 2, 4, 6
A_GROUP = A_H // A_KV
CQ, CKV, CR, CN = 256, 128, 32, 64
CD = CN + CR
WIDTHS = (A_H * HD, A_KV * HD, A_KV * HD, B_H * HD, B_H * HD, B_H * HD, CQ, CKV, CR)
OFF = [sum(WIDTHS[:i]) for i in range(len(WIDTHS) + 1)]
O_QA, O_KA, O_VA, O_QB, O_KB, O_VB, O_CQ, O_CKV, O_KR, IN_COLS = OFF
NZ = IN_COLS // 4
HEAD_SCALE = HD ** -0.5
C_SCALE = CD ** -0.5
GRID_W, NA_KH, NA_KW = 64, 8, 16
ROWS = T // GRID_W
EPS = 1e-6
NEG = -1e30
E, TOP_K, GROUPS, TOP_G, DE = 64, 6, 8, 4, 256
PER = E // GROUPS
ROUTED_SCALE = 2.5
CAP = 64
PAIRS = E // 2
XU = 32
XP_MAX = 12
NU = E + XU
SLOT = 6144
NSLOT = 4
KEYT = 3
KH = A_KV + B_H + C_H
BW = GRID_W + 2 * (NA_KW - 1)
BB = 6144
RPB_R, RPB_C = 2 * NA_KH - 1, 2 * NA_KW - 1

V_B, V_N1, V_N2, V_QG, V_C, V_F, V_ROWS = 0, 48, 56, 64, 66, 82, 90

C_ROT64, C_ROT32, C_MASK, C_ID, C_UP = 0, 64, 96, 224, 352
C_CUM, C_TIE, C_SLOT, C_PART, C_EVEN, C_COLS = 480, 608, 672, 736, 737, 753


def constants():
    t = np.arange(T)
    row, col = (t // GRID_W).astype(np.float32), (t % GRID_W).astype(np.float32)
    k = np.zeros((P, C_COLS), np.float32)
    for at, dim in ((C_ROT64, HD), (C_ROT32, CR)):
        n = dim // 4
        inv = (np.float32(10000.0) ** (-np.arange(n, dtype=np.float32) / np.float32(n))).astype(np.float32)
        ang = np.concatenate([row[:, None] * inv, col[:, None] * inv], axis=-1).astype(np.float32)
        k[:, at:at + dim // 2] = np.cos(ang)
        k[:, at + dim // 2:at + dim] = np.sin(ang)
    start = np.clip(np.arange(GRID_W) - NA_KW // 2, 0, GRID_W - NA_KW)
    c = t % GRID_W
    inside = (c[None, :] >= start[c][:, None]) & (c[None, :] < start[c][:, None] + NA_KW)
    k[:, C_MASK:C_MASK + T] = np.where(inside, 0.0, NEG)
    k[:, C_ID:C_ID + P] = np.eye(P)
    k[:, C_UP:C_UP + P] = np.triu(np.ones((P, P)), 1)
    k[:E, C_CUM:C_CUM + E] = np.triu(np.ones((E, E)))
    k[:E, C_CUM + E:C_CUM + 2 * E] = np.triu(np.ones((E, E)), 1)
    k[:, C_TIE:C_TIE + 64] = np.tril(np.ones((GROUPS, GROUPS)), -1).reshape(1, 64)
    k[:, C_SLOT:C_SLOT + CAP] = np.arange(1, CAP + 1)
    k[:, C_PART] = np.arange(P)
    k[:, C_EVEN:C_EVEN + 16] = 2 * np.arange(16)
    return k


def backbone(nc, I, consts, skew, O):
    y_prompt, y_sample, new_ak, new_av, new_bk, new_bv, new_ckv, new_kr = O
    ctx = ExitStack()
    with ctx:
        def sb(name, shape, dt=F32):
            return ctx.enter_context(nc.sbuf_tensor(name, shape, dt))

        def carve(buf):
            at = [0]

            def view(shape, parts=P):
                n = int(np.prod(shape))
                v = buf[0:parts, at[0]:at[0] + n]
                at[0] += n
                assert at[0] <= buf.shape[1]
                if len(shape) == 1:
                    return v
                names = "abcd"[:len(shape)]
                return v.rearrange(f"p ({' '.join(names)}) -> p {' '.join(names)}", **dict(zip(names, shape)))
            return view

        def sem(name):
            return ctx.enter_context(nc.semaphore(name))

        ring = sb("ring", [P, NSLOT, SLOT])
        xt = sb("xt", [P, KD, NG * T])
        ht = sb("ht", [P, KD, NG * T])
        wide = sb("wide", [P, NG, D])
        z = sb("z", [P, NG, IN_COLS])
        h2 = z[:, :, 0:D]
        tbl = sb("tbl", [P, C_COLS])
        ones = sb("ones", [P, P])
        mhalf = sb("mhalf", [P, 4])
        vec_rows = sb("vec_rows", [V_ROWS, DEPTH, P])
        colsl = sb("colsl", [P, DEPTH, V_ROWS])
        csilu = sb("csilu", [P, KD, 32])
        ada_sb = sb("ada_sb", [P, 512])
        ctanh = sb("ctanh", [P, NG, KD])
        modl = sb("modl", [P, DEPTH, 48, NG])
        gs1 = sb("gs1", [P, KD, NG])
        gs2 = sb("gs2", [P, KD, NG])
        ms = sb("ms", [P, NG])
        rs = sb("rs", [P, NG])
        rdiag = sb("rdiag", [P, NG, T])
        w_uq = sb("w_uq", [P, 2, C_H * CD])
        w_ukv = sb("w_ukv", [P, C_H * 2 * HD])
        w_router = sb("w_router", [P, KD, E])
        rbias = sb("rbias", [P, E])
        kvg = sb("kvg", [P, CKV])
        sink = sb("sink", [P, NH])
        nsink = sb("nsink", [P, NH])
        cache = sb("cache", [P, 2 * A_KV * HD + 2 * B_H * HD + CKV + CR])
        bias_b = sb("bias_b", [P, B_H, T])
        st = sb("st", [P, 4])
        rst = sb("rst", [P, 4])
        kc_buf = sb("kc_buf", [P, KEYT * C_H * CD])
        vc_buf = sb("vc_buf", [P, KEYT * C_H * HD])
        qt_buf = sb("qt_buf", [P, NH * T])
        kt_buf = sb("kt_buf", [P, KEYT * KH * T])
        pr_buf = sb("pr_buf", [P, 2 * 512])
        kc = carve(kc_buf)([KEYT, C_H, CD])
        vc = carve(vc_buf)([KEYT, C_H, HD])
        qt = carve(qt_buf)([NH, T])
        kt = carve(kt_buf)([KEYT, KH, T])
        pr = carve(pr_buf)([2, 512])
        rtmp = carve(pr_buf)([4, 256])
        lat = carve(ht[:].rearrange("p a b -> p (a b)"))
        cqt = lat([2, NG, T])
        ckvt = lat([KEYT, T])
        qc = lat([NG, C_H, CD])
        pt = sb("pt", [P, 2, 512])
        nmax = sb("nmax", [P, NH])
        sums = sb("sums", [P, NH])
        esink = sb("esink", [P, NH])
        rden = sb("rden", [P, NH])
        route_view, plan_view = carve(kc_buf), carve(vc_buf)
        score = route_view([NG, E])
        selv = route_view([NG, E])
        repl = route_view([NG, E])
        mask = route_view([NG, E])
        top8 = route_view([NG, GROUPS, 8])
        gsc = route_view([NG, GROUPS])
        cmp1 = route_view([NG, GROUPS, GROUPS])
        cmp2 = route_view([NG, GROUPS, GROUPS])
        rank = route_view([NG, GROUPS])
        t8 = route_view([NG, 8])
        wsum = route_view([NG])
        pos1 = route_view([NG, NU])
        wu = route_view([NG, NU])
        cnt = plan_view([4], E)
        nbb = plan_view([P], E)
        cum = plan_view([2 * E], XU)
        fin = plan_view([E], XU)
        inr = plan_view([E], XU)
        ns = plan_view([E], XU)
        uv = plan_view([4], XU)
        oneh = plan_view([XU], E)
        diag = plan_view([2 * XU], XU)
        urow = plan_view([2 * XU])
        xexp = sb("xexp", [1, XU], I32)
        xcount = sb("xcount", [1, 2])
        xpairs = sb("xpairs", [1, 1], I32)
        moe_view = carve(kt_buf)
        pick = moe_view([NG, 2 * CAP])
        pickw = moe_view([NG, 2 * CAP])
        xg = moe_view([KD, 2 * CAP])
        th = moe_view([DE])
        a1 = moe_view([DE])
        act_ = moe_view([NG, DE])
        sa = moe_view([512])
        ysb = moe_view([D])
        sht = moe_view([2, NG * T])

        ps = ctx.enter_context(nc.psum_tensor("ps", [P, 8, 512], F32))
        ident = tbl[:, C_ID:C_ID + P]
        xview = ps[:, 0:4, :].rearrange("p b (c n) -> p (b c) n", c=2)

        cache_ak, cache_av = cache[:, 0:128], cache[:, 128:256]
        cache_bk, cache_bv = cache[:, 256:512], cache[:, 512:768]
        cache_ckv, cache_kr = cache[:, 768:896], cache[:, 896:928]

        ADA_K = ((0, 3), (3, 6), (6, 8))
        ada_early = (0, 0)
        ada_late = [(0, 1), (0, 2), (1, 0), (1, 1), (1, 2)]
        WIN_K = ((0, 3), (3, 6), (6, 8))

        tail = [("out", 0), ("out", 1), ("shared", 0)]
        entries = [[("ada", *ada_early, i) for i in range(3)] + [("in", i) for i in range(3)]
                   + [("ada", *a, i) for a in ada_late for i in range(3)] + tail,
                   [("in", i) for i in range(3)] + tail]
        slots = [{e: (i - len(es)) % NSLOT for i, e in enumerate(es)} for es in entries]

        s_const = sem("s_const")
        s_x = sem("s_x")
        s_vec = sem("s_vec")
        s_small = sem("s_small")
        s_skew0, s_skew1, s_bias = sem("s_skew0"), sem("s_skew1"), sem("s_bias")
        s_zero = sem("s_zero")
        s_ent = [{e: sem("s_l%d_%s" % (l, "_".join(map(str, e)))) for e in es} for l, es in enumerate(entries)]
        s_exp = [sem(f"s_exp{q}") for q in range(NSLOT)]
        s_xw = sem("s_xw")
        s_out = sem("s_out")
        s_sp = sem("s_sp")
        s_set = sem("s_set")
        s_dve, s_act, s_pool = sem("s_dve"), sem("s_act"), sem("s_pool")
        names = ("xt_t", "xt_c", "vec_t", "cols_c", "ctanh", "csilu", "ada_mm", "ada_c", "ada_t", "ada_add", "win_mm", "mod", "sq", "ssq", "ms", "rs", "rdiag", "rs_mm",
                 "hn", "ht_d", "ht_a", "z_mm", "z_d", "z_a", "stat_d", "stat_a", "stat_r", "lat_d", "kcq_t",
                 "kcq_c", "qkv_mm", "qkv_c", "rope", "qk_t", "qk_d", "qk_a", "s_mm", "nmax", "prob", "p_t", "pt_c",
                 "pv", "esum", "esink", "o", "o_t", "ot_c", "y_mm", "x1", "h2_t", "h2_d", "h2_a", "logit", "rtanh",
                 "mask", "pos_mm", "cnt_mm", "nb", "cum_mm", "inr", "one_t", "oneh", "ext_mm", "plan", "sh_mm",
                 "sh_th", "sh_a", "sh_t", "sht_c", "sh_acc", "sel", "sw", "ga", "gb", "xga", "xgb", "gu", "th", "a",
                 "tt", "sa", "y0", "y1", "ya", "yb", "low_read", "x2",
                 "fin", "fin_t", "fin_c", "cval")
        S = {n: sem("s_" + n) for n in names}

        block = ctx.enter_context(nc.Block())

        def gu_of(slot, k):
            return ring[:, slot, 0:4096].rearrange("p (g k f) -> p g k f", g=2, k=KD)[:, :, k, :]

        def down_of(slot):
            return ring[:, slot, 4096:6144].rearrange("p (k d) -> p k d", k=2)

        def ada_count(ent):
            return [e for e in entries[0] if e[0] == "ada"].index(ent) + 1

        score_groups = [(0, h, 4) for h in range(0, NH, 4)] + [(1, h, 2) for h in range(0, NH, 2)]
        NSG = len(score_groups)

        def key_head(h):
            return h // A_GROUP if h < A_H else h - A_H + A_KV

        def value_of(h, key_tile):
            if h < A_H:
                o = HD * (h // A_GROUP)
                return cache_av[:, o:o + HD] if key_tile == 2 else z[:, key_tile, O_VA + o:O_VA + o + HD]
            if h < A_H + B_H:
                o = HD * (h - A_H)
                return cache_bv[:, o:o + HD] if key_tile == 2 else z[:, key_tile, O_VB + o:O_VB + o + HD]
            return vc[:, key_tile, h - A_H - B_H, :]

        def query_of(h, t):
            if h < A_H:
                return z[:, t, O_QA + h * HD:O_QA + (h + 1) * HD]
            if h < A_H + B_H:
                o = O_QB + (h - A_H) * HD
                return z[:, t, o:o + HD]
            return qc[:, t, h - A_H - B_H, :]

        def key_of(kh, key_tile):
            if kh < A_KV:
                return cache_ak[:, kh * HD:(kh + 1) * HD] if key_tile == 2 else \
                    z[:, key_tile, O_KA + kh * HD:O_KA + (kh + 1) * HD]
            if kh < A_KV + B_H:
                o = (kh - A_KV) * HD
                return cache_bk[:, o:o + HD] if key_tile == 2 else z[:, key_tile, O_KB + o:O_KB + o + HD]
            return kc[:, key_tile, kh - A_KV - B_H, :]

        def dim_of(h):
            return HD if h < A_H + B_H else CD

        q_sets = [[("q", t, h) for h in range(0, NH, 4)] for t in range(NG)]
        k_sets = [("k", kt_, h) for kt_ in range(KEYT) for h in range(0, KH, 4)]
        NKQ = len(k_sets) + 4
        QK_T = NKQ + 4
        QK_D0, QK_A0 = (NKQ + 1) // 2, NKQ // 2
        QK_D, QK_A = QK_D0 + 2, QK_A0 + 2

        def copy_heads(eng, sets, n, bank, on_act):
            kind, i, h0 = sets[n]
            first_c = A_H + B_H if kind == "q" else A_KV + B_H
            runs = [(a, b) for a, b in ((h0, min(h0 + 4, first_c)), (max(h0, first_c), h0 + 4)) if a < b]
            for a, b in runs:
                wide_head = a >= first_c
                d = CD if wide_head else HD
                src = ps[0:d, bank, (a - h0) * T:(b - h0) * T].rearrange("p (h n) -> p h n", n=T)
                dst = qt[0:d, a:b, :] if kind == "q" else kt[0:d, i, a:b, :]
                scale = 1.0 if kind == "k" else (C_SCALE if wide_head else HEAD_SCALE)
                if on_act:
                    last = eng.activation(dst, src, ACT.Copy, scale=scale)
                else:
                    last = eng.tensor_scalar(dst, src, scale, None, ALU.mult)
            last.then_inc(S["qk_a" if on_act else "qk_d"], 1)

        def move_tokens(eng, t, on_act):
            src = ps[:, 2 * t:2 * t + 2, :].rearrange("p h (m b) -> p h m b", b=8)
            dst = h2[:, t, :].rearrange("p (b h m) -> p h m b", b=8, h=2)
            if on_act:
                eng.activation(dst, src, ACT.Copy).then_inc(S["h2_a"], 1)
            else:
                eng.tensor_copy(dst, src).then_inc(S["h2_d"], 1)

        @block.sync
        def _(sp):
            sp.dma_start(tbl[:], consts).then_inc(s_const, 16)
            sp.dma_start(wide[:, 0, :], I["x_prompt"][0]).then_inc(s_x, 16)
            sp.dma_start(wide[:, 1, :], I["x_sample"][0]).then_inc(s_x, 16)
            done = xdone = 0
            for l in range(DEPTH):
                w_in, w_out = I["w_in"][l], I["w_out"][l]
                es = entries[l]
                for i, ent in enumerate(es):
                    q = slots[l][ent]
                    dst = ring[:, q, :]
                    if i < NSLOT and l:
                        if q >= 2:
                            sp.wait_ge(S["y1"], first_done)
                        else:
                            sp.wait_ge(S["y1"], done)
                    if i >= NSLOT:
                        before = es[i - NSLOT]
                        if before[0] == "ada":
                            sp.wait_ge(S["ada_mm"], ada_count(before))
                        elif before[0] == "in":
                            sp.wait_ge(S["win_mm"], 3 * l + before[1] + 1)
                    if ent[0] == "ada":
                        _, al, third, part = ent
                        k0, k1 = ADA_K[part]
                        sp.dma_start(dst[:, 0:(k1 - k0) * 2048].rearrange("p (k n) -> p k n", k=k1 - k0),
                                     I["w_ada"][al, k0 * P:k1 * P, third * 2048:(third + 1) * 2048]
                                     .rearrange("(k p) n -> p k n", p=P)).then_inc(s_ent[l][ent], 16)
                    elif ent[0] == "in":
                        k0, k1 = WIN_K[ent[1]]
                        sp.dma_start(dst[:, 0:(k1 - k0) * IN_COLS].rearrange("p (k n) -> p k n", k=k1 - k0),
                                     w_in[k0 * P:k1 * P, :].rearrange("(k p) n -> p k n", p=P)
                                     ).then_inc(s_ent[l][ent], 16)
                    elif ent[0] == "out":
                        k0 = 4 * ent[1]
                        sp.dma_start(dst[:, 0:4 * D].rearrange("p (k n) -> p k n", k=4),
                                     w_out[k0 * P:(k0 + 4) * P, :].rearrange("(k p) n -> p k n", p=P)
                                     ).then_inc(s_ent[l][ent], 16)
                    else:
                        for g, name in enumerate(("sh_w_gate", "sh_w_up")):
                            sp.dma_start(dst[:, g * 2048:(g + 1) * 2048].rearrange("p (k f) -> p k f", k=KD),
                                         I[name][l].rearrange("(k p) f -> p k f", p=P)).then_inc(s_ent[l][ent], 16)
                        sp.dma_start(down_of(q), I["sh_w_down"][l].rearrange("(k p) d -> p k d", p=P)
                                     ).then_inc(s_ent[l][ent], 16)

                def settle():
                    sp.sem_inc(s_sp, 1)

                def load_expert(e, q, landed):
                    sp.dma_start(ring[:, q, 0:2048],
                                 I["exp_w_gate"][l, e, :, :].rearrange("(p k) f -> p (k f)", k=KD)).then_inc(landed, 16)
                    sp.dma_start(ring[:, q, 2048:4096],
                                 I["exp_w_up"][l, e, :, :].rearrange("(p k) f -> p (k f)", k=KD)).then_inc(landed, 16)
                    sp.dma_start(down_of(q),
                                 I["exp_w_down"][l, e, :, :].rearrange("(k p) d -> p k d", p=P)).then_inc(landed, 16)

                before = es[-4]
                sp.wait_ge(S["ada_mm"] if before[0] == "ada" else S["win_mm"],
                           ada_count(before) if before[0] == "ada" else 3 * l + before[1] + 1)
                load_expert(0, 0, s_exp[0])
                sp.wait_ge(S["y_mm"], 2 * l + 2)
                load_expert(1, 1, s_exp[1])
                load_expert(2, 2, s_exp[2])
                sp.wait_ge(S["sh_acc"], l + 1)
                load_expert(3, 3, s_exp[3])
                with sp.Fori(0, E // NSLOT - 1) as r:
                    for q in range(NSLOT):
                        if q % 2 == 0:
                            sp.wait_ge(S["y1"], 2 * r + (done + q // 2 + 1))
                            settle()
                        load_expert(4 * r + (NSLOT + q), q, s_exp[q])
                first_done = done + PAIRS
                sp.wait_ge(S["plan"], 2 * l + 2)
                extra = sp.value_load(xpairs[0:1, 0:1], min_val=1, max_val=XP_MAX)
                with sp.Fori(0, extra) as x:
                    e = [sp.value_load(xexp[0:1, bass.ds(2 * x + q, 1)], min_val=0, max_val=E - 1) for q in range(2)]
                    sp.wait_ge(S["low_read"], x + (xdone + PAIRS // 2 * (l + 1)))
                    settle()
                    for q in range(2):
                        load_expert(e[q], q, s_xw)
                done, xdone = extra + (done + PAIRS), extra + xdone

        @block.gpsimd
        def _(pool):
            def small_loads(l):
                for dst, src in ((w_uq[:], I["c_w_uq"][l].rearrange("(k p) n -> p k n", p=P)),
                                 (w_ukv[:], I["c_w_ukv"][l]),
                                 (w_router[:], I["router_w"][l].rearrange("(k p) n -> p k n", p=P)),
                                 (rbias[:], I["router_bias"][l:l + 1, :].to_broadcast([P, E])),
                                 (kvg[:], I["c_kv_norm_g"][l:l + 1, :].to_broadcast([P, CKV])),
                                 (sink[:, 0:A_H], I["a_sink"][l:l + 1, :].to_broadcast([P, A_H])),
                                 (cache_ak, I["cache_a_k"][0, l].rearrange("t h d -> t (h d)")),
                                 (cache_av, I["cache_a_v"][0, l].rearrange("t h d -> t (h d)")),
                                 (cache_bk, I["cache_b_k"][0, l].rearrange("t h d -> t (h d)")),
                                 (cache_bv, I["cache_b_v"][0, l].rearrange("t h d -> t (h d)")),
                                 (cache_ckv, I["cache_c_kv"][0, l]),
                                 (cache_kr, I["cache_c_krope"][0, l])):
                    pool.dma_start(dst, src).then_inc(s_small, 16)

            def bias_table(l):
                for h in range(B_H):
                    for r in range(3):
                        out = bass.AP(skew.tensor, skew.offset + (h * 3 + r) * BB,
                                      [[BW + 1, GRID_W], [1, RPB_C]])
                        rr = NA_KH - ROWS + r
                        src = I["b_rpb"][l, h, rr:rr + 1, :].to_broadcast([GRID_W, RPB_C])
                        pool.dma_start(out, src).then_inc(s_skew1, 16)

            pool.memset(ones[:], 1.0).then_inc(s_set, 1)
            pool.memset(mhalf[:], -0.5).then_inc(s_set, 1)
            pool.memset(csilu[:], 0.0).then_inc(s_set, 1)
            pool.memset(sink[:], NEG).then_inc(s_set, 1)
            pool.memset(xg[:], 0.0).then_inc(s_set, 1)
            pool.wait_ge(s_set, 5)
            sz = B_H * 3 * BB
            pool.dma_start(bass.AP(skew.tensor, skew.offset, [[sz // P, P], [1, sz // P]]),
                           xg[:, :, :].rearrange("p a b -> p (a b)")[:, 0:sz // P]).then_inc(s_skew0, 16)
            small_loads(0)
            pool.wait_ge(s_skew0, 16)
            bias_table(0)
            for l in range(DEPTH):
                pool.wait_ge(s_skew1, 16 * 12 * (l + 1))
                if l:
                    pool.wait_ge(S["o"], 2 * l)
                for r in range(ROWS):
                    for c in range(ROWS):
                        rr = c - r + ROWS - 1
                        src = bass.AP(skew.tensor, skew.offset + rr * BB + NA_KW - 1,
                                      [[BW, GRID_W], [3 * BB, B_H], [1, GRID_W]])
                        pool.dma_start(bias_b[r * GRID_W:(r + 1) * GRID_W, :, c * GRID_W:(c + 1) * GRID_W],
                                       src).then_inc(s_bias, 16)
                pool.wait_ge(s_set, 5)
                pool.wait_ge(S["ms"], 2 * l + 1)
                pool.tensor_tensor(rs[:], ms[:], mhalf[:, 0:NG], ALU.pow).then_inc(S["rs"], 1)
                pool.wait_ge(S["z_d"], 4 * l + 2)
                pool.wait_ge(S["z_a"], 4 * l + 2)
                for out, o, w in ((new_ak, O_KA, A_KV * HD), (new_av, O_VA, A_KV * HD),
                                  (new_bk, O_KB, B_H * HD), (new_bv, O_VB, B_H * HD)):
                    pool.dma_start(out[0, l].rearrange("t h d -> t (h d)"), z[:, 0, o:o + w]).then_inc(s_out, 16)
                pool.dma_start(new_kr[0, l], z[:, 0, O_KR:IN_COLS]).then_inc(s_out, 16)
                pool.wait_ge(S["stat_d"], l + 1)
                pool.tensor_tensor(rst[:], st[:], mhalf[:, 0:4], ALU.pow).then_inc(S["stat_r"], 1)
                pool.wait_ge(S["lat_d"], l + 1)
                pool.dma_start(new_ckv[0, l], z[:, 0, O_CKV:O_KR]).then_inc(s_out, 16)
                pool.wait_ge(S["ms"], 2 * l + 2)
                pool.tensor_tensor(rs[:], ms[:], mhalf[:, 0:NG], ALU.pow).then_inc(S["rs"], 1)
                if l + 1 < DEPTH:
                    pool.wait_ge(S["nb"], l + 1)
                    small_loads(l + 1)
                    bias_table(l + 1)
            pool.wait_ge(S["ms"], 2 * DEPTH + 1)
            pool.tensor_tensor(rs[:], ms[:], mhalf[:, 0:NG], ALU.pow).then_inc(S["rs"], 1)
            pool.wait_ge(S["fin_c"], 2)
            pool.dma_start(y_prompt[0], wide[:, 0, :]).then_inc(s_out, 16)
            pool.dma_start(y_sample[0], wide[:, 1, :]).then_inc(s_out, 16)
            pool.wait_ge(s_out, 16 * (6 * DEPTH + 2))

        @block.tensor
        def _(pe):
            pe.wait_ge(s_const, 16)
            pe.wait_ge(s_set, 5)
            pe.wait_ge(s_x, 32)
            for c in range(KD):
                for t in range(NG):
                    last = pe.transpose(xview[:, c, t * T:(t + 1) * T], wide[:, t, c * P:(c + 1) * P], ident)
            last.then_inc(S["xt_t"], 1)

            def sum_squares(n):
                pe.wait_ge(S["sq"], n)
                for g in range(NG):
                    for k in range(KD):
                        o = (k % 4) * 256 + g * T
                        last = pe.matmul(ps[:, 5, 2 * g:2 * g + 2], wide[:, k // 4, o:o + T], ones[:, 0:2],
                                         start=(k == 0), stop=(k == KD - 1))
                last.then_inc(S["ssq"], 1)
                pe.wait_ge(S["rdiag"], n)
                pe.matmul(ps[:, 5, 256:512], ones[:], rdiag[:].rearrange("p g n -> p (g n)"),
                          start=True, stop=True).then_inc(S["rs_mm"], 1)

            pe.wait_ge(s_vec, 16 * 7 * DEPTH)
            for l in range(DEPTH):
                last = pe.transpose(ps[:, 4, l * P:l * P + V_ROWS], vec_rows[:, l, :], ident[0:V_ROWS, 0:V_ROWS])
            last.then_inc(S["vec_t"], 1)
            pe.wait_ge(S["csilu"], 1)

            def ada_part(third, part):
                ent = ("ada", *third, part)
                pe.wait_ge(s_ent[0][ent], 16)
                for k in range(*ADA_K[part]):
                    for q in range(4):
                        o = (k - ADA_K[part][0]) * 2048 + q * 512
                        last = pe.matmul(ps[32 * q:32 * q + 32, 7, :], csilu[:, k, :], ring[:, slots[0][ent], o:o + 512],
                                         start=(k == 0), stop=(k == KD - 1))
                last.then_inc(S["ada_mm"], 1)

            def ada_turn(n):
                pe.wait_ge(S["ada_c"], n + 1)
                for j in range(4):
                    last = pe.transpose(ps[:, 6, j * P:(j + 1) * P], ada_sb[:, j * P:(j + 1) * P], ident)
                last.then_inc(S["ada_t"], 1)

            for part in range(3):
                ada_part(ada_early, part)
            ada_turn(0)

            done = xdone = 0
            for l in range(DEPTH):
                sum_squares(2 * l + 1)
                pe.wait_ge(S["ht_d"], 2 * l + 1)
                pe.wait_ge(S["ht_a"], 2 * l + 1)
                for i in range(3):
                    pe.wait_ge(s_ent[l][("in", i)], 16)
                    for k in range(*WIN_K[i]):
                        for t in range(NG):
                            for n in range(4):
                                o = (k - WIN_K[i][0]) * IN_COLS + n * NZ
                                last = pe.matmul(ps[:, 4 * t + n, 0:NZ], ht[:, k, t * T:(t + 1) * T],
                                                 ring[:, slots[l][("in", i)], o:o + NZ],
                                                 start=(k == 0), stop=(k == KD - 1))
                            if k == KD - 1:
                                last.then_inc(S["z_mm"] if t == 0 else S["win_mm"], 1)
                    if i < 2:
                        last.then_inc(S["win_mm"], 1)
                pe.wait_ge(S["lat_d"], l + 1)
                for t in range(NG):
                    for c in range(2):
                        last = pe.transpose(ps[:, 0, (2 * c + t) * T:(2 * c + t + 1) * T],
                                            z[:, t, O_CQ + c * P:O_CQ + (c + 1) * P], ident)
                last.then_inc(S["kcq_t"], 1)
                pe.wait_ge(s_small, 16 * 12 * (l + 1))
                for i in range(KEYT):
                    src = cache_ckv if i == 2 else z[:, i, O_CKV:O_KR]
                    last = pe.transpose(ps[:, 1, i * T:(i + 1) * T], src, ident)
                last.then_inc(S["kcq_t"], 1)
                if l == 0:
                    ada_part(ada_late[0], 0)
                    ada_part(ada_late[0], 1)
                pe.wait_ge(S["kcq_c"], 2 * l + 2)
                half = C_H * CD // 2
                for t in range(NG):
                    for n in range(2):
                        for c in range(2):
                            last = pe.matmul(ps[:, 2 + 2 * t + n, 0:half], cqt[:, c, t, :],
                                             w_uq[:, c, n * half:(n + 1) * half], start=(c == 0), stop=(c == 1))
                    last.then_inc(S["qkv_mm"], 1)
                for i in range(KEYT):
                    b = 2 * i
                    if i:
                        pe.wait_ge(S["qkv_c"], 5 * l + i)
                    for n in range(2):
                        last = pe.matmul(ps[:, b + n, 0:384], ckvt[:, i, :], w_ukv[:, n * 384:(n + 1) * 384],
                                         start=True, stop=True)
                    last.then_inc(S["qkv_mm"], 1)
                if l == 0:
                    ada_part(ada_late[0], 2)
                sets = k_sets + q_sets[0] + q_sets[1]
                pe.wait_ge(S["rope"], l + 1)
                pe.wait_ge(S["qkv_c"], 5 * l + 5)

                def head_set(n):
                    kind, i, h0 = sets[n]
                    if n >= 6:
                        if n % 2 == 0:
                            pe.wait_ge(S["qk_d"], QK_D * l + (n - 6) // 2 + 1)
                        else:
                            pe.wait_ge(S["qk_a"], QK_A * l + (n - 6) // 2 + 1)
                    for j in range(4):
                        if kind == "q":
                            src, d = query_of(h0 + j, i), dim_of(h0 + j)
                        else:
                            src = key_of(h0 + j, i)
                            d = HD if h0 + j < A_KV + B_H else CD
                        last = pe.transpose(ps[0:d, n % 6, j * T:(j + 1) * T], src, ident)
                    last.then_inc(S["qk_t"], 1)

                for n in range(NKQ):
                    head_set(n)
                pe.wait_ge(S["qk_d"], QK_D * l + QK_D0)
                pe.wait_ge(S["qk_a"], QK_A * l + QK_A0)
                if l == 0:
                    ada_turn(1)

                def scores(n):
                    t, h0, nh = score_groups[n]
                    b = n % 2
                    tiles = (0,) if t == 0 else (1, 2)
                    if n >= 2:
                        pe.wait_ge(S["prob"], NSG * l + n - 1)
                    for j in range(nh):
                        h = h0 + j
                        d = dim_of(h)
                        for m, i in enumerate(tiles):
                            o = (j * len(tiles) + m) * T
                            last = pe.matmul(ps[:, b, o:o + T], qt[0:d, h, :], kt[0:d, i, key_head(h), :],
                                             start=True, stop=True)
                    last.then_inc(S["s_mm"], 1)

                def probs_by_key(n):
                    pe.wait_ge(S["prob"], NSG * l + n + 1)
                    for j in range(4):
                        last = pe.transpose(ps[:, 2 + n % 2, j * T:(j + 1) * T], pr[:, n % 2, j * T:(j + 1) * T], ident)
                    last.then_inc(S["p_t"], 1)

                def weighted_values(n):
                    t, h0, nh = score_groups[n]
                    tiles = (0,) if t == 0 else (1, 2)
                    pe.wait_ge(S["pt_c"], NSG * l + n + 1)
                    if n == 4:
                        pe.wait_ge(S["o"], 2 * l + 1)
                    for j in range(nh):
                        h = h0 + j
                        for m, i in enumerate(tiles):
                            o = (j * len(tiles) + m) * T
                            last = pe.matmul(ps[:, 4 + h // 8, (h % 8) * HD:(h % 8 + 1) * HD],
                                             pt[:, n % 2, o:o + T], value_of(h, i),
                                             start=(m == 0), stop=(m == len(tiles) - 1))
                    last.then_inc(S["pv"], 1)

                scores(0)
                scores(1)
                for n in range(NSG):
                    probs_by_key(n)
                    if n + 2 < 4:
                        scores(n + 2)
                    if n >= 1 and n != 4:
                        weighted_values(n - 1)
                    if n == 3:
                        weighted_values(3)
                        if l == 0:
                            ada_turn(2)
                            pe.wait_ge(S["ada_add"], 3)
                        for m in range(4):
                            kind, i, h0 = q_sets[1][m]
                            if m:
                                name, at = ("qk_a", QK_A * l + QK_A0) if m % 2 == 0 else ("qk_d", QK_D * l + QK_D0)
                                pe.wait_ge(S[name], at + (m + 1) // 2)
                            for j in range(4):
                                last = pe.transpose(ps[0:dim_of(h0 + j), 6, j * T:(j + 1) * T],
                                                    query_of(h0 + j, i), ident)
                            last.then_inc(S["qk_t"], 1)
                        pe.wait_ge(S["qk_d"], QK_D * (l + 1))
                        pe.wait_ge(S["qk_a"], QK_A * (l + 1))
                        scores(4)
                        scores(5)
                    if n >= 4 and n + 2 < NSG:
                        scores(n + 2)
                    if l == 0:
                        if n in (6, 9):
                            ada_turn(n // 3 + 1)
                        ada_part(ada_late[1 + n // 3], n % 3)
                weighted_values(NSG - 1)
                if l == 0:
                    ada_turn(5)
                for t in range(NG):
                    pe.wait_ge(S["o"], 2 * l + t + 1)
                    for c in range(KD):
                        last = pe.transpose(xview[:, c, t * T:(t + 1) * T], wide[:, t, c * P:(c + 1) * P], ident)
                last.then_inc(S["o_t"], 1)
                pe.wait_ge(S["ot_c"], 2 * l + 2)
                if l == 0:
                    pe.wait_ge(S["ada_add"], 6)
                for i in range(2):
                    pe.wait_ge(s_ent[l][("out", i)], 16)
                for c in range(KD):
                    for k in range(KD):
                        w = ring[:, slots[l][("out", k // 4)], (k % 4) * D + c * P:(k % 4) * D + (c + 1) * P]
                        last = pe.matmul(ps[:, 4 + c // 2, (c % 2) * 256:(c % 2) * 256 + 256], w, ht[:, k, :],
                                         start=(k == 0), stop=(k == KD - 1))
                    if c % 4 == 3:
                        last.then_inc(S["y_mm"], 1)
                pe.wait_ge(S["x1"], 2 * l + 2)
                sum_squares(2 * l + 2)
                pe.wait_ge(S["ht_d"], 2 * l + 2)
                pe.wait_ge(S["ht_a"], 2 * l + 2)
                for t in range(NG):
                    for k in range(KD):
                        last = pe.matmul(ps[:, 4, t * E:(t + 1) * E], ht[:, k, t * T:(t + 1) * T], w_router[:, k, :],
                                         start=(k == 0), stop=(k == KD - 1))
                last.then_inc(S["logit"], 1)
                for t in range(NG):
                    for c in range(KD):
                        last = pe.transpose(ps[:, 2 * t + c // 4, (c % 4) * P:(c % 4 + 1) * P],
                                            ht[:, c, t * T:(t + 1) * T], ident)
                    last.then_inc(S["h2_t"], 1)
                pe.wait_ge(s_ent[l][("shared", 0)], 48)
                q = slots[l][("shared", 0)]
                for t in range(NG):
                    for k in range(KD):
                        last = pe.matmul(ps[:, 6 + t, :], ht[:, k, t * T:(t + 1) * T], gu_of(q, k),
                                         start=(k == 0), stop=(k == KD - 1))
                    last.then_inc(S["sh_mm"], 1)
                pe.wait_ge(S["mask"], l + 1)
                pe.matmul(ps[:, 4, 0:E], tbl[:, C_UP:C_UP + P], mask[:, 0, :], start=True, stop=True)
                pe.matmul(ps[:, 4, E:2 * E], tbl[:, C_UP:C_UP + P], mask[:, 1, :], start=True, stop=False)
                pe.matmul(ps[:, 4, E:2 * E], ones[:], mask[:, 0, :], start=False, stop=True).then_inc(S["pos_mm"], 1)
                for t in range(NG):
                    last = pe.matmul(ps[0:E, 5, 0:2], mask[:, t, :], ones[:, 0:2], start=(t == 0), stop=(t == 1))
                last.then_inc(S["cnt_mm"], 1)
                pe.wait_ge(S["sh_a"], 2 * l + 2)
                for t in range(NG):
                    for c in range(2):
                        last = pe.transpose(ps[:, 7, c * 256 + t * T:c * 256 + (t + 1) * T],
                                            act_[:, t, c * P:(c + 1) * P], ident)
                last.then_inc(S["sh_t"], 1)
                pe.wait_ge(S["nb"], l + 1)
                pe.matmul(ps[0:XU, 5, 128:128 + 2 * E], nbb[:, 0:XU], tbl[0:E, C_CUM:C_CUM + 2 * E],
                          start=True, stop=True).then_inc(S["cum_mm"], 1)
                pe.wait_ge(S["sht_c"], l + 1)
                pe.wait_ge(S["h2_d"], l + 1)
                pe.wait_ge(S["h2_a"], l + 1)
                for c in range(KD):
                    for k in range(2):
                        last = pe.matmul(xview[:, c, :], down_of(q)[:, k, c * P:(c + 1) * P], sht[:, k, :],
                                         start=(c % 2 == 0 and k == 0), stop=(k == 1), skip_group_check=True)
                last.then_inc(S["sh_acc"], 1)
                pe.wait_ge(S["inr"], l + 1)
                pe.transpose(ps[0:E, 5, 0:XU], inr[:], ident[0:XU, 0:XU]).then_inc(S["one_t"], 1)
                pe.matmul(ps[:, 5, 64:64 + 2 * XU], ones[0:XU, :], diag[:], start=True, stop=True)\
                    .then_inc(S["one_t"], 1)
                for i in range(4):
                    src = (pos1 if i < 2 else wu)[:, i % 2, 0:E]
                    last = pe.transpose(ps[0:E, 6, i * T:(i + 1) * T], src, ident)
                last.then_inc(S["ext_mm"], 1)
                pe.wait_ge(S["oneh"], l + 1)
                for i in range(4):
                    last = pe.matmul(ps[:, 7, i * XU:(i + 1) * XU], sa[0:E, i * T:(i + 1) * T], oneh[:],
                                     start=True, stop=True)
                last.then_inc(S["ext_mm"], 1)

                def gather(G):
                    pe.wait_ge(S["sel"], G + 1)
                    yield
                    for b in range(2):
                        for c in range(4 * b, 4 * b + 4):
                            for t in range(NG):
                                last = pe.matmul(ps[:, 4 + b, (c % 4) * P:(c % 4 + 1) * P],
                                                 h2[:, t, c * P:(c + 1) * P], pick[:, t, :],
                                                 start=(t == 0), stop=(t == 1))
                        last.then_inc(S["ga" if b == 0 else "gb"], 1)
                        yield

                def pair(J, at, landed, count):
                    G = J + l
                    pe.wait_ge(S["xga"], G + 1)
                    pe.wait_ge(S["xgb"], G + 1)
                    for s in landed:
                        pe.wait_ge(s, count)
                    for k in range(KD):
                        for e in range(2):
                            last = pe.matmul(ps[CAP * e:CAP * (e + 1), 6, :], xg[:, k, CAP * e:CAP * (e + 1)],
                                             gu_of(at[e], k), start=(k == 0), stop=(k == KD - 1))
                    last.then_inc(S["gu"], 1)
                    g = gather(G + 1)
                    next(g)
                    next(g)
                    pe.wait_ge(S["sw"], G + 1)
                    pe.wait_ge(S["a"], J + 1)
                    for t in range(NG):
                        pe.transpose(ps[:, 7, t * T:(t + 1) * T], pickw[:, t, :], ident)
                    for c in range(2):
                        last = pe.transpose(ps[:, 7, 256 + c * P:256 + (c + 1) * P], act_[:, 0, c * P:(c + 1) * P], ident)
                    last.then_inc(S["tt"], 1)
                    next(g)
                    pe.wait_ge(S["sa"], J + 1)
                    for b in range(2):
                        pe.wait_ge(S["xga" if b == 0 else "xgb"], G + 2)
                        for k in range(2):
                            for e in range(2):
                                last = pe.matmul(ps[CAP * e:CAP * (e + 1), 4 + b, :],
                                                 sa[:, 256 + k * P + CAP * e:256 + k * P + CAP * (e + 1)],
                                                 down_of(at[e])[:, k, b * 512:(b + 1) * 512],
                                                 start=(k == 0), stop=(k == 1))
                        last.then_inc(S["y0" if b == 0 else "y1"], 1)
                    for c in range(KD):
                        if c % 4 == 0:
                            pe.wait_ge(S["ya" if c == 0 else "yb"], J + 1)
                        last = pe.matmul(xview[:, c, :], ysb[:, c * P:(c + 1) * P], sa[:, 0:NG * T],
                                         start=False, stop=True, skip_group_check=True)
                    if at[0] == 0:
                        last.then_inc(S["low_read"], 1)

                pe.wait_ge(S["plan"], 2 * l + 2)
                for _ in gather(done + l):
                    pass
                with pe.Fori(0, PAIRS // 2) as r:
                    for b in range(2):
                        pair(2 * r + (done + b), (2 * b, 2 * b + 1), s_exp[2 * b:2 * b + 2],
                             48 * r + 48 * (l * PAIRS // 2 + 1))
                extra = pe.value_load(xpairs[0:1, 0:1], min_val=1, max_val=XP_MAX)
                with pe.Fori(0, extra) as x:
                    pair(x + (done + PAIRS), (0, 1), [s_xw], (x + (xdone + 1)) * 96)
                done, xdone = extra + (done + PAIRS), extra + xdone
                pe.wait_ge(S["xga"], done + l + 1)
                pe.wait_ge(S["xgb"], done + l + 1)
            sum_squares(2 * DEPTH + 1)
            pe.wait_ge(S["fin"], 1)
            for t in range(NG):
                for c in range(KD):
                    last = pe.transpose(ps[:, 2 * t + c // 4, (c % 4) * P:(c % 4 + 1) * P],
                                        ht[:, c, t * T:(t + 1) * T], ident)
                last.then_inc(S["fin_t"], 1)

        @block.scalar
        def _(act):
            own = [0]

            def then(ins):
                own[0] += 1
                ins.then_inc(s_act, 1)
                act.wait_ge(s_act, own[0])

            def squares():
                act.activation(wide[:].rearrange("p a b -> p (a b)"), xt[:].rearrange("p a b -> p (a b)"),
                               ACT.Square).then_inc(S["sq"], 1)

            for l in range(DEPTH):
                for lo, src in ((V_B, I["b_ada"][l].rearrange("(r p) -> r p", p=P)),
                                (V_N1, I["norm1_g"][l].rearrange("(r p) -> r p", p=P)),
                                (V_N2, I["norm2_g"][l].rearrange("(r p) -> r p", p=P)),
                                (V_QG, I["c_q_norm_g"][l].rearrange("(r p) -> r p", p=P)),
                                (V_C, I["c_ctx"].rearrange("(r p) -> r p", p=P)),
                                (V_C + KD, I["c"][0].rearrange("(r p) -> r p", p=P)),
                                (V_F, I["final_norm_g"].rearrange("(r p) -> r p", p=P))):
                    act.dma_start(vec_rows[lo:lo + src.shape[0], l, :], src).then_inc(s_vec, 16)
            act.wait_ge(S["xt_t"], 1)
            act.activation(xt[:, 4:8, :], xview[:, 4:8, :], ACT.Copy).then_inc(S["xt_c"], 1)
            done = xdone = 0
            for l in range(DEPTH):
                mod = modl[:, l]
                if l == 0:
                    act.wait_ge(S["cols_c"], 1)
                    act.activation(ctanh[:].rearrange("p a b -> p (a b)"), colsl[:, 0, V_C:V_C + 2 * KD], ACT.Tanh,
                                   scale=0.5).then_inc(S["ctanh"], 1)
                act.wait_ge(S["xt_c"], 2)
                if l:
                    act.wait_ge(S["x2"], l)
                squares()
                act.wait_ge(S["hn"], 2 * l + 1)
                act.wait_ge(S["mod"], 2 * l + 1)
                for c in range(4, KD):
                    for g in range(NG):
                        last = act.activation(ht[:, c, g * T:(g + 1) * T], ht[:, c, g * T:(g + 1) * T], ACT.Identity,
                                              scale=gs1[:, c, g:g + 1], bias=mod[:, c, g:g + 1])
                last.then_inc(S["ht_a"], 1)
                for t in range(NG):
                    act.wait_ge(S["z_mm"] if t == 0 else S["win_mm"], l + 1 if t == 0 else 3 * l + 3)
                    for n in (1, 3):
                        act.activation(z[:, t, n * NZ:(n + 1) * NZ], ps[:, 4 * t + n, 0:NZ], ACT.Copy)\
                            .then_inc(S["z_a"], 1)
                act.wait_ge(S["z_d"], 4 * l + 4)
                act.wait_ge(S["z_a"], 4 * l + 4)
                for t in range(NG):
                    act.activation(wide[:, t, 0:CQ], z[:, t, O_CQ:O_CKV], ACT.Square, accum_out=st[:, t:t + 1])
                    last = act.activation(wide[:, t, CQ:CQ + CKV], z[:, t, O_CKV:O_KR], ACT.Square,
                                          accum_out=st[:, 2 + t:3 + t])
                last.then_inc(S["stat_a"], 1)
                act.wait_ge(S["kcq_t"], 2 * l + 2)
                act.activation(ckvt[:].rearrange("p a b -> p (a b)"), ps[:, 1, 0:KEYT * T], ACT.Copy)\
                    .then_inc(S["kcq_c"], 1)
                sets = k_sets + q_sets[0] + q_sets[1]
                for n in range(1, NKQ, 2):
                    act.wait_ge(S["qk_t"], QK_T * l + n + 1)
                    copy_heads(act, sets, n, n % 6, True)
                def probs(n):
                    t, h0, nh = score_groups[n]
                    w = 512 // nh
                    act.wait_ge(S["nmax"], NSG * l + n + 1)
                    if n >= 2:
                        act.wait_ge(S["p_t"], NSG * l + n - 1)
                    for j in range(nh):
                        last = act.activation(pr[:, n % 2, j * w:(j + 1) * w], ps[:, n % 2, j * w:(j + 1) * w], ACT.Exp,
                                              bias=nmax[:, h0 + j:h0 + j + 1], accum_out=sums[:, h0 + j:h0 + j + 1])
                    last.then_inc(S["prob"], 1)

                def key_copy(n):
                    act.wait_ge(S["p_t"], NSG * l + n + 1)
                    if n >= 2:
                        act.wait_ge(S["pv"], NSG * l + n - 1)
                    act.activation(pt[:, n % 2, :], ps[:, 2 + n % 2, :], ACT.Copy).then_inc(S["pt_c"], 1)

                for n in range(NSG):
                    if n == 4:
                        key_copy(3)
                        act.wait_ge(S["esum"], 2 * l + 1)
                        act.activation(esink[:], esink[:], ACT.Exp).then_inc(S["esink"], 1)
                        for m in range(1, 4, 2):
                            act.wait_ge(S["qk_t"], QK_T * l + NKQ + m + 1)
                            copy_heads(act, sets, NKQ + m, 6, True)
                    probs(n)
                    if n >= 1 and n != 4:
                        key_copy(n - 1)
                key_copy(NSG - 1)
                act.wait_ge(S["esum"], 2 * l + 2)
                act.activation(esink[:], esink[:], ACT.Exp).then_inc(S["esink"], 1)
                act.wait_ge(S["o_t"], l + 1)
                act.activation(ht[:, 4:8, :], xview[:, 4:8, :], ACT.Copy).then_inc(S["ot_c"], 1)
                act.wait_ge(S["x1"], 2 * l + 2)
                squares()
                act.wait_ge(S["hn"], 2 * l + 2)
                act.wait_ge(S["mod"], 2 * l + 2)
                for c in range(4, KD):
                    for g in range(NG):
                        last = act.activation(ht[:, c, g * T:(g + 1) * T], ht[:, c, g * T:(g + 1) * T], ACT.Identity,
                                              scale=gs2[:, c, g:g + 1], bias=mod[:, 24 + c, g:g + 1])
                last.then_inc(S["ht_a"], 1)
                act.wait_ge(S["logit"], l + 1)
                act.activation(score[:].rearrange("p a b -> p (a b)"), ps[:, 4, 0:NG * E], ACT.Tanh, scale=0.5)\
                    .then_inc(S["rtanh"], 1)
                act.wait_ge(S["h2_t"], 2 * l + 2)
                act.wait_ge(s_out, 96 * (l + 1))
                move_tokens(act, 1, True)
                for t in range(NG):
                    act.wait_ge(S["sh_mm"], 2 * l + t + 1)
                    if t:
                        act.wait_ge(S["sh_a"], 2 * l + 1)
                    act.activation(th[:], ps[:, 6 + t, 0:DE], ACT.Tanh, scale=0.5).then_inc(S["sh_th"], 1)
                act.wait_ge(S["sh_t"], l + 1)
                act.activation(sht[:].rearrange("p a b -> p (a b)"), ps[:, 7, :], ACT.Copy).then_inc(S["sht_c"], 1)

                def copy_second(G):
                    act.wait_ge(S["gb"], G + 1)
                    act.activation(xg[:, 4:8, :].rearrange("p a b -> p (a b)"), ps[:, 5, :], ACT.Copy)\
                        .then_inc(S["xgb"], 1)

                def pair(J):
                    act.wait_ge(S["gu"], J + 1)
                    act.activation(th[:], ps[:, 6, 0:DE], ACT.Tanh, scale=0.5).then_inc(S["th"], 1)
                    act.wait_ge(S["tt"], J + 1)
                    act.activation(sa[:], ps[:, 7, :], ACT.Copy).then_inc(S["sa"], 1)
                    copy_second(J + (l + 1))
                    act.wait_ge(S["y1"], J + 1)
                    act.activation(ysb[:, 512:1024], ps[:, 5, :], ACT.Copy).then_inc(S["yb"], 1)

                act.wait_ge(S["plan"], 2 * l + 2)
                copy_second(done + l)
                with act.Fori(0, PAIRS) as r:
                    pair(r + done)
                extra = act.value_load(xpairs[0:1, 0:1], min_val=1, max_val=XP_MAX)
                with act.Fori(0, extra) as x:
                    pair(x + (done + PAIRS))
                done, xdone = extra + (done + PAIRS), extra + xdone
            act.wait_ge(S["x2"], DEPTH)
            squares()
            act.wait_ge(S["fin_t"], 2)
            act.activation(wide[:, 1, :].rearrange("p (a b) -> p a b", a=2), ps[:, 2:4, :], ACT.Copy)\
                .then_inc(S["fin_c"], 1)

        @block.vector
        def _(dve):
            own = [0]

            def then(ins):
                own[0] += 1
                ins.then_inc(s_dve, 1)
                dve.wait_ge(s_dve, own[0])

            def norm(n, gs=None, shift=None, mod=None):
                dve.wait_ge(S["ssq"], n)
                dve.tensor_scalar(ms[:], ps[:, 5, 0:4].rearrange("p (g c) -> p g c", g=NG)[:, :, 0], 1.0 / D, EPS,
                                  ALU.mult, ALU.add).then_inc(S["ms"], 1)
                dve.wait_ge(S["rs"], n)
                for g in range(NG):
                    last = dve.tensor_scalar(rdiag[:, g, :], ident, rs[:, g:g + 1], None, ALU.mult)
                last.then_inc(S["rdiag"], 1)
                dve.wait_ge(S["rs_mm"], n)
                rsb = ps[:, 5, 256:512].unsqueeze(1).to_broadcast([P, 4, NG * T])
                dve.tensor_tensor(ht[:, 4:8, :], xt[:, 4:8, :], rsb, ALU.mult).then_inc(S["hn"], 1)
                then(dve.tensor_tensor(ht[:, 0:4, :], xt[:, 0:4, :], rsb, ALU.mult))
                if gs is not None:
                    for c in range(4):
                        for g in range(NG):
                            last = dve.tensor_scalar(ht[:, c, g * T:(g + 1) * T], ht[:, c, g * T:(g + 1) * T],
                                                     gs[:, c, g:g + 1], mod[:, shift + c, g:g + 1], ALU.mult, ALU.add)
                    last.then_inc(S["ht_d"], 1)

            dve.wait_ge(S["xt_t"], 1)
            dve.tensor_copy(xt[:, 0:4, :], xview[:, 0:4, :]).then_inc(S["xt_c"], 1)
            dve.wait_ge(S["vec_t"], 1)
            dve.tensor_copy(colsl[:], ps[:, 4, 0:DEPTH * P].rearrange("p (l r) -> p l r", l=DEPTH)[:, :, 0:V_ROWS])\
                .then_inc(S["cols_c"], 1)
            dve.wait_ge(S["ctanh"], 1)
            dve.wait_ge(s_set, 5)
            then(dve.scalar_tensor_tensor(ctanh[:].rearrange("p a b -> p (a b)"),
                                          ctanh[:].rearrange("p a b -> p (a b)"), 1.0,
                                          colsl[:, 0, V_C:V_C + 2 * KD], ALU.add, ALU.mult))
            dve.tensor_scalar(csilu[:, :, 0:NG].rearrange("p k g -> p g k"), ctanh[:], 0.5, None, ALU.mult)\
                .then_inc(S["csilu"], 1)

            def ada_copy(n):
                dve.wait_ge(S["ada_mm"], 3 * (n + 1))
                dve.tensor_copy(ada_sb[:], ps[:, 7, :]).then_inc(S["ada_c"], 1)

            def ada_add(n):
                al, third = ([ada_early] + ada_late)[n]
                dve.wait_ge(S["ada_t"], n + 1)
                lo = 16 * third
                dve.tensor_tensor(modl[:, al, lo:lo + 16, :].rearrange("p (q j) g -> p j q g", q=4),
                                  ps[:, 6, :].rearrange("p (j q r) -> p j q r", j=4, q=4)[:, :, :, 0:NG],
                                  colsl[:, al, V_B + lo:V_B + lo + 16].rearrange("p (q j) -> p j q", q=4).unsqueeze(3)
                                  .to_broadcast([P, 4, 4, NG]), ALU.add).then_inc(S["ada_add"], 1)

            def gains(l, gs, at, gain):
                dve.scalar_tensor_tensor(gs[:], modl[:, l, at:at + KD, :], 1.0,
                                         colsl[:, l, gain:gain + KD].unsqueeze(2).to_broadcast([P, KD, NG]),
                                         ALU.add, ALU.mult).then_inc(S["mod"], 1)
                dve.wait_ge(S["mod"], 2 * l + (1 if gs is gs1 else 2))

            ada_copy(0)
            ada_add(0)
            dve.wait_ge(S["ada_add"], 1)
            gains(0, gs1, 8, V_N1)
            done = xdone = 0
            for l in range(DEPTH):
                mod, cols = modl[:, l], colsl[:, l]
                if l:
                    gains(l, gs1, 8, V_N1)
                norm(2 * l + 1, gs1, 0, mod)
                for t in range(NG):
                    dve.wait_ge(S["z_mm"] if t == 0 else S["win_mm"], l + 1 if t == 0 else 3 * l + 3)
                    for n in (0, 2):
                        dve.tensor_copy(z[:, t, n * NZ:(n + 1) * NZ], ps[:, 4 * t + n, 0:NZ]).then_inc(S["z_d"], 1)
                dve.wait_ge(S["stat_a"], l + 1)
                dve.tensor_scalar(st[:, 0:2], st[:, 0:2], 1.0 / CQ, EPS, ALU.mult, ALU.add)
                dve.tensor_scalar(st[:, 2:4], st[:, 2:4], 1.0 / CKV, EPS, ALU.mult, ALU.add).then_inc(S["stat_d"], 1)
                dve.wait_ge(s_small, 16 * 12 * (l + 1))
                dve.wait_ge(s_bias, 64 * (l + 1))
                dve.wait_ge(s_const, 16)
                dve.tensor_tensor(bias_b[:], bias_b[:],
                                  tbl[:, C_MASK:C_MASK + T].unsqueeze(1).to_broadcast([P, B_H, T]), ALU.add)
                dve.tensor_scalar(nsink[:], sink[:], -1.0, None, ALU.mult)
                dve.wait_ge(S["stat_r"], l + 1)
                for t in range(NG):
                    dve.tensor_scalar(z[:, t, O_CQ:O_CKV], z[:, t, O_CQ:O_CKV], rst[:, t:t + 1], None, ALU.mult)
                    last = dve.scalar_tensor_tensor(z[:, t, O_CKV:O_KR], z[:, t, O_CKV:O_KR], rst[:, 2 + t:3 + t],
                                                    kvg[:], ALU.mult, ALU.mult)
                last.then_inc(S["lat_d"], 1)

                def rotate(x, at, width, heads, signal=None):
                    cos = tbl[:, at:at + width].unsqueeze(1).to_broadcast([P, heads, width])
                    sin = tbl[:, at + width:at + 2 * width].unsqueeze(1).to_broadcast([P, heads, width])
                    tmp = [rtmp[:, i, 0:heads * width].rearrange("p (h w) -> p h w", h=heads) for i in range(4)]
                    dve.tensor_tensor(tmp[0], x[:, :, 0, :], cos, ALU.mult)
                    dve.tensor_tensor(tmp[1], x[:, :, 1, :], sin, ALU.mult)
                    dve.tensor_tensor(tmp[2], x[:, :, 1, :], cos, ALU.mult)
                    then(dve.tensor_tensor(tmp[3], x[:, :, 0, :], sin, ALU.mult))
                    dve.tensor_tensor(x[:, :, 0, :], tmp[0], tmp[1], ALU.subtract)
                    last = dve.tensor_tensor(x[:, :, 1, :], tmp[2], tmp[3], ALU.add)
                    if signal is None:
                        then(last)
                    else:
                        last.then_inc(signal, 1)

                rotate(z[:, 1, 0:O_VA].rearrange("p (h s w) -> p h s w", s=2, w=32), C_ROT64, 32, A_H + A_KV)
                rotate(z[:, 1, O_KR:IN_COLS].rearrange("p (h s w) -> p h s w", s=2, w=16), C_ROT32, 16, 1)
                dve.wait_ge(S["kcq_t"], 2 * l + 1)
                for c in range(2):
                    last = dve.tensor_scalar(cqt[:, c, :, :], ps[:, 0, c * 256:(c + 1) * 256]
                                             .rearrange("p (t n) -> p t n", t=NG),
                                             cols[:, V_QG + c:V_QG + c + 1], None, ALU.mult)
                last.then_inc(S["kcq_c"], 1)
                half = C_H * CD // 2
                for t in range(NG):
                    dve.wait_ge(S["qkv_mm"], 5 * l + t + 1)
                    dve.tensor_copy(qc[:, t, :, :].rearrange("p (a h) d -> p a (h d)", a=2),
                                    ps[:, 2 + 2 * t:4 + 2 * t, 0:half]).then_inc(S["qkv_c"], 1)
                for i in range(KEYT):
                    b = 2 * i
                    dve.wait_ge(S["qkv_mm"], 5 * l + i + 3)
                    for n in range(2):
                        src = ps[:, b + n, 0:384].rearrange("p (h d) -> p h d", d=2 * HD)
                        dve.tensor_copy(kc[:, i, 3 * n:3 * n + 3, 0:CN], src[:, :, 0:CN])
                        dve.tensor_copy(vc[:, i, 3 * n:3 * n + 3, :], src[:, :, CN:])
                    kr = cache_kr if i == 2 else z[:, i, O_KR:IN_COLS]
                    dve.tensor_copy(kc[:, i, :, CN:CD], kr.unsqueeze(1).to_broadcast([P, C_H, CR]))\
                        .then_inc(S["qkv_c"], 1)
                dve.wait_ge(S["qkv_c"], 5 * l + 2)
                rotate(qc[:, 1, :, CN:CD].rearrange("p h (s w) -> p h s w", s=2), C_ROT32, 16, C_H,
                       S["rope"])
                if l == 0:
                    ada_copy(1)
                sets = k_sets + q_sets[0] + q_sets[1]
                for n in range(0, NKQ, 2):
                    dve.wait_ge(S["qk_t"], QK_T * l + n + 1)
                    copy_heads(dve, sets, n, n % 6, False)

                def maxima(n):
                    t, h0, nh = score_groups[n]
                    w = 512 // nh
                    dve.wait_ge(S["s_mm"], NSG * l + n + 1)
                    b = ps[:, n % 2, :].rearrange("p (h w) -> p h w", h=nh)
                    if t == 1 and A_H <= h0 < A_H + B_H:
                        then(dve.tensor_tensor(b[:, :, 0:T], b[:, :, 0:T], bias_b[:, h0 - A_H:h0 - A_H + nh, :], ALU.add))
                    then(dve.tensor_reduce(nmax[:, h0:h0 + nh], b, AX.X, ALU.max, negate=True))
                    dve.tensor_tensor(nmax[:, h0:h0 + nh], nmax[:, h0:h0 + nh], nsink[:, h0:h0 + nh], ALU.min)\
                        .then_inc(S["nmax"], 1)

                def finish(t):
                    dve.wait_ge(S["prob"], NSG * l + (4 if t == 0 else NSG))
                    dve.wait_ge(S["nmax"], NSG * l + (4 if t == 0 else NSG))
                    dve.tensor_tensor(esink[:], sink[:], nmax[:], ALU.add).then_inc(S["esum"], 1)
                    dve.wait_ge(S["esink"], 2 * l + t + 1)
                    then(dve.tensor_tensor(sums[:], sums[:], esink[:], ALU.add))
                    then(dve.reciprocal(rden[:], sums[:]))
                    dve.wait_ge(S["pv"], NSG * l + (4 if t == 0 else NSG))
                    dve.tensor_tensor(wide[:, t, :].rearrange("p (b h d) -> p b h d", b=2, d=HD),
                                      ps[:, 4:6, :].rearrange("p b (h d) -> p b h d", d=HD),
                                      rden[:].rearrange("p (b h) -> p b h", b=2).unsqueeze(3)
                                      .to_broadcast([P, 2, 8, HD]), ALU.mult).then_inc(S["o"], 1)

                if l == 0:
                    ada_add(1)
                for n in range(NSG):
                    if n == 4:
                        if l == 0:
                            ada_copy(2)
                            ada_add(2)
                        finish(0)
                        for m in range(0, 4, 2):
                            dve.wait_ge(S["qk_t"], QK_T * l + NKQ + m + 1)
                            copy_heads(dve, sets, NKQ + m, 6, False)
                    maxima(n)
                    if l == 0:
                        if n in (6, 9):
                            ada_copy(n // 3 + 1)
                        if n in (7, 10):
                            ada_add(n // 3 + 1)
                if l == 0:
                    ada_copy(5)
                finish(1)
                if l == 0:
                    ada_add(5)
                    dve.wait_ge(S["ada_add"], 6)
                dve.wait_ge(S["o_t"], l + 1)
                dve.tensor_copy(ht[:, 0:4, :], xview[:, 0:4, :]).then_inc(S["ot_c"], 1)
                for c in range(KD):
                    if c % 4 == 0:
                        dve.wait_ge(S["y_mm"], 2 * l + c // 4 + 1)
                    for g in range(NG):
                        o = (c % 2) * 256 + g * T
                        last = dve.scalar_tensor_tensor(xt[:, c, g * T:(g + 1) * T], ps[:, 4 + c // 2, o:o + T],
                                                        mod[:, 16 + c, g:g + 1], xt[:, c, g * T:(g + 1) * T],
                                                        ALU.mult, ALU.add)
                    if c % 4 == 3:
                        last.then_inc(S["x1"], 1)
                dve.wait_ge(S["x1"], 2 * l + 2)
                gains(l, gs2, 32, V_N2)
                norm(2 * l + 2, gs2, 24, mod)
                dve.wait_ge(S["rtanh"], l + 1)
                then(dve.tensor_scalar(score[:], score[:], 0.5, 0.5, ALU.mult, ALU.add))
                then(dve.tensor_tensor(selv[:], score[:], rbias[:].unsqueeze(1).to_broadcast([P, NG, E]), ALU.add))
                for t in range(NG):
                    for g in range(GROUPS):
                        last = dve.max(top8[:, t, g, :], selv[:, t, g * PER:(g + 1) * PER])
                then(last)
                then(dve.tensor_tensor(gsc[:], top8[:, :, :, 0], top8[:, :, :, 1], ALU.add))
                for t in range(NG):
                    other = gsc[:, t, :].unsqueeze(1).to_broadcast([P, GROUPS, GROUPS])
                    this = gsc[:, t, :].unsqueeze(2).to_broadcast([P, GROUPS, GROUPS])
                    dve.tensor_tensor(cmp1[:, t], other, this, ALU.is_gt)
                    then(dve.tensor_tensor(cmp2[:, t], other, this, ALU.is_equal))
                    then(dve.tensor_tensor(cmp2[:, t], cmp2[:, t],
                                           tbl[:, C_TIE:C_TIE + 64].rearrange("p (i j) -> p i j", i=GROUPS), ALU.mult))
                    then(dve.tensor_tensor(cmp1[:, t], cmp1[:, t], cmp2[:, t], ALU.add))
                then(dve.tensor_reduce(rank[:], cmp1[:], AX.X, ALU.add))
                then(dve.tensor_scalar(rank[:], rank[:], float(TOP_G), None, ALU.is_lt))
                for t in range(NG):
                    keep_t = rank[:, t, :].unsqueeze(2).to_broadcast([P, GROUPS, PER])
                    sel_t = selv[:, t, :].rearrange("p (g e) -> p g e", g=GROUPS)
                    rep_t = repl[:, t, :].rearrange("p (g e) -> p g e", g=GROUPS)
                    dve.tensor_tensor(sel_t, sel_t, keep_t, ALU.mult)
                    then(dve.tensor_scalar(rep_t, keep_t, -NEG, NEG, ALU.mult, ALU.add))
                then(dve.tensor_tensor(selv[:], selv[:], repl[:], ALU.add))
                for t in range(NG):
                    last = dve.max(t8[:, t, :], selv[:, t, :])
                then(last)
                then(dve.memset(t8[:, :, TOP_K:8], NEG))
                for t in range(NG):
                    last = dve.match_replace(repl[:, t, :], t8[:, t, :], selv[:, t, :], 3.0 * NEG)
                then(last)
                then(dve.tensor_scalar(mask[:], repl[:], 2.0 * NEG, None, ALU.is_lt))
                then(dve.tensor_scalar(repl[:], selv[:], 0.5 * NEG, None, ALU.is_gt))
                dve.tensor_tensor(mask[:], mask[:], repl[:], ALU.mult).then_inc(S["mask"], 1)
                dve.wait_ge(S["mask"], l + 1)
                then(dve.tensor_tensor(repl[:], score[:], mask[:], ALU.mult))
                then(dve.tensor_reduce(wsum[:], repl[:], AX.X, ALU.add))
                then(dve.reciprocal(wsum[:], wsum[:]))
                for t in range(NG):
                    last = dve.tensor_scalar(wu[:, t, 0:E], repl[:, t, :], wsum[:, t:t + 1], 0.5 * ROUTED_SCALE,
                                             ALU.mult, ALU.mult)
                then(last)
                dve.wait_ge(S["pos_mm"], l + 1)
                for t in range(NG):
                    last = dve.scalar_tensor_tensor(pos1[:, t, 0:E], ps[:, 4, t * E:(t + 1) * E], 1.0, mask[:, t, :],
                                                    ALU.add, ALU.mult)
                then(last)
                dve.wait_ge(S["cnt_mm"], l + 1)
                for i in range(1, NG * T // CAP):
                    last = dve.tensor_scalar(cnt[:, i - 1:i], ps[0:E, 5, 0:1], i * CAP + 0.5, None, ALU.is_gt)
                then(last)
                then(dve.tensor_tensor(cnt[:, 0:1], cnt[:, 0:1], cnt[:, 1:2], ALU.add))
                then(dve.tensor_tensor(cnt[:, 0:1], cnt[:, 0:1], cnt[:, 2:3], ALU.add))
                dve.tensor_scalar(nbb[:], ones[0:E, :], cnt[:, 0:1], None, ALU.mult).then_inc(S["nb"], 1)
                dve.wait_ge(S["h2_t"], 2 * l + 2)
                dve.wait_ge(s_out, 96 * (l + 1))
                move_tokens(dve, 0, False)
                for t in range(NG):
                    dve.wait_ge(S["sh_th"], 2 * l + t + 1)
                    then(dve.scalar_tensor_tensor(a1[:], th[:], 1.0, ps[:, 6 + t, 0:DE], ALU.add, ALU.mult))
                    dve.scalar_tensor_tensor(act_[:, t, :], a1[:], 0.5, ps[:, 6 + t, DE:2 * DE], ALU.mult, ALU.mult)\
                        .then_inc(S["sh_a"], 1)
                dve.wait_ge(S["cum_mm"], l + 1)
                then(dve.tensor_copy(cum[:], ps[0:XU, 5, 128:128 + 2 * E]))
                number = tbl[0:XU, C_PART:C_PART + 1]
                dve.tensor_scalar(fin[:], cum[:, 0:E], number, None, ALU.is_le)
                dve.tensor_scalar(inr[:], cum[:, E:2 * E], number, None, ALU.is_le)
                then(dve.tensor_scalar(ns[:], cum[:, E:2 * E], -1.0, number, ALU.mult, ALU.add))
                then(dve.tensor_tensor(inr[:], inr[:], fin[:], ALU.subtract))
                then(dve.tensor_tensor(ns[:], ns[:], inr[:], ALU.mult))
                dve.tensor_reduce(uv[:, 0:1], ns[:], AX.X, ALU.add)
                then(dve.tensor_reduce(uv[:, 1:2], fin[:], AX.X, ALU.add))
                dve.tensor_scalar(uv[:, 2:3], uv[:, 0:1], float(CAP), float(CAP), ALU.mult, ALU.add)
                then(dve.tensor_scalar(uv[:, 3:4], uv[:, 1:2], float(E - 1), None, ALU.min))
                dve.tensor_scalar(diag[:, 0:XU], ident[0:XU, 0:XU], uv[:, 2:3], None, ALU.mult)
                dve.tensor_scalar(diag[:, XU:2 * XU], ident[0:XU, 0:XU], uv[:, 3:4], None, ALU.mult)\
                    .then_inc(S["inr"], 1)
                then(dve.tensor_scalar(fin[0:1, 0:16], tbl[0:1, C_EVEN:C_EVEN + 16], cum[0:1, E - 1:E], None,
                                       ALU.is_lt))
                then(dve.tensor_reduce(xcount[:, 0:1], fin[0:1, 0:16], AX.X, ALU.add))
                dve.tensor_scalar(xpairs[:], xcount[:, 0:1], 1.0, None, ALU.max).then_inc(S["plan"], 1)
                dve.wait_ge(S["one_t"], 2 * l + 2)
                dve.wait_ge(S["ext_mm"], 2 * l + 1)
                dve.tensor_copy(urow[:], ps[:, 5, 64:64 + 2 * XU])
                dve.tensor_copy(sa[0:E, :], ps[0:E, 6, :])
                dve.tensor_copy(oneh[:], ps[0:E, 5, 0:XU]).then_inc(S["oneh"], 1)
                dve.wait_ge(S["ext_mm"], 2 * l + 2)
                dve.wait_ge(S["oneh"], l + 1)
                for t in range(NG):
                    dve.tensor_tensor(pos1[:, t, E:NU], ps[:, 7, t * XU:(t + 1) * XU], urow[:, 0:XU], ALU.subtract)
                    dve.tensor_copy(wu[:, t, E:NU], ps[:, 7, (2 + t) * XU:(3 + t) * XU])
                dve.tensor_copy(xexp[:], urow[0:1, XU:2 * XU]).then_inc(S["plan"], 1)
                dve.wait_ge(S["plan"], 2 * l + 2)

                def choose(u):
                    at = pos1[:, :, bass.ds(u, 2)] if not isinstance(u, int) else pos1[:, :, u:u + 2]
                    dve.tensor_tensor(pick[:].rearrange("p t (e s) -> p t e s", e=2),
                                      tbl[:, C_SLOT:C_SLOT + CAP].unsqueeze(1).unsqueeze(1)
                                      .to_broadcast([P, NG, 2, CAP]),
                                      at.unsqueeze(3).to_broadcast([P, NG, 2, CAP]), ALU.is_equal)\
                        .then_inc(S["sel"], 1)

                def weigh(u, G):
                    at = wu[:, :, bass.ds(u, 2)] if not isinstance(u, int) else wu[:, :, u:u + 2]
                    dve.wait_ge(S["sel"], G + 1)
                    dve.tensor_tensor(pickw[:].rearrange("p t (e s) -> p t e s", e=2),
                                      pick[:].rearrange("p t (e s) -> p t e s", e=2),
                                      at.unsqueeze(3).to_broadcast([P, NG, 2, CAP]), ALU.mult).then_inc(S["sw"], 1)

                def copy_first(G):
                    dve.wait_ge(S["ga"], G + 1)
                    dve.tensor_copy(xg[:, 0:4, :].rearrange("p a b -> p (a b)"), ps[:, 4, :]).then_inc(S["xga"], 1)

                def pair(j, J):
                    G = J + l
                    dve.wait_ge(S["gb"], G + 1)
                    dve.wait_ge(S["sw"], G + 1)
                    choose(2 * j + 2)
                    dve.wait_ge(S["th"], J + 1)
                    dve.scalar_tensor_tensor(a1[:], th[:], 1.0, ps[:, 6, 0:DE], ALU.add, ALU.mult).then_inc(S["cval"], 1)
                    dve.wait_ge(S["cval"], J + 1)
                    dve.tensor_tensor(act_[:, 0, :], a1[:], ps[:, 6, DE:2 * DE], ALU.mult).then_inc(S["a"], 1)
                    copy_first(G + 1)
                    dve.wait_ge(S["tt"], J + 1)
                    weigh(2 * j + 2, G + 1)
                    dve.wait_ge(S["y0"], J + 1)
                    dve.tensor_copy(ysb[:, 0:512], ps[:, 4, :]).then_inc(S["ya"], 1)

                choose(0)
                weigh(0, done + l)
                copy_first(done + l)
                with dve.Fori(0, PAIRS) as r:
                    pair(r, r + done)
                extra = dve.value_load(xpairs[0:1, 0:1], min_val=1, max_val=XP_MAX)
                with dve.Fori(0, extra) as x:
                    pair(x + PAIRS, x + (done + PAIRS))
                done, xdone = extra + (done + PAIRS), extra + xdone
                dve.wait_ge(S["low_read"], xdone + PAIRS // 2 * (l + 1))
                for c in range(KD):
                    for g in range(NG):
                        last = dve.scalar_tensor_tensor(xt[:, c, g * T:(g + 1) * T], xview[:, c, g * T:(g + 1) * T],
                                                        mod[:, 40 + c, g:g + 1], xt[:, c, g * T:(g + 1) * T],
                                                        ALU.mult, ALU.add)
                last.then_inc(S["x2"], 1)
            dve.wait_ge(S["x2"], DEPTH)
            norm(2 * DEPTH + 1)
            dve.wait_ge(S["hn"], 2 * DEPTH + 1)
            for c in range(KD):
                last = dve.tensor_scalar(ht[:, c, :], ht[:, c, :], colsl[:, 0, V_F + c:V_F + c + 1], None, ALU.mult)
            last.then_inc(S["fin"], 1)
            dve.wait_ge(S["fin_t"], 2)
            dve.tensor_copy(wide[:, 0, :].rearrange("p (a b) -> p a b", a=2), ps[:, 0:2, :]).then_inc(S["fin_c"], 1)


_INS = ["x_prompt", "x_sample", "cache_a_k", "cache_a_v", "cache_b_k", "cache_b_v", "cache_c_kv", "cache_c_krope",
        "c", "c_ctx", "norm1_g", "norm2_g", "w_ada", "b_ada", "w_in", "a_sink", "b_rpb", "c_q_norm_g", "c_w_uq",
        "c_kv_norm_g", "c_w_ukv", "w_out", "router_w", "router_bias", "exp_w_gate", "exp_w_up", "exp_w_down",
        "sh_w_gate", "sh_w_up", "sh_w_down", "final_norm_g"]
_OUTS = [(1, T, D), (1, T, D), (1, DEPTH, T, A_KV, HD), (1, DEPTH, T, A_KV, HD), (1, DEPTH, T, B_H, HD),
         (1, DEPTH, T, B_H, HD), (1, DEPTH, T, CKV), (1, DEPTH, T, CR)]


def kernel(**inputs):
    import concourse.bacc as bacc
    from concourse.bass_utils import run_bass_kernel_spmd

    nc = bacc.Bacc("TRN2", target_bir_lowering=False, num_devices=1)
    arrays, aps = {}, {}
    for name in _INS:
        a = np.ascontiguousarray(inputs[name])
        arrays[f"in_{name}"] = a
        aps[name] = nc.dram_tensor(f"in_{name}", a.shape, mybir.dt.from_np(a.dtype), kind="ExternalInput").ap()
    arrays["consts"] = constants()
    consts = nc.dram_tensor("consts", (P, C_COLS), F32, kind="ExternalInput").ap()
    skew = nc.dram_tensor("skew", (B_H, 3, BB), F32, kind="Internal").ap()
    outs = [nc.dram_tensor(f"out_{i}", s, F32, kind="ExternalOutput").ap() for i, s in enumerate(_OUTS)]
    backbone(nc, aps, consts, skew, outs)
    r = run_bass_kernel_spmd(nc, [arrays], core_ids=[0])
    return tuple(r.results[0][f"out_{i}"] for i in range(len(_OUTS)))
```

```python
from contextlib import ExitStack

import numpy as np
import concourse.bass as bass
from concourse import mybir

F32 = mybir.dt.float32
BF16 = mybir.dt.bfloat16
I32 = mybir.dt.int32
ALU = mybir.AluOpType
ACT = mybir.ActivationFunctionType
AX = mybir.AxisListType

P = 128
DEPTH, D, T = 2, 1024, 128
KD = D // P
NG = 2
HD, NH = 64, 16
A_H, A_KV, B_H, C_H = 6, 2, 4, 6
A_GROUP = A_H // A_KV
CQ, CKV, CR, CN = 256, 128, 32, 64
CD = CN + CR
WIDTHS = (A_H * HD, A_KV * HD, A_KV * HD, B_H * HD, B_H * HD, B_H * HD, CQ, CKV, CR)
OFF = [sum(WIDTHS[:i]) for i in range(len(WIDTHS) + 1)]
O_QA, O_KA, O_VA, O_QB, O_KB, O_VB, O_CQ, O_CKV, O_KR, IN_COLS = OFF
NZ = IN_COLS // 4
HEAD_SCALE = HD ** -0.5
C_SCALE = CD ** -0.5
GRID_W, NA_KH, NA_KW = 64, 8, 16
ROWS = T // GRID_W
EPS = 1e-6
NEG = -1e30
E, TOP_K, GROUPS, TOP_G, DE = 64, 6, 8, 4, 256
PER = E // GROUPS
ROUTED_SCALE = 2.5
CAP = 64
PAIRS = E // 2
XU = 32
XP_MAX = 12
NU = E + XU
SLOT = 6144
NSLOT = 4
KEYT = 3
KH = A_KV + B_H + C_H
BW = GRID_W + 2 * (NA_KW - 1)
BB = 6144
RPB_R, RPB_C = 2 * NA_KH - 1, 2 * NA_KW - 1

V_B, V_N1, V_N2, V_QG, V_C, V_F, V_ROWS = 0, 48, 56, 64, 66, 82, 90

C_ROT64, C_ROT32, C_MASK, C_ID, C_UP = 0, 64, 96, 224, 352
C_CUM, C_TIE, C_SLOT, C_PART, C_EVEN, C_COLS = 480, 608, 672, 736, 737, 753


def constants():
    t = np.arange(T)
    row, col = (t // GRID_W).astype(np.float32), (t % GRID_W).astype(np.float32)
    k = np.zeros((P, C_COLS), np.float32)
    for at, dim in ((C_ROT64, HD), (C_ROT32, CR)):
        n = dim // 4
        inv = (np.float32(10000.0) ** (-np.arange(n, dtype=np.float32) / np.float32(n))).astype(np.float32)
        ang = np.concatenate([row[:, None] * inv, col[:, None] * inv], axis=-1).astype(np.float32)
        k[:, at:at + dim // 2] = np.cos(ang)
        k[:, at + dim // 2:at + dim] = np.sin(ang)
    start = np.clip(np.arange(GRID_W) - NA_KW // 2, 0, GRID_W - NA_KW)
    c = t % GRID_W
    inside = (c[None, :] >= start[c][:, None]) & (c[None, :] < start[c][:, None] + NA_KW)
    k[:, C_MASK:C_MASK + T] = np.where(inside, 0.0, NEG)
    k[:, C_ID:C_ID + P] = np.eye(P)
    k[:, C_UP:C_UP + P] = np.triu(np.ones((P, P)), 1)
    k[:E, C_CUM:C_CUM + E] = np.triu(np.ones((E, E)))
    k[:E, C_CUM + E:C_CUM + 2 * E] = np.triu(np.ones((E, E)), 1)
    k[:, C_TIE:C_TIE + 64] = np.tril(np.ones((GROUPS, GROUPS)), -1).reshape(1, 64)
    k[:, C_SLOT:C_SLOT + CAP] = np.arange(1, CAP + 1)
    k[:, C_PART] = np.arange(P)
    k[:, C_EVEN:C_EVEN + 16] = 2 * np.arange(16)
    return k


def backbone(nc, I, consts, skew, O):
    y_prompt, y_sample, new_ak, new_av, new_bk, new_bv, new_ckv, new_kr = O
    ctx = ExitStack()
    with ctx:
        def sb(name, shape, dt=F32):
            return ctx.enter_context(nc.sbuf_tensor(name, shape, dt))

        def carve(buf):
            at = [0]

            def view(shape, parts=P):
                n = int(np.prod(shape))
                v = buf[0:parts, at[0]:at[0] + n]
                at[0] += n
                assert at[0] <= buf.shape[1]
                if len(shape) == 1:
                    return v
                names = "abcd"[:len(shape)]
                return v.rearrange(f"p ({' '.join(names)}) -> p {' '.join(names)}", **dict(zip(names, shape)))
            return view

        def sem(name):
            return ctx.enter_context(nc.semaphore(name))

        ring = sb("ring", [P, NSLOT, SLOT])
        xt = sb("xt", [P, KD, NG * T])
        ht = sb("ht", [P, KD, NG * T])
        wide = sb("wide", [P, NG, D])
        z = sb("z", [P, NG, IN_COLS])
        h2 = z.bitcast(BF16)[:, :, 0:3 * D].rearrange("p t (s d) -> p t s d", s=3)
        tbl = sb("tbl", [P, C_COLS])
        ones = sb("ones", [P, P])
        mhalf = sb("mhalf", [P, 4])
        vec_rows = sb("vec_rows", [V_ROWS, DEPTH, P])
        colsl = sb("colsl", [P, DEPTH, V_ROWS])
        csilu = sb("csilu", [P, KD, 32])
        ada_sb = sb("ada_sb", [P, 512])
        ctanh = sb("ctanh", [P, NG, KD])
        modl = sb("modl", [P, DEPTH, 48, NG])
        gs1 = sb("gs1", [P, KD, NG])
        gs2 = sb("gs2", [P, KD, NG])
        ms = sb("ms", [P, NG])
        rs = sb("rs", [P, NG])
        rdiag = sb("rdiag", [P, NG, T])
        w_uq = sb("w_uq", [P, 2, C_H * CD])
        w_ukv = sb("w_ukv", [P, C_H * 2 * HD])
        w_router = sb("w_router", [P, KD, E])
        rbias = sb("rbias", [P, E])
        kvg = sb("kvg", [P, CKV])
        sink = sb("sink", [P, NH])
        nsink = sb("nsink", [P, NH])
        cache = sb("cache", [P, 2 * A_KV * HD + 2 * B_H * HD + CKV + CR])
        bias_b = sb("bias_b", [P, B_H, T])
        st = sb("st", [P, 4])
        rst = sb("rst", [P, 4])
        kc_buf = sb("kc_buf", [P, KEYT * C_H * CD])
        vc_buf = sb("vc_buf", [P, KEYT * C_H * HD])
        qt_buf = sb("qt_buf", [P, NH * T])
        kt_buf = sb("kt_buf", [P, KEYT * KH * T])
        pr_buf = sb("pr_buf", [P, 2 * 512])
        kc = carve(kc_buf)([KEYT, C_H, CD])
        vc = carve(vc_buf)([KEYT, C_H, HD])
        qt = carve(qt_buf)([NH, T])
        kt = carve(kt_buf)([KEYT, KH, T])
        pr = carve(pr_buf)([2, 512])
        rtmp = carve(pr_buf)([4, 256])
        lat = carve(ht[:].rearrange("p a b -> p (a b)"))
        cqt = lat([2, NG, T])
        ckvt = lat([KEYT, T])
        qc = lat([NG, C_H, CD])
        pt = sb("pt", [P, 2, 512])
        nmax = sb("nmax", [P, NH])
        sums = sb("sums", [P, NH])
        esink = sb("esink", [P, NH])
        rden = sb("rden", [P, NH])
        route_view, plan_view = carve(kc_buf), carve(vc_buf)
        score = route_view([NG, E])
        selv = route_view([NG, E])
        repl = route_view([NG, E])
        mask = route_view([NG, E])
        top8 = route_view([NG, GROUPS, 8])
        gsc = route_view([NG, GROUPS])
        cmp1 = route_view([NG, GROUPS, GROUPS])
        cmp2 = route_view([NG, GROUPS, GROUPS])
        rank = route_view([NG, GROUPS])
        t8 = route_view([NG, 8])
        wsum = route_view([NG])
        pos1 = route_view([NG, NU])
        wu = route_view([NG, NU])
        cnt = plan_view([4], E)
        nbb = plan_view([P], E)
        cum = plan_view([2 * E], XU)
        fin = plan_view([E], XU)
        inr = plan_view([E], XU)
        ns = plan_view([E], XU)
        uv = plan_view([4], XU)
        oneh = plan_view([XU], E)
        diag = plan_view([2 * XU], XU)
        urow = plan_view([2 * XU])
        xexp = sb("xexp", [1, XU], I32)
        xcount = sb("xcount", [1, 2])
        xpairs = sb("xpairs", [1, 1], I32)
        moe_view = carve(kt_buf)
        pick = moe_view([NG * CAP]).bitcast(BF16).rearrange("p (t s) -> p t s", t=NG)
        pickw = moe_view([NG, 2 * CAP])
        xg = moe_view([KD, 2 * CAP])
        th = moe_view([DE])
        a1 = moe_view([DE])
        act_ = moe_view([NG, DE])
        sa = moe_view([512])
        ysb = moe_view([D])
        sht = moe_view([2, NG * T])

        ps = ctx.enter_context(nc.psum_tensor("ps", [P, 8, 512], F32))
        ident = tbl[:, C_ID:C_ID + P]
        xview = ps[:, 0:4, :].rearrange("p b (c n) -> p (b c) n", c=2)

        cache_ak, cache_av = cache[:, 0:128], cache[:, 128:256]
        cache_bk, cache_bv = cache[:, 256:512], cache[:, 512:768]
        cache_ckv, cache_kr = cache[:, 768:896], cache[:, 896:928]

        ADA_K = ((0, 3), (3, 6), (6, 8))
        ada_early = (0, 0)
        ada_late = [[(0, 1), (0, 2), (1, 0)], [(1, 1), (1, 2)]]
        ada_first = [1, 1 + len(ada_late[0])]
        ada_at = [[(2, 4, 5), (7, 8, 9)], [(4, 6, 8)]]
        WIN_K = ((0, 2), (2, 4), (4, 6), (6, 7), (7, 8))
        NWIN = len(WIN_K)

        tail = [("out", 0), ("out", 1), ("shared", 0)]
        entries = [(early if l == 0 else []) + [("in", i) for i in range(NWIN)]
                   + [("ada", *a, i) for a in ada_late[l] for i in range(3)] + tail
                   for l, early in enumerate([[("ada", *ada_early, i) for i in range(3)], None])]
        slots = [{e: (i - len(es)) % NSLOT for i, e in enumerate(es)} for es in entries]

        s_const = sem("s_const")
        s_x = sem("s_x")
        s_vec = sem("s_vec")
        s_small = sem("s_small")
        s_skew0, s_skew1, s_bias = sem("s_skew0"), sem("s_skew1"), sem("s_bias")
        s_zero = sem("s_zero")
        s_ent = [{e: sem("s_l%d_%s" % (l, "_".join(map(str, e)))) for e in es} for l, es in enumerate(entries)]
        s_exp = [sem(f"s_exp{q}") for q in range(NSLOT)]
        s_xw = sem("s_xw")
        s_out = sem("s_out")
        s_sp = sem("s_sp")
        s_set = sem("s_set")
        s_dve, s_act, s_pool = sem("s_dve"), sem("s_act"), sem("s_pool")
        names = ("xt_t", "xt_c", "vec_t", "cols_c", "ctanh", "csilu", "ada_mm", "ada_c", "ada_t", "ada_add", "win_mm", "mod", "sq", "ssq", "ms", "zl_mm", "rs", "rdiag", "rs_mm",
                 "hn", "ht_d", "ht_a", "z_mm", "z_d", "z_a", "stat_d", "stat_a", "stat_r", "lat_d", "kcq_t",
                 "kcq_c", "qkv_mm", "qkv_c", "rope", "qk_t", "qk_d", "qk_a", "s_mm", "nmax", "prob", "p_t", "pt_c",
                 "pv", "esum", "esink", "o", "o_t", "ot_c", "y_mm", "x1", "h2_t", "h2_a", "h2_r", "h2_m", "h2_l", "logit", "rtanh",
                 "mask", "pos_mm", "cnt_mm", "nb", "cum_mm", "inr", "one_t", "oneh", "ext_mm", "plan", "sh_mm",
                 "sh_th", "sh_a", "sh_t", "sht_c", "sh_acc", "sel", "sw", "ga", "gb", "xga", "xgb", "gu", "th", "a",
                 "tt", "sa", "y0", "y1", "ya", "yb", "low_read", "added", "x2",
                 "fin", "fin_t", "fin_c", "cval")
        S = {n: sem("s_" + n) for n in names}

        block = ctx.enter_context(nc.Block())

        def gu_of(slot, k):
            return ring[:, slot, 0:4096].rearrange("p (g k f) -> p g k f", g=2, k=KD)[:, :, k, :]

        def down_of(slot):
            return ring[:, slot, 4096:6144].rearrange("p (k d) -> p k d", k=2)

        def ada_count(ent):
            return [e for es in entries for e in es if e[0] == "ada"].index(ent) + 1

        score_groups = [(0, h, 4) for h in range(0, NH, 4)] + [(1, h, 2) for h in range(0, NH, 2)]
        NSG = len(score_groups)

        def key_head(h):
            return h // A_GROUP if h < A_H else h - A_H + A_KV

        def value_of(h, key_tile):
            if h < A_H:
                o = HD * (h // A_GROUP)
                return cache_av[:, o:o + HD] if key_tile == 2 else z[:, key_tile, O_VA + o:O_VA + o + HD]
            if h < A_H + B_H:
                o = HD * (h - A_H)
                return cache_bv[:, o:o + HD] if key_tile == 2 else z[:, key_tile, O_VB + o:O_VB + o + HD]
            return vc[:, key_tile, h - A_H - B_H, :]

        def query_of(h, t):
            if h < A_H:
                return z[:, t, O_QA + h * HD:O_QA + (h + 1) * HD]
            if h < A_H + B_H:
                o = O_QB + (h - A_H) * HD
                return z[:, t, o:o + HD]
            return qc[:, t, h - A_H - B_H, :]

        def key_of(kh, key_tile):
            if kh < A_KV:
                return cache_ak[:, kh * HD:(kh + 1) * HD] if key_tile == 2 else \
                    z[:, key_tile, O_KA + kh * HD:O_KA + (kh + 1) * HD]
            if kh < A_KV + B_H:
                o = (kh - A_KV) * HD
                return cache_bk[:, o:o + HD] if key_tile == 2 else z[:, key_tile, O_KB + o:O_KB + o + HD]
            return kc[:, key_tile, kh - A_KV - B_H, :]

        def dim_of(h):
            return HD if h < A_H + B_H else CD

        q_sets = [[("q", t, h) for h in range(0, NH, 4)] for t in range(NG)]
        k_sets = [("k", kt_, h) for kt_ in range(KEYT) for h in range(0, KH, 4)]
        NKQ = len(k_sets) + 4
        QK_T = NKQ + 4
        QK_D0, QK_A0 = (NKQ + 1) // 2, NKQ // 2
        QK_D, QK_A = QK_D0 + 2, QK_A0 + 2
        Q1_BANK = (0, 1, 6, 0)

        def copy_heads(eng, sets, n, bank, on_act):
            kind, i, h0 = sets[n]
            first_c = A_H + B_H if kind == "q" else A_KV + B_H
            runs = [(a, b) for a, b in ((h0, min(h0 + 4, first_c)), (max(h0, first_c), h0 + 4)) if a < b]
            for a, b in runs:
                wide_head = a >= first_c
                d = CD if wide_head else HD
                src = ps[0:d, bank, (a - h0) * T:(b - h0) * T].rearrange("p (h n) -> p h n", n=T)
                dst = qt[0:d, a:b, :] if kind == "q" else kt[0:d, i, a:b, :]
                scale = 1.0 if kind == "k" else (C_SCALE if wide_head else HEAD_SCALE)
                if on_act:
                    last = eng.activation(dst, src, ACT.Copy, scale=scale)
                else:
                    last = eng.tensor_scalar(dst, src, scale, None, ALU.mult)
            last.then_inc(S["qk_a" if on_act else "qk_d"], 1)

        @block.sync
        def _(sp):
            sp.dma_start(tbl[:], consts).then_inc(s_const, 16)
            sp.dma_start(wide[:, 0, :], I["x_prompt"][0]).then_inc(s_x, 16)
            sp.dma_start(wide[:, 1, :], I["x_sample"][0]).then_inc(s_x, 16)
            for l in range(DEPTH):
                for lo, src in ((V_B, I["b_ada"][l].rearrange("(r p) -> r p", p=P)),
                                (V_N1, I["norm1_g"][l].rearrange("(r p) -> r p", p=P)),
                                (V_N2, I["norm2_g"][l].rearrange("(r p) -> r p", p=P)),
                                (V_QG, I["c_q_norm_g"][l].rearrange("(r p) -> r p", p=P)),
                                (V_C, I["c_ctx"].rearrange("(r p) -> r p", p=P)),
                                (V_C + KD, I["c"][0].rearrange("(r p) -> r p", p=P)),
                                (V_F, I["final_norm_g"].rearrange("(r p) -> r p", p=P))):
                    sp.dma_start(vec_rows[lo:lo + src.shape[0], l, :], src).then_inc(s_vec, 16)
            done = xdone = 0
            for l in range(DEPTH):
                w_in, w_out = I["w_in"][l], I["w_out"][l]
                es = entries[l]
                for i, ent in enumerate(es):
                    q = slots[l][ent]
                    dst = ring[:, q, :]
                    if i < NSLOT and l:
                        if q >= 2:
                            sp.wait_ge(S["y1"], first_done)
                        else:
                            sp.wait_ge(S["y1"], done)
                    if i >= NSLOT:
                        before = es[i - NSLOT]
                        if before[0] == "ada":
                            sp.wait_ge(S["ada_mm"], ada_count(before))
                        elif before[0] == "in":
                            sp.wait_ge(S["win_mm"], NWIN * l + before[1] + 1)
                    if ent[0] == "ada":
                        _, al, third, part = ent
                        k0, k1 = ADA_K[part]
                        sp.dma_start(dst[:, 0:(k1 - k0) * 2048].rearrange("p (k n) -> p k n", k=k1 - k0),
                                     I["w_ada"][al, k0 * P:k1 * P, third * 2048:(third + 1) * 2048]
                                     .rearrange("(k p) n -> p k n", p=P)).then_inc(s_ent[l][ent], 16)
                    elif ent[0] == "in":
                        k0, k1 = WIN_K[ent[1]]
                        sp.dma_start(dst[:, 0:(k1 - k0) * IN_COLS].rearrange("p (k n) -> p k n", k=k1 - k0),
                                     w_in[k0 * P:k1 * P, :].rearrange("(k p) n -> p k n", p=P)
                                     ).then_inc(s_ent[l][ent], 16)
                    elif ent[0] == "out":
                        k0 = 4 * ent[1]
                        sp.dma_start(dst[:, 0:4 * D].rearrange("p (k n) -> p k n", k=4),
                                     w_out[k0 * P:(k0 + 4) * P, :].rearrange("(k p) n -> p k n", p=P)
                                     ).then_inc(s_ent[l][ent], 16)
                    else:
                        for g, name in enumerate(("sh_w_gate", "sh_w_up")):
                            sp.dma_start(dst[:, g * 2048:(g + 1) * 2048].rearrange("p (k f) -> p k f", k=KD),
                                         I[name][l].rearrange("(k p) f -> p k f", p=P)).then_inc(s_ent[l][ent], 16)
                        sp.dma_start(down_of(q), I["sh_w_down"][l].rearrange("(k p) d -> p k d", p=P)
                                     ).then_inc(s_ent[l][ent], 16)

                def settle():
                    sp.sem_inc(s_sp, 1)

                def load_expert(e, q, landed):
                    sp.dma_start(ring[:, q, 0:2048],
                                 I["exp_w_gate"][l, e, :, :].rearrange("(p k) f -> p (k f)", k=KD)).then_inc(landed, 16)
                    sp.dma_start(ring[:, q, 2048:4096],
                                 I["exp_w_up"][l, e, :, :].rearrange("(p k) f -> p (k f)", k=KD)).then_inc(landed, 16)
                    sp.dma_start(down_of(q),
                                 I["exp_w_down"][l, e, :, :].rearrange("(k p) d -> p k d", p=P)).then_inc(landed, 16)

                before = es[-4]
                sp.wait_ge(S["ada_mm"] if before[0] == "ada" else S["win_mm"],
                           ada_count(before) if before[0] == "ada" else NWIN * l + before[1] + 1)
                load_expert(0, 0, s_exp[0])
                sp.wait_ge(S["y_mm"], 4 * l + 4)
                load_expert(1, 1, s_exp[1])
                load_expert(2, 2, s_exp[2])
                sp.wait_ge(S["sh_acc"], l + 1)
                load_expert(3, 3, s_exp[3])
                with sp.Fori(0, E // NSLOT - 1) as r:
                    for q in range(NSLOT):
                        if q % 2 == 0:
                            sp.wait_ge(S["y1"], 2 * r + (done + q // 2 + 1))
                            settle()
                        load_expert(4 * r + (NSLOT + q), q, s_exp[q])
                first_done = done + PAIRS
                sp.wait_ge(S["plan"], 2 * l + 2)
                extra = sp.value_load(xpairs[0:1, 0:1], min_val=1, max_val=XP_MAX)
                with sp.Fori(0, extra) as x:
                    e = [sp.value_load(xexp[0:1, bass.ds(2 * x + q, 1)], min_val=0, max_val=E - 1) for q in range(2)]
                    sp.wait_ge(S["low_read"], x + (xdone + PAIRS // 2 * (l + 1)))
                    settle()
                    for q in range(2):
                        load_expert(e[q], q, s_xw)
                done, xdone = extra + (done + PAIRS), extra + xdone

        @block.gpsimd
        def _(pool):
            def small_loads(l):
                for dst, src in ((w_uq[:], I["c_w_uq"][l].rearrange("(k p) n -> p k n", p=P)),
                                 (w_ukv[:], I["c_w_ukv"][l]),
                                 (w_router[:], I["router_w"][l].rearrange("(k p) n -> p k n", p=P)),
                                 (rbias[:], I["router_bias"][l:l + 1, :].to_broadcast([P, E])),
                                 (kvg[:], I["c_kv_norm_g"][l:l + 1, :].to_broadcast([P, CKV])),
                                 (sink[:, 0:A_H], I["a_sink"][l:l + 1, :].to_broadcast([P, A_H])),
                                 (cache_ak, I["cache_a_k"][0, l].rearrange("t h d -> t (h d)")),
                                 (cache_av, I["cache_a_v"][0, l].rearrange("t h d -> t (h d)")),
                                 (cache_bk, I["cache_b_k"][0, l].rearrange("t h d -> t (h d)")),
                                 (cache_bv, I["cache_b_v"][0, l].rearrange("t h d -> t (h d)")),
                                 (cache_ckv, I["cache_c_kv"][0, l]),
                                 (cache_kr, I["cache_c_krope"][0, l])):
                    pool.dma_start(dst, src).then_inc(s_small, 16)

            def bias_table(l):
                for h in range(B_H):
                    for r in range(3):
                        out = bass.AP(skew.tensor, skew.offset + (h * 3 + r) * BB,
                                      [[BW + 1, GRID_W], [1, RPB_C]])
                        rr = NA_KH - ROWS + r
                        src = I["b_rpb"][l, h, rr:rr + 1, :].to_broadcast([GRID_W, RPB_C])
                        pool.dma_start(out, src).then_inc(s_skew1, 16)

            pool.memset(ones[:], 1.0).then_inc(s_set, 1)
            pool.memset(mhalf[:], -0.5).then_inc(s_set, 1)
            pool.memset(csilu[:], 0.0).then_inc(s_set, 1)
            pool.memset(sink[:], NEG).then_inc(s_set, 1)
            pool.memset(xg[:], 0.0).then_inc(s_set, 1)
            pool.wait_ge(s_set, 5)
            sz = B_H * 3 * BB
            pool.dma_start(bass.AP(skew.tensor, skew.offset, [[sz // P, P], [1, sz // P]]),
                           xg[:, :, :].rearrange("p a b -> p (a b)")[:, 0:sz // P]).then_inc(s_skew0, 16)
            small_loads(0)
            for l in range(DEPTH):
                pool.wait_ge(S["ms"], 2 * l + 1)
                pool.tensor_tensor(rs[:], ms[:], mhalf[:, 0:NG], ALU.pow).then_inc(S["rs"], 1)
                if l == 0:
                    pool.wait_ge(s_skew0, 16)
                    bias_table(0)
                pool.wait_ge(s_skew1, 16 * 12 * (l + 1))
                if l:
                    pool.wait_ge(S["o"], 2 * l)
                for r in range(ROWS):
                    for c in range(ROWS):
                        rr = c - r + ROWS - 1
                        src = bass.AP(skew.tensor, skew.offset + rr * BB + NA_KW - 1,
                                      [[BW, GRID_W], [3 * BB, B_H], [1, GRID_W]])
                        pool.dma_start(bias_b[r * GRID_W:(r + 1) * GRID_W, :, c * GRID_W:(c + 1) * GRID_W],
                                       src).then_inc(s_bias, 16)
                pool.wait_ge(S["stat_d"], l + 1)
                pool.tensor_tensor(rst[:], st[:], mhalf[:, 0:4], ALU.pow).then_inc(S["stat_r"], 1)
                pool.wait_ge(S["z_d"], 4 * l + 2)
                pool.wait_ge(S["z_a"], 4 * l + 3)
                for out, o, w in ((new_ak, O_KA, A_KV * HD), (new_av, O_VA, A_KV * HD),
                                  (new_bk, O_KB, B_H * HD), (new_bv, O_VB, B_H * HD)):
                    pool.dma_start(out[0, l].rearrange("t h d -> t (h d)"), z[:, 0, o:o + w]).then_inc(s_out, 16)
                pool.dma_start(new_kr[0, l], z[:, 0, O_KR:IN_COLS]).then_inc(s_out, 16)
                pool.wait_ge(S["lat_d"], l + 1)
                pool.dma_start(new_ckv[0, l], z[:, 0, O_CKV:O_KR]).then_inc(s_out, 16)
                pool.wait_ge(S["ms"], 2 * l + 2)
                pool.tensor_tensor(rs[:], ms[:], mhalf[:, 0:NG], ALU.pow).then_inc(S["rs"], 1)
                if l + 1 < DEPTH:
                    pool.wait_ge(S["nb"], l + 1)
                    small_loads(l + 1)
                    bias_table(l + 1)
            pool.wait_ge(S["ms"], 2 * DEPTH + 1)
            pool.tensor_tensor(rs[:], ms[:], mhalf[:, 0:NG], ALU.pow).then_inc(S["rs"], 1)
            pool.wait_ge(S["fin_c"], 2)
            pool.dma_start(y_prompt[0], wide[:, 0, :]).then_inc(s_out, 16)
            pool.dma_start(y_sample[0], wide[:, 1, :]).then_inc(s_out, 16)
            pool.wait_ge(s_out, 16 * (6 * DEPTH + 2))

        @block.tensor
        def _(pe):
            pe.wait_ge(s_const, 16)
            pe.wait_ge(s_set, 5)
            pe.wait_ge(s_x, 32)
            for c in range(KD):
                for t in range(NG):
                    last = pe.transpose(xview[:, c, t * T:(t + 1) * T], wide[:, t, c * P:(c + 1) * P], ident)
            last.then_inc(S["xt_t"], 1)

            def sum_squares(n, i, b):
                pe.wait_ge(S["sq"], 4 * (n - 1) + i + 1)
                for k in (2 * i, 2 * i + 1):
                    for g in range(NG):
                        o = (k % 4) * 256 + g * T
                        last = pe.matmul(ps[:, b, 2 * g:2 * g + 2], wide[:, k // 4, o:o + T], ones[:, 0:2],
                                         start=(k == 0 and g == 0), stop=(k == KD - 1), skip_group_check=True)
                if i == 3:
                    last.then_inc(S["ssq"], 1)

            def spread(n, b):
                pe.wait_ge(S["rdiag"], n)
                pe.matmul(ps[:, b, 256:512], ones[:], rdiag[:].rearrange("p g n -> p (g n)"),
                          start=True, stop=True).then_inc(S["rs_mm"], 1)

            pe.wait_ge(s_vec, 16 * 7 * DEPTH)
            for l in range(DEPTH):
                last = pe.transpose(ps[:, 4, l * P:l * P + V_ROWS], vec_rows[:, l, :], ident[0:V_ROWS, 0:V_ROWS])
            last.then_inc(S["vec_t"], 1)
            pe.wait_ge(S["csilu"], 1)

            def ada_part(l, third, part):
                ent = ("ada", *third, part)
                pe.wait_ge(s_ent[l][ent], 16)
                for k in range(*ADA_K[part]):
                    for q in range(4):
                        o = (k - ADA_K[part][0]) * 2048 + q * 512
                        last = pe.matmul(ps[32 * q:32 * q + 32, 7, :], csilu[:, k, :], ring[:, slots[l][ent], o:o + 512],
                                         start=(k == 0), stop=(k == KD - 1))
                last.then_inc(S["ada_mm"], 1)

            def ada_turn(n):
                pe.wait_ge(S["ada_c"], n + 1)
                for j in range(4):
                    last = pe.transpose(ps[:, 6, j * P:(j + 1) * P], ada_sb[:, j * P:(j + 1) * P], ident)
                last.then_inc(S["ada_t"], 1)

            for i in range(4):
                sum_squares(1, i, 5)
            for part in range(3):
                ada_part(0, ada_early, part)
            ada_turn(0)

            done = xdone = 0
            for l in range(DEPTH):
                if l:
                    for i in range(4):
                        sum_squares(2 * l + 1, i, 5)
                spread(2 * l + 1, 5)
                pe.wait_ge(S["ht_d"], 4 * l + 1)
                for i in range(NWIN):
                    pe.wait_ge(s_ent[l][("in", i)], 16)
                    for k in range(*WIN_K[i]):
                        if k == 1:
                            pe.wait_ge(S["ht_d"], 4 * l + 2)
                        if k == 4:
                            pe.wait_ge(S["ht_a"], 2 * l + 1)
                        order = [(t, n) for t in range(NG) for n in range(4)] if k < KD - 1 else \
                            [(0, 3), (1, 3)] + [(t, n) for t in range(NG) for n in range(3)]
                        for t, n in order:
                            if (k, t, n) == (0, 1, 0):
                                pe.wait_ge(S["hn"], 2 * l + 1)
                            o = (k - WIN_K[i][0]) * IN_COLS + n * NZ
                            last = pe.matmul(ps[:, 4 * t + n, 0:NZ], ht[:, k, t * T:(t + 1) * T],
                                             ring[:, slots[l][("in", i)], o:o + NZ],
                                             start=(k == 0), stop=(k == KD - 1))
                            if k == KD - 1:
                                if (t, n) == (1, 3):
                                    last.then_inc(S["zl_mm"], 1)
                                elif n == 2:
                                    last.then_inc(S["z_mm"] if t == 0 else S["win_mm"], 1)
                    if i < NWIN - 1:
                        last.then_inc(S["win_mm"], 1)
                pe.wait_ge(S["z_d"], 4 * l + 1)
                pe.wait_ge(S["z_a"], 4 * l + 1)
                pe.wait_ge(S["lat_d"], l + 1)
                for t in range(NG):
                    for c in range(2):
                        last = pe.transpose(ps[:, 0, (2 * c + t) * T:(2 * c + t + 1) * T],
                                            z[:, t, O_CQ + c * P:O_CQ + (c + 1) * P], ident)
                last.then_inc(S["kcq_t"], 1)
                pe.wait_ge(s_small, 16 * 12 * (l + 1))
                for i in range(KEYT):
                    src = cache_ckv if i == 2 else z[:, i, O_CKV:O_KR]
                    last = pe.transpose(ps[:, 1, i * T:(i + 1) * T], src, ident)
                last.then_inc(S["kcq_t"], 1)
                pe.wait_ge(S["z_d"], 4 * l + 4)
                pe.wait_ge(S["z_a"], 4 * l + 4)
                ada_part(l, ada_late[l][0], 0)
                ada_part(l, ada_late[l][0], 1)
                pe.wait_ge(S["kcq_c"], 2 * l + 2)
                half = C_H * CD // 2
                for t in range(NG):
                    for n in range(2):
                        for c in range(2):
                            last = pe.matmul(ps[:, 2 + 2 * t + n, 0:half], cqt[:, c, t, :],
                                             w_uq[:, c, n * half:(n + 1) * half], start=(c == 0), stop=(c == 1))
                    last.then_inc(S["qkv_mm"], 1)
                for i in range(KEYT):
                    b = 2 * i
                    if i:
                        pe.wait_ge(S["qkv_c"], 5 * l + i)
                    for n in range(2):
                        last = pe.matmul(ps[:, b + n, 0:384], ckvt[:, i, :], w_ukv[:, n * 384:(n + 1) * 384],
                                         start=True, stop=True)
                    last.then_inc(S["qkv_mm"], 1)
                ada_part(l, ada_late[l][0], 2)
                sets = k_sets + q_sets[0] + q_sets[1]
                pe.wait_ge(S["rope"], l + 1)
                pe.wait_ge(S["qkv_c"], 5 * l + 5)

                def head_set(n):
                    kind, i, h0 = sets[n]
                    if n >= 6:
                        if n % 2 == 0:
                            pe.wait_ge(S["qk_d"], QK_D * l + (n - 6) // 2 + 1)
                        else:
                            pe.wait_ge(S["qk_a"], QK_A * l + (n - 6) // 2 + 1)
                    for j in range(4):
                        if kind == "q":
                            src, d = query_of(h0 + j, i), dim_of(h0 + j)
                        else:
                            src = key_of(h0 + j, i)
                            d = HD if h0 + j < A_KV + B_H else CD
                        last = pe.transpose(ps[0:d, n % 6, j * T:(j + 1) * T], src, ident)
                    last.then_inc(S["qk_t"], 1)

                for n in range(NKQ):
                    head_set(n)
                pe.wait_ge(S["qk_d"], QK_D * l + QK_D0)
                pe.wait_ge(S["qk_a"], QK_A * l + QK_A0)
                ada_turn(ada_first[l])

                def scores(n):
                    t, h0, nh = score_groups[n]
                    b = n % 2
                    tiles = (0,) if t == 0 else (1, 2)
                    if n >= 2:
                        pe.wait_ge(S["prob"], NSG * l + n - 1)
                    for j in range(nh):
                        h = h0 + j
                        d = dim_of(h)
                        for m, i in enumerate(tiles):
                            o = (j * len(tiles) + m) * T
                            last = pe.matmul(ps[:, b, o:o + T], qt[0:d, h, :], kt[0:d, i, key_head(h), :],
                                             start=True, stop=True)
                    last.then_inc(S["s_mm"], 1)

                def probs_by_key(n):
                    pe.wait_ge(S["prob"], NSG * l + n + 1)
                    for j in range(4):
                        last = pe.transpose(ps[:, 2 + n % 2, j * T:(j + 1) * T], pr[:, n % 2, j * T:(j + 1) * T], ident)
                    last.then_inc(S["p_t"], 1)

                def weighted_values(n):
                    t, h0, nh = score_groups[n]
                    tiles = (0,) if t == 0 else (1, 2)
                    pe.wait_ge(S["pt_c"], NSG * l + n + 1)
                    if n == 4:
                        pe.wait_ge(S["o"], 2 * l + 1)
                    for j in range(nh):
                        h = h0 + j
                        for m, i in enumerate(tiles):
                            o = (j * len(tiles) + m) * T
                            last = pe.matmul(ps[:, 4 + h // 8, (h % 8) * HD:(h % 8 + 1) * HD],
                                             pt[:, n % 2, o:o + T], value_of(h, i),
                                             start=(m == 0), stop=(m == len(tiles) - 1))
                    last.then_inc(S["pv"], 1)

                scores(0)
                scores(1)
                for n in range(NSG):
                    probs_by_key(n)
                    if n + 2 < 4:
                        scores(n + 2)
                    if n >= 1 and n != 4:
                        weighted_values(n - 1)
                    if n == 3:
                        weighted_values(3)
                        pe.wait_ge(S["ada_add"], ada_first[l] + 1)
                        for m in range(4):
                            kind, i, h0 = q_sets[1][m]
                            if m == 3:
                                pe.wait_ge(S["qk_d"], QK_D * l + QK_D0 + 1)
                            for j in range(4):
                                last = pe.transpose(ps[0:dim_of(h0 + j), Q1_BANK[m], j * T:(j + 1) * T],
                                                    query_of(h0 + j, i), ident)
                            last.then_inc(S["qk_t"], 1)
                        pe.wait_ge(S["qk_d"], QK_D * (l + 1))
                        pe.wait_ge(S["qk_a"], QK_A * (l + 1))
                        scores(4)
                        scores(5)
                    if n >= 4 and n + 2 < NSG:
                        scores(n + 2)
                    for i, at in enumerate(ada_at[l]):
                        if n == at[-1] + 2:
                            ada_turn(ada_first[l] + 1 + i)
                    for i, at in enumerate(ada_at[l]):
                        if n in at:
                            ada_part(l, ada_late[l][1 + i], at.index(n))
                weighted_values(NSG - 1)
                for t in range(NG):
                    pe.wait_ge(S["o"], 2 * l + t + 1)
                    for c in range(KD):
                        last = pe.transpose(xview[:, c, t * T:(t + 1) * T], wide[:, t, c * P:(c + 1) * P], ident)
                last.then_inc(S["o_t"], 1)
                pe.wait_ge(S["ot_c"], 2 * l + 2)
                pe.wait_ge(S["ada_add"], ada_first[l] + len(ada_late[l]))
                for i in range(2):
                    pe.wait_ge(s_ent[l][("out", i)], 16)
                for c in range(KD):
                    for k in range(KD):
                        w = ring[:, slots[l][("out", k // 4)], (k % 4) * D + c * P:(k % 4) * D + (c + 1) * P]
                        last = pe.matmul(ps[:, 4 + c // 2, (c % 2) * 256:(c % 2) * 256 + 256], w, ht[:, k, :],
                                         start=(k == 0), stop=(k == KD - 1))
                    if c % 2 == 1:
                        last.then_inc(S["y_mm"], 1)
                        if c > 1:
                            sum_squares(2 * l + 2, c // 2 - 1, 0)
                sum_squares(2 * l + 2, 3, 0)
                spread(2 * l + 2, 0)
                for k in range(KD):
                    if k < 2:
                        pe.wait_ge(S["ht_d"], 4 * l + 3 + k)
                    if k == 4:
                        pe.wait_ge(S["ht_a"], 2 * l + 2)
                    for t in range(NG):
                        last = pe.matmul(ps[:, 4, t * E:(t + 1) * E], ht[:, k, t * T:(t + 1) * T], w_router[:, k, :],
                                         start=(k == 0 and t == 0), stop=(k == KD - 1), skip_group_check=True)
                last.then_inc(S["logit"], 1)
                for t in range(NG):
                    for c in range(KD):
                        last = pe.transpose(ps[:, 2 * t + c // 4, (c % 4) * P:(c % 4 + 1) * P],
                                            ht[:, c, t * T:(t + 1) * T], ident)
                    last.then_inc(S["h2_t"], 1)
                pe.wait_ge(s_ent[l][("shared", 0)], 48)
                q = slots[l][("shared", 0)]
                for t in range(NG):
                    for k in range(KD):
                        last = pe.matmul(ps[:, 6 + t, :], ht[:, k, t * T:(t + 1) * T], gu_of(q, k),
                                         start=(k == 0), stop=(k == KD - 1))
                    last.then_inc(S["sh_mm"], 1)
                    if t:
                        break
                    pe.wait_ge(S["mask"], l + 1)
                    pe.matmul(ps[:, 4, 0:E], tbl[:, C_UP:C_UP + P], mask[:, 0, :], start=True, stop=True)
                    pe.matmul(ps[:, 4, E:2 * E], tbl[:, C_UP:C_UP + P], mask[:, 1, :], start=True, stop=False)
                    pe.matmul(ps[:, 4, E:2 * E], ones[:], mask[:, 0, :], start=False, stop=True)\
                        .then_inc(S["pos_mm"], 1)
                    for i in range(NG):
                        last = pe.matmul(ps[0:E, 5, 0:2], mask[:, i, :], ones[:, 0:2], start=(i == 0), stop=(i == 1))
                    last.then_inc(S["cnt_mm"], 1)
                pe.wait_ge(S["nb"], l + 1)
                pe.matmul(ps[0:XU, 5, 128:128 + 2 * E], nbb[:, 0:XU], tbl[0:E, C_CUM:C_CUM + 2 * E],
                          start=True, stop=True).then_inc(S["cum_mm"], 1)
                pe.wait_ge(S["sh_a"], 2 * l + 1)
                for i in range(4):
                    src = (pos1 if i < 2 else wu)[:, i % 2, 0:E]
                    last = pe.transpose(ps[0:E, 6, i * T:(i + 1) * T], src, ident)
                last.then_inc(S["ext_mm"], 1)
                pe.wait_ge(S["sh_a"], 2 * l + 2)
                for t in range(NG):
                    for c in range(2):
                        last = pe.transpose(ps[:, 7, c * 256 + t * T:c * 256 + (t + 1) * T],
                                            act_[:, t, c * P:(c + 1) * P], ident)
                last.then_inc(S["sh_t"], 1)
                pe.wait_ge(S["sht_c"], l + 1)
                pe.wait_ge(S["h2_a"], 2 * l + 2)
                for c in range(KD):
                    for k in range(2):
                        last = pe.matmul(xview[:, c, :], down_of(q)[:, k, c * P:(c + 1) * P], sht[:, k, :],
                                         start=(c % 2 == 0 and k == 0), stop=(k == 1), skip_group_check=True)
                last.then_inc(S["sh_acc"], 1)
                pe.wait_ge(S["inr"], l + 1)
                pe.transpose(ps[0:E, 5, 0:XU], inr[:], ident[0:XU, 0:XU]).then_inc(S["one_t"], 1)
                pe.matmul(ps[:, 5, 64:64 + 2 * XU], ones[0:XU, :], diag[:], start=True, stop=True)\
                    .then_inc(S["one_t"], 1)
                pe.wait_ge(S["oneh"], l + 1)
                for i in range(4):
                    last = pe.matmul(ps[:, 7, i * XU:(i + 1) * XU], sa[0:E, i * T:(i + 1) * T], oneh[:],
                                     start=True, stop=True)
                last.then_inc(S["ext_mm"], 1)

                def gather(G):
                    pe.wait_ge(S["sel"], G + 1)
                    yield
                    for b in range(2):
                        for c in range(4 * b, 4 * b + 4):
                            for t in range(NG):
                                for i in range(3):
                                    last = pe.matmul(ps[:, 4 + b, (c % 4) * P:(c % 4 + 1) * P],
                                                     h2[:, t, i, c * P:(c + 1) * P], pick[:, t, :],
                                                     start=(t == 0 and i == 0), stop=(t == 1 and i == 2))
                        last.then_inc(S["ga" if b == 0 else "gb"], 1)
                        yield

                def pair(J, at, landed, count):
                    G = J + l
                    pe.wait_ge(S["xga"], G + 1)
                    pe.wait_ge(S["xgb"], G + 1)
                    for s in landed:
                        pe.wait_ge(s, count)
                    for k in range(KD):
                        for e in range(2):
                            last = pe.matmul(ps[CAP * e:CAP * (e + 1), 6, :], xg[:, k, CAP * e:CAP * (e + 1)],
                                             gu_of(at[e], k), start=(k == 0), stop=(k == KD - 1))
                    last.then_inc(S["gu"], 1)
                    g = gather(G + 1)
                    next(g)
                    next(g)
                    pe.wait_ge(S["sw"], G + 1)
                    pe.wait_ge(S["a"], J + 1)
                    for t in range(NG):
                        pe.transpose(ps[:, 7, t * T:(t + 1) * T], pickw[:, t, :], ident)
                    for c in range(2):
                        last = pe.transpose(ps[:, 7, 256 + c * P:256 + (c + 1) * P], act_[:, 0, c * P:(c + 1) * P], ident)
                    last.then_inc(S["tt"], 1)
                    next(g)
                    pe.wait_ge(S["sa"], J + 1)
                    for b in range(2):
                        pe.wait_ge(S["xga" if b == 0 else "xgb"], G + 2)
                        for k in range(2):
                            for e in range(2):
                                last = pe.matmul(ps[CAP * e:CAP * (e + 1), 4 + b, :],
                                                 sa[:, 256 + k * P + CAP * e:256 + k * P + CAP * (e + 1)],
                                                 down_of(at[e])[:, k, b * 512:(b + 1) * 512],
                                                 start=(k == 0), stop=(k == 1))
                        last.then_inc(S["y0" if b == 0 else "y1"], 1)
                    for c in range(KD):
                        if c % 4 == 0:
                            pe.wait_ge(S["ya" if c == 0 else "yb"], J + 1)
                        last = pe.matmul(xview[:, c, :], ysb[:, c * P:(c + 1) * P], sa[:, 0:NG * T],
                                         start=False, stop=True, skip_group_check=True)
                        if c == 0 and at[0] == 0:
                            last.then_inc(S["low_read"], 1)
                    last.then_inc(S["added"], 1)

                pe.wait_ge(S["plan"], 2 * l + 2)
                pe.wait_ge(S["h2_l"], 2 * l + 2)
                for _ in gather(done + l):
                    pass
                with pe.Fori(0, PAIRS // 2) as r:
                    for b in range(2):
                        pair(2 * r + (done + b), (2 * b, 2 * b + 1), s_exp[2 * b:2 * b + 2],
                             48 * r + 48 * (l * PAIRS // 2 + 1))
                extra = pe.value_load(xpairs[0:1, 0:1], min_val=1, max_val=XP_MAX)
                with pe.Fori(0, extra) as x:
                    pair(x + (done + PAIRS), (0, 1), [s_xw], (x + (xdone + 1)) * 96)
                done, xdone = extra + (done + PAIRS), extra + xdone
                pe.wait_ge(S["xga"], done + l + 1)
                pe.wait_ge(S["xgb"], done + l + 1)
            for i in range(4):
                sum_squares(2 * DEPTH + 1, i, 5)
            spread(2 * DEPTH + 1, 5)
            pe.wait_ge(S["fin"], 1)
            for t in range(NG):
                for c in range(KD):
                    last = pe.transpose(ps[:, 2 * t + c // 4, (c % 4) * P:(c % 4 + 1) * P],
                                        ht[:, c, t * T:(t + 1) * T], ident)
                last.then_inc(S["fin_t"], 1)

        @block.scalar
        def _(act):
            own = [0]

            def then(ins):
                own[0] += 1
                ins.then_inc(s_act, 1)
                act.wait_ge(s_act, own[0])

            def squares(stream, at):
                for i in range(4):
                    act.wait_ge(stream, at + i + 1 if stream is not S["xt_c"] else 2)
                    act.activation(wide[:].rearrange("p a b -> p (a b)")[:, i * 512:(i + 1) * 512],
                                   xt[:].rearrange("p a b -> p (a b)")[:, i * 512:(i + 1) * 512],
                                   ACT.Square).then_inc(S["sq"], 1)

            act.wait_ge(S["xt_t"], 1)
            act.activation(xt[:, 4:8, :], xview[:, 4:8, :], ACT.Copy).then_inc(S["xt_c"], 1)
            done = xdone = 0
            for l in range(DEPTH):
                mod = modl[:, l]
                squares(S["x2"] if l else S["xt_c"], 4 * (l - 1))
                if l == 0:
                    act.wait_ge(S["cols_c"], 1)
                    act.activation(ctanh[:].rearrange("p a b -> p (a b)"), colsl[:, 0, V_C:V_C + 2 * KD], ACT.Tanh,
                                   scale=0.5).then_inc(S["ctanh"], 1)
                act.wait_ge(S["hn"], 2 * l + 1)
                act.wait_ge(S["mod"], 2 * l + 1)
                for c in range(4, KD):
                    for g in range(NG):
                        last = act.activation(ht[:, c, g * T:(g + 1) * T], ht[:, c, g * T:(g + 1) * T], ACT.Identity,
                                              scale=gs1[:, c, g:g + 1], bias=mod[:, c, g:g + 1])
                last.then_inc(S["ht_a"], 1)
                act.wait_ge(S["zl_mm"], l + 1)
                for t in range(NG):
                    act.activation(wide[:, t, 0:CQ], ps[:, 4 * t + 3, O_CQ - 3 * NZ:O_CKV - 3 * NZ], ACT.Square,
                                   accum_out=st[:, t:t + 1])
                    last = act.activation(wide[:, t, CQ:CQ + CKV], ps[:, 4 * t + 3, O_CKV - 3 * NZ:O_KR - 3 * NZ],
                                          ACT.Square, accum_out=st[:, 2 + t:3 + t])
                last.then_inc(S["stat_a"], 1)
                for t in range(NG):
                    act.wait_ge(S["z_mm"] if t == 0 else S["win_mm"], l + 1 if t == 0 else NWIN * (l + 1))
                    act.activation(z[:, t, NZ:2 * NZ], ps[:, 4 * t + 1, 0:NZ], ACT.Copy).then_inc(S["z_a"], 1)
                act.wait_ge(S["lat_d"], l + 1)
                for t in range(NG):
                    act.activation(z[:, t, 3 * NZ:O_CQ], ps[:, 4 * t + 3, 0:O_CQ - 3 * NZ], ACT.Copy)
                    act.activation(z[:, t, O_KR:IN_COLS], ps[:, 4 * t + 3, O_KR - 3 * NZ:NZ], ACT.Copy)\
                        .then_inc(S["z_a"], 1)
                act.wait_ge(S["kcq_t"], 2 * l + 2)
                act.activation(ckvt[:].rearrange("p a b -> p (a b)"), ps[:, 1, 0:KEYT * T], ACT.Copy)\
                    .then_inc(S["kcq_c"], 1)
                sets = k_sets + q_sets[0] + q_sets[1]
                for n in range(1, NKQ, 2):
                    act.wait_ge(S["qk_t"], QK_T * l + n + 1)
                    copy_heads(act, sets, n, n % 6, True)
                def probs(n):
                    t, h0, nh = score_groups[n]
                    w = 512 // nh
                    act.wait_ge(S["nmax"], NSG * l + n + 1)
                    if n >= 2:
                        act.wait_ge(S["p_t"], NSG * l + n - 1)
                    for j in range(nh):
                        last = act.activation(pr[:, n % 2, j * w:(j + 1) * w], ps[:, n % 2, j * w:(j + 1) * w], ACT.Exp,
                                              bias=nmax[:, h0 + j:h0 + j + 1], accum_out=sums[:, h0 + j:h0 + j + 1])
                    last.then_inc(S["prob"], 1)

                def key_copy(n):
                    act.wait_ge(S["p_t"], NSG * l + n + 1)
                    if n >= 2:
                        act.wait_ge(S["pv"], NSG * l + n - 1)
                    act.activation(pt[:, n % 2, :], ps[:, 2 + n % 2, :], ACT.Copy).then_inc(S["pt_c"], 1)

                for n in range(NSG):
                    if n == 4:
                        key_copy(3)
                        act.wait_ge(S["esum"], 2 * l + 1)
                        act.activation(esink[:], esink[:], ACT.Exp).then_inc(S["esink"], 1)
                        for m in range(1, 4, 2):
                            act.wait_ge(S["qk_t"], QK_T * l + NKQ + m + 1)
                            copy_heads(act, sets, NKQ + m, Q1_BANK[m], True)
                    probs(n)
                    if n >= 1 and n != 4:
                        key_copy(n - 1)
                key_copy(NSG - 1)
                act.wait_ge(S["esum"], 2 * l + 2)
                act.activation(esink[:], esink[:], ACT.Exp).then_inc(S["esink"], 1)
                act.wait_ge(S["o_t"], l + 1)
                act.activation(ht[:, 4:8, :], xview[:, 4:8, :], ACT.Copy).then_inc(S["ot_c"], 1)
                squares(S["x1"], 4 * l)
                act.wait_ge(S["hn"], 2 * l + 2)
                act.wait_ge(S["mod"], 2 * l + 2)
                for c in range(4, KD):
                    for g in range(NG):
                        last = act.activation(ht[:, c, g * T:(g + 1) * T], ht[:, c, g * T:(g + 1) * T], ACT.Identity,
                                              scale=gs2[:, c, g:g + 1], bias=mod[:, 24 + c, g:g + 1])
                last.then_inc(S["ht_a"], 1)
                act.wait_ge(S["logit"], l + 1)
                act.activation(score[:].rearrange("p a b -> p (a b)"), ps[:, 4, 0:NG * E], ACT.Tanh, scale=0.5)\
                    .then_inc(S["rtanh"], 1)
                act.wait_ge(S["h2_t"], 2 * l + 2)
                act.wait_ge(s_out, 96 * (l + 1))
                for t in range(NG):
                    src = ps[:, 2 * t:2 * t + 2, :].rearrange("p h (m b) -> p h m b", b=8)
                    for dst in (wide[:, t, :], h2[:, t, 0, :]):
                        last = act.activation(dst.rearrange("p (b h m) -> p h m b", b=8, h=2), src, ACT.Copy)
                    last.then_inc(S["h2_a"], 1)
                for t in range(NG):
                    act.wait_ge(S["sh_mm"], 2 * l + t + 1)
                    if t:
                        act.wait_ge(S["sh_a"], 2 * l + 1)
                    act.activation(th[:], ps[:, 6 + t, 0:DE], ACT.Tanh, scale=0.5).then_inc(S["sh_th"], 1)
                    if t == 0:
                        for i in range(NG):
                            act.wait_ge(S["h2_r"], 2 * l + i + 1)
                            act.activation(h2[:, i, 1, :], wide[:, i, :], ACT.Copy).then_inc(S["h2_m"], 1)
                act.wait_ge(S["sh_t"], l + 1)
                act.activation(sht[:].rearrange("p a b -> p (a b)"), ps[:, 7, :], ACT.Copy).then_inc(S["sht_c"], 1)

                def copy_second(G):
                    act.wait_ge(S["gb"], G + 1)
                    act.activation(xg[:, 4:8, :].rearrange("p a b -> p (a b)"), ps[:, 5, :], ACT.Copy)\
                        .then_inc(S["xgb"], 1)

                def pair(J):
                    act.wait_ge(S["gu"], J + 1)
                    act.activation(th[:], ps[:, 6, 0:DE], ACT.Tanh, scale=0.5).then_inc(S["th"], 1)
                    act.wait_ge(S["tt"], J + 1)
                    act.activation(sa[:], ps[:, 7, :], ACT.Copy).then_inc(S["sa"], 1)
                    copy_second(J + (l + 1))
                    act.wait_ge(S["y1"], J + 1)
                    act.activation(ysb[:, 512:1024], ps[:, 5, :], ACT.Copy).then_inc(S["yb"], 1)

                act.wait_ge(S["plan"], 2 * l + 2)
                copy_second(done + l)
                with act.Fori(0, PAIRS) as r:
                    pair(r + done)
                extra = act.value_load(xpairs[0:1, 0:1], min_val=1, max_val=XP_MAX)
                with act.Fori(0, extra) as x:
                    pair(x + (done + PAIRS))
                done, xdone = extra + (done + PAIRS), extra + xdone
            squares(S["x2"], 4 * (DEPTH - 1))
            act.wait_ge(S["fin_t"], 2)
            act.activation(wide[:, 1, :].rearrange("p (a b) -> p a b", a=2), ps[:, 2:4, :], ACT.Copy)\
                .then_inc(S["fin_c"], 1)

        @block.vector
        def _(dve):
            own = [0]

            def then(ins):
                own[0] += 1
                ins.then_inc(s_dve, 1)
                dve.wait_ge(s_dve, own[0])

            def norm(n, b, gs=None, shift=None, mod=None):
                dve.wait_ge(S["ssq"], n)
                dve.tensor_scalar(ms[:], ps[:, b, 0:4].rearrange("p (g c) -> p g c", g=NG)[:, :, 0], 1.0 / D, EPS,
                                  ALU.mult, ALU.add).then_inc(S["ms"], 1)
                dve.wait_ge(S["rs"], n)
                for g in range(NG):
                    last = dve.tensor_scalar(rdiag[:, g, :], ident, rs[:, g:g + 1], None, ALU.mult)
                last.then_inc(S["rdiag"], 1)
                dve.wait_ge(S["rs_mm"], n)
                rsb = ps[:, b, 256:512].unsqueeze(1).to_broadcast([P, 4, NG * T])
                def shape(chunks):
                    for c in chunks:
                        for g in range(NG):
                            last = dve.tensor_scalar(ht[:, c, g * T:(g + 1) * T], ht[:, c, g * T:(g + 1) * T],
                                                     gs[:, c, g:g + 1], mod[:, shift + c, g:g + 1], ALU.mult, ALU.add)
                    last.then_inc(S["ht_d"], 1)

                then(dve.tensor_tensor(ht[:, 0:4, :], xt[:, 0:4, :], rsb, ALU.mult))
                if gs is not None:
                    shape([0])
                dve.tensor_tensor(ht[:, 4:8, :], xt[:, 4:8, :], rsb, ALU.mult).then_inc(S["hn"], 1)
                if gs is not None:
                    shape([1, 2, 3])

            dve.wait_ge(S["xt_t"], 1)
            dve.tensor_copy(xt[:, 0:4, :], xview[:, 0:4, :]).then_inc(S["xt_c"], 1)
            dve.wait_ge(S["vec_t"], 1)
            dve.tensor_copy(colsl[:], ps[:, 4, 0:DEPTH * P].rearrange("p (l r) -> p l r", l=DEPTH)[:, :, 0:V_ROWS])\
                .then_inc(S["cols_c"], 1)
            dve.wait_ge(S["ctanh"], 1)
            dve.wait_ge(s_set, 5)
            then(dve.scalar_tensor_tensor(ctanh[:].rearrange("p a b -> p (a b)"),
                                          ctanh[:].rearrange("p a b -> p (a b)"), 1.0,
                                          colsl[:, 0, V_C:V_C + 2 * KD], ALU.add, ALU.mult))
            dve.tensor_scalar(csilu[:, :, 0:NG].rearrange("p k g -> p g k"), ctanh[:], 0.5, None, ALU.mult)\
                .then_inc(S["csilu"], 1)

            def ada_copy(n):
                dve.wait_ge(S["ada_mm"], 3 * (n + 1))
                dve.tensor_copy(ada_sb[:], ps[:, 7, :]).then_inc(S["ada_c"], 1)

            def ada_add(n):
                al, third = ([ada_early] + ada_late[0] + ada_late[1])[n]
                dve.wait_ge(S["ada_t"], n + 1)
                lo = 16 * third
                dve.tensor_tensor(modl[:, al, lo:lo + 16, :].rearrange("p (q j) g -> p j q g", q=4),
                                  ps[:, 6, :].rearrange("p (j q r) -> p j q r", j=4, q=4)[:, :, :, 0:NG],
                                  colsl[:, al, V_B + lo:V_B + lo + 16].rearrange("p (q j) -> p j q", q=4).unsqueeze(3)
                                  .to_broadcast([P, 4, 4, NG]), ALU.add).then_inc(S["ada_add"], 1)

            def gains(l, gs, at, gain):
                dve.scalar_tensor_tensor(gs[:], modl[:, l, at:at + KD, :], 1.0,
                                         colsl[:, l, gain:gain + KD].unsqueeze(2).to_broadcast([P, KD, NG]),
                                         ALU.add, ALU.mult).then_inc(S["mod"], 1)
                dve.wait_ge(S["mod"], 2 * l + (1 if gs is gs1 else 2))

            ada_copy(0)
            ada_add(0)
            dve.wait_ge(S["ada_add"], 1)
            gains(0, gs1, 8, V_N1)
            done = xdone = 0
            for l in range(DEPTH):
                mod, cols = modl[:, l], colsl[:, l]
                if l:
                    gains(l, gs1, 8, V_N1)
                norm(2 * l + 1, 5, gs1, 0, mod)
                dve.wait_ge(S["stat_a"], l + 1)
                dve.tensor_scalar(st[:, 0:2], st[:, 0:2], 1.0 / CQ, EPS, ALU.mult, ALU.add)
                dve.tensor_scalar(st[:, 2:4], st[:, 2:4], 1.0 / CKV, EPS, ALU.mult, ALU.add).then_inc(S["stat_d"], 1)
                dve.wait_ge(s_small, 16 * 12 * (l + 1))
                dve.tensor_scalar(nsink[:], sink[:], -1.0, None, ALU.mult)

                def move_z(t, n):
                    dve.tensor_copy(z[:, t, n * NZ:(n + 1) * NZ], ps[:, 4 * t + n, 0:NZ]).then_inc(S["z_d"], 1)

                dve.wait_ge(S["z_mm"], l + 1)
                move_z(0, 0)
                dve.wait_ge(S["stat_r"], l + 1)
                for t in range(NG):
                    dve.tensor_scalar(z[:, t, O_CQ:O_CKV], ps[:, 4 * t + 3, O_CQ - 3 * NZ:O_CKV - 3 * NZ],
                                      rst[:, t:t + 1], None, ALU.mult)
                    last = dve.scalar_tensor_tensor(z[:, t, O_CKV:O_KR],
                                                    ps[:, 4 * t + 3, O_CKV - 3 * NZ:O_KR - 3 * NZ],
                                                    rst[:, 2 + t:3 + t], kvg[:], ALU.mult, ALU.mult)
                last.then_inc(S["lat_d"], 1)
                move_z(0, 2)
                dve.wait_ge(S["win_mm"], NWIN * (l + 1))
                move_z(1, 0)
                move_z(1, 2)
                dve.wait_ge(s_bias, 64 * (l + 1))
                dve.wait_ge(s_const, 16)
                dve.tensor_tensor(bias_b[:], bias_b[:],
                                  tbl[:, C_MASK:C_MASK + T].unsqueeze(1).to_broadcast([P, B_H, T]), ALU.add)
                dve.wait_ge(S["z_d"], 4 * l + 4)
                dve.wait_ge(S["z_a"], 4 * l + 4)

                def rotate(x, at, width, heads, signal=None):
                    cos = tbl[:, at:at + width].unsqueeze(1).to_broadcast([P, heads, width])
                    sin = tbl[:, at + width:at + 2 * width].unsqueeze(1).to_broadcast([P, heads, width])
                    tmp = [rtmp[:, i, 0:heads * width].rearrange("p (h w) -> p h w", h=heads) for i in range(4)]
                    dve.tensor_tensor(tmp[0], x[:, :, 0, :], cos, ALU.mult)
                    dve.tensor_tensor(tmp[1], x[:, :, 1, :], sin, ALU.mult)
                    dve.tensor_tensor(tmp[2], x[:, :, 1, :], cos, ALU.mult)
                    then(dve.tensor_tensor(tmp[3], x[:, :, 0, :], sin, ALU.mult))
                    dve.tensor_tensor(x[:, :, 0, :], tmp[0], tmp[1], ALU.subtract)
                    last = dve.tensor_tensor(x[:, :, 1, :], tmp[2], tmp[3], ALU.add)
                    if signal is None:
                        then(last)
                    else:
                        last.then_inc(signal, 1)

                rotate(z[:, 1, 0:O_VA].rearrange("p (h s w) -> p h s w", s=2, w=32), C_ROT64, 32, A_H + A_KV)
                rotate(z[:, 1, O_KR:IN_COLS].rearrange("p (h s w) -> p h s w", s=2, w=16), C_ROT32, 16, 1)
                dve.wait_ge(S["kcq_t"], 2 * l + 1)
                for c in range(2):
                    last = dve.tensor_scalar(cqt[:, c, :, :], ps[:, 0, c * 256:(c + 1) * 256]
                                             .rearrange("p (t n) -> p t n", t=NG),
                                             cols[:, V_QG + c:V_QG + c + 1], None, ALU.mult)
                last.then_inc(S["kcq_c"], 1)
                half = C_H * CD // 2
                for t in range(NG):
                    dve.wait_ge(S["qkv_mm"], 5 * l + t + 1)
                    dve.tensor_copy(qc[:, t, :, :].rearrange("p (a h) d -> p a (h d)", a=2),
                                    ps[:, 2 + 2 * t:4 + 2 * t, 0:half]).then_inc(S["qkv_c"], 1)
                for i in range(KEYT):
                    b = 2 * i
                    dve.wait_ge(S["qkv_mm"], 5 * l + i + 3)
                    for n in range(2):
                        src = ps[:, b + n, 0:384].rearrange("p (h d) -> p h d", d=2 * HD)
                        dve.tensor_copy(kc[:, i, 3 * n:3 * n + 3, 0:CN], src[:, :, 0:CN])
                        dve.tensor_copy(vc[:, i, 3 * n:3 * n + 3, :], src[:, :, CN:])
                    kr = cache_kr if i == 2 else z[:, i, O_KR:IN_COLS]
                    dve.tensor_copy(kc[:, i, :, CN:CD], kr.unsqueeze(1).to_broadcast([P, C_H, CR]))\
                        .then_inc(S["qkv_c"], 1)
                dve.wait_ge(S["qkv_c"], 5 * l + 2)
                rotate(qc[:, 1, :, CN:CD].rearrange("p h (s w) -> p h s w", s=2), C_ROT32, 16, C_H,
                       S["rope"])
                ada_copy(ada_first[l])
                sets = k_sets + q_sets[0] + q_sets[1]
                for n in range(0, NKQ, 2):
                    dve.wait_ge(S["qk_t"], QK_T * l + n + 1)
                    copy_heads(dve, sets, n, n % 6, False)

                def maxima(n):
                    t, h0, nh = score_groups[n]
                    w = 512 // nh
                    dve.wait_ge(S["s_mm"], NSG * l + n + 1)
                    b = ps[:, n % 2, :].rearrange("p (h w) -> p h w", h=nh)
                    if t == 1 and A_H <= h0 < A_H + B_H:
                        then(dve.tensor_tensor(b[:, :, 0:T], b[:, :, 0:T], bias_b[:, h0 - A_H:h0 - A_H + nh, :], ALU.add))
                    then(dve.tensor_reduce(nmax[:, h0:h0 + nh], b, AX.X, ALU.max, negate=True))
                    dve.tensor_tensor(nmax[:, h0:h0 + nh], nmax[:, h0:h0 + nh], nsink[:, h0:h0 + nh], ALU.min)\
                        .then_inc(S["nmax"], 1)

                def finish(t):
                    dve.wait_ge(S["prob"], NSG * l + (4 if t == 0 else NSG))
                    dve.wait_ge(S["nmax"], NSG * l + (4 if t == 0 else NSG))
                    dve.tensor_tensor(esink[:], sink[:], nmax[:], ALU.add).then_inc(S["esum"], 1)
                    dve.wait_ge(S["esink"], 2 * l + t + 1)
                    then(dve.tensor_tensor(sums[:], sums[:], esink[:], ALU.add))
                    then(dve.reciprocal(rden[:], sums[:]))
                    dve.wait_ge(S["pv"], NSG * l + (4 if t == 0 else NSG))
                    dve.tensor_tensor(wide[:, t, :].rearrange("p (b h d) -> p b h d", b=2, d=HD),
                                      ps[:, 4:6, :].rearrange("p b (h d) -> p b h d", d=HD),
                                      rden[:].rearrange("p (b h) -> p b h", b=2).unsqueeze(3)
                                      .to_broadcast([P, 2, 8, HD]), ALU.mult).then_inc(S["o"], 1)

                ada_add(ada_first[l])
                for n in range(NSG):
                    if n == 4:
                        finish(0)
                        for m in range(0, 4, 2):
                            dve.wait_ge(S["qk_t"], QK_T * l + NKQ + m + 1)
                            copy_heads(dve, sets, NKQ + m, Q1_BANK[m], False)
                    maxima(n)
                    for i, at in enumerate(ada_at[l]):
                        if n == at[-1] + 1:
                            ada_copy(ada_first[l] + 1 + i)
                        if n == at[-1] + 2:
                            ada_add(ada_first[l] + 1 + i)
                finish(1)
                dve.wait_ge(S["ada_add"], ada_first[l] + len(ada_late[l]))
                dve.wait_ge(S["o_t"], l + 1)
                dve.tensor_copy(ht[:, 0:4, :], xview[:, 0:4, :]).then_inc(S["ot_c"], 1)
                for c in range(KD):
                    if c % 2 == 0:
                        dve.wait_ge(S["y_mm"], 4 * l + c // 2 + 1)
                    for g in range(NG):
                        o = (c % 2) * 256 + g * T
                        last = dve.scalar_tensor_tensor(xt[:, c, g * T:(g + 1) * T], ps[:, 4 + c // 2, o:o + T],
                                                        mod[:, 16 + c, g:g + 1], xt[:, c, g * T:(g + 1) * T],
                                                        ALU.mult, ALU.add)
                    if c % 2 == 1:
                        last.then_inc(S["x1"], 1)
                dve.wait_ge(S["x1"], 4 * l + 4)
                gains(l, gs2, 32, V_N2)
                norm(2 * l + 2, 0, gs2, 24, mod)
                dve.wait_ge(S["rtanh"], l + 1)
                then(dve.tensor_scalar(score[:], score[:], 0.5, 0.5, ALU.mult, ALU.add))
                then(dve.tensor_tensor(selv[:], score[:], rbias[:].unsqueeze(1).to_broadcast([P, NG, E]), ALU.add))
                for t in range(NG):
                    for g in range(GROUPS):
                        last = dve.max(top8[:, t, g, :], selv[:, t, g * PER:(g + 1) * PER])
                then(last)
                then(dve.tensor_tensor(gsc[:], top8[:, :, :, 0], top8[:, :, :, 1], ALU.add))
                for t in range(NG):
                    other = gsc[:, t, :].unsqueeze(1).to_broadcast([P, GROUPS, GROUPS])
                    this = gsc[:, t, :].unsqueeze(2).to_broadcast([P, GROUPS, GROUPS])
                    dve.tensor_tensor(cmp1[:, t], other, this, ALU.is_gt)
                    then(dve.tensor_tensor(cmp2[:, t], other, this, ALU.is_equal))
                    then(dve.tensor_tensor(cmp2[:, t], cmp2[:, t],
                                           tbl[:, C_TIE:C_TIE + 64].rearrange("p (i j) -> p i j", i=GROUPS), ALU.mult))
                    then(dve.tensor_tensor(cmp1[:, t], cmp1[:, t], cmp2[:, t], ALU.add))
                then(dve.tensor_reduce(rank[:], cmp1[:], AX.X, ALU.add))
                then(dve.tensor_scalar(rank[:], rank[:], float(TOP_G), None, ALU.is_lt))
                for t in range(NG):
                    keep_t = rank[:, t, :].unsqueeze(2).to_broadcast([P, GROUPS, PER])
                    sel_t = selv[:, t, :].rearrange("p (g e) -> p g e", g=GROUPS)
                    rep_t = repl[:, t, :].rearrange("p (g e) -> p g e", g=GROUPS)
                    dve.tensor_tensor(sel_t, sel_t, keep_t, ALU.mult)
                    then(dve.tensor_scalar(rep_t, keep_t, -NEG, NEG, ALU.mult, ALU.add))
                then(dve.tensor_tensor(selv[:], selv[:], repl[:], ALU.add))
                for t in range(NG):
                    last = dve.max(t8[:, t, :], selv[:, t, :])
                then(last)
                then(dve.memset(t8[:, :, TOP_K:8], NEG))
                for t in range(NG):
                    last = dve.match_replace(repl[:, t, :], t8[:, t, :], selv[:, t, :], 3.0 * NEG)
                then(last)
                then(dve.tensor_scalar(mask[:], repl[:], 2.0 * NEG, None, ALU.is_lt))
                then(dve.tensor_scalar(repl[:], selv[:], 0.5 * NEG, None, ALU.is_gt))
                dve.tensor_tensor(mask[:], mask[:], repl[:], ALU.mult).then_inc(S["mask"], 1)
                dve.wait_ge(S["mask"], l + 1)
                then(dve.tensor_tensor(repl[:], score[:], mask[:], ALU.mult))
                then(dve.tensor_reduce(wsum[:], repl[:], AX.X, ALU.add))
                then(dve.reciprocal(wsum[:], wsum[:]))
                for t in range(NG):
                    last = dve.tensor_scalar(wu[:, t, 0:E], repl[:, t, :], wsum[:, t:t + 1], 0.5 * ROUTED_SCALE,
                                             ALU.mult, ALU.mult)
                then(last)

                def shared_act(t):
                    dve.wait_ge(S["sh_th"], 2 * l + t + 1)
                    then(dve.scalar_tensor_tensor(a1[:], th[:], 1.0, ps[:, 6 + t, 0:DE], ALU.add, ALU.mult))
                    dve.scalar_tensor_tensor(act_[:, t, :], a1[:], 0.5, ps[:, 6 + t, DE:2 * DE], ALU.mult, ALU.mult)\
                        .then_inc(S["sh_a"], 1)

                shared_act(0)
                dve.wait_ge(S["pos_mm"], l + 1)
                for t in range(NG):
                    last = dve.scalar_tensor_tensor(pos1[:, t, 0:E], ps[:, 4, t * E:(t + 1) * E], 1.0, mask[:, t, :],
                                                    ALU.add, ALU.mult)
                then(last)
                dve.wait_ge(S["cnt_mm"], l + 1)
                for i in range(1, NG * T // CAP):
                    last = dve.tensor_scalar(cnt[:, i - 1:i], ps[0:E, 5, 0:1], i * CAP + 0.5, None, ALU.is_gt)
                then(last)
                then(dve.tensor_tensor(cnt[:, 0:1], cnt[:, 0:1], cnt[:, 1:2], ALU.add))
                then(dve.tensor_tensor(cnt[:, 0:1], cnt[:, 0:1], cnt[:, 2:3], ALU.add))
                dve.tensor_scalar(nbb[:], ones[0:E, :], cnt[:, 0:1], None, ALU.mult).then_inc(S["nb"], 1)
                for t in range(NG):
                    dve.wait_ge(S["h2_a"], 2 * l + t + 1)
                    dve.tensor_tensor(wide[:, t, :], wide[:, t, :], h2[:, t, 0, :], ALU.subtract)\
                        .then_inc(S["h2_r"], 1)
                for t in range(NG):
                    dve.wait_ge(S["h2_m"], 2 * l + t + 1)
                    dve.tensor_tensor(h2[:, t, 2, :], wide[:, t, :], h2[:, t, 1, :], ALU.subtract)\
                        .then_inc(S["h2_l"], 1)
                shared_act(1)
                dve.wait_ge(S["cum_mm"], l + 1)
                then(dve.tensor_copy(cum[:], ps[0:XU, 5, 128:128 + 2 * E]))
                number = tbl[0:XU, C_PART:C_PART + 1]
                dve.tensor_scalar(fin[:], cum[:, 0:E], number, None, ALU.is_le)
                dve.tensor_scalar(inr[:], cum[:, E:2 * E], number, None, ALU.is_le)
                then(dve.tensor_scalar(ns[:], cum[:, E:2 * E], -1.0, number, ALU.mult, ALU.add))
                then(dve.tensor_tensor(inr[:], inr[:], fin[:], ALU.subtract))
                then(dve.tensor_tensor(ns[:], ns[:], inr[:], ALU.mult))
                dve.tensor_reduce(uv[:, 0:1], ns[:], AX.X, ALU.add)
                then(dve.tensor_reduce(uv[:, 1:2], fin[:], AX.X, ALU.add))
                dve.tensor_scalar(uv[:, 2:3], uv[:, 0:1], float(CAP), float(CAP), ALU.mult, ALU.add)
                then(dve.tensor_scalar(uv[:, 3:4], uv[:, 1:2], float(E - 1), None, ALU.min))
                dve.tensor_scalar(diag[:, 0:XU], ident[0:XU, 0:XU], uv[:, 2:3], None, ALU.mult)
                dve.tensor_scalar(diag[:, XU:2 * XU], ident[0:XU, 0:XU], uv[:, 3:4], None, ALU.mult)\
                    .then_inc(S["inr"], 1)
                then(dve.tensor_scalar(fin[0:1, 0:16], tbl[0:1, C_EVEN:C_EVEN + 16], cum[0:1, E - 1:E], None,
                                       ALU.is_lt))
                then(dve.tensor_reduce(xcount[:, 0:1], fin[0:1, 0:16], AX.X, ALU.add))
                dve.tensor_scalar(xpairs[:], xcount[:, 0:1], 1.0, None, ALU.max).then_inc(S["plan"], 1)
                dve.wait_ge(S["one_t"], 2 * l + 2)
                dve.wait_ge(S["ext_mm"], 2 * l + 1)
                dve.tensor_copy(urow[:], ps[:, 5, 64:64 + 2 * XU])
                dve.tensor_copy(sa[0:E, :], ps[0:E, 6, :])
                dve.tensor_copy(oneh[:], ps[0:E, 5, 0:XU]).then_inc(S["oneh"], 1)
                dve.wait_ge(S["ext_mm"], 2 * l + 2)
                dve.wait_ge(S["oneh"], l + 1)
                for t in range(NG):
                    dve.tensor_tensor(pos1[:, t, E:NU], ps[:, 7, t * XU:(t + 1) * XU], urow[:, 0:XU], ALU.subtract)
                    dve.tensor_copy(wu[:, t, E:NU], ps[:, 7, (2 + t) * XU:(3 + t) * XU])
                dve.tensor_copy(xexp[:], urow[0:1, XU:2 * XU]).then_inc(S["plan"], 1)

                def choose(u):
                    at = pos1[:, :, bass.ds(u, 2)] if not isinstance(u, int) else pos1[:, :, u:u + 2]
                    dve.tensor_tensor(pick[:].rearrange("p t (e s) -> p t e s", e=2),
                                      tbl[:, C_SLOT:C_SLOT + CAP].unsqueeze(1).unsqueeze(1)
                                      .to_broadcast([P, NG, 2, CAP]),
                                      at.unsqueeze(3).to_broadcast([P, NG, 2, CAP]), ALU.is_equal)\
                        .then_inc(S["sel"], 1)

                def weigh(u, G):
                    at = wu[:, :, bass.ds(u, 2)] if not isinstance(u, int) else wu[:, :, u:u + 2]
                    dve.wait_ge(S["sel"], G + 1)
                    dve.tensor_tensor(pickw[:].rearrange("p t (e s) -> p t e s", e=2),
                                      pick[:].rearrange("p t (e s) -> p t e s", e=2),
                                      at.unsqueeze(3).to_broadcast([P, NG, 2, CAP]), ALU.mult).then_inc(S["sw"], 1)

                def copy_first(G):
                    dve.wait_ge(S["ga"], G + 1)
                    dve.tensor_copy(xg[:, 0:4, :].rearrange("p a b -> p (a b)"), ps[:, 4, :]).then_inc(S["xga"], 1)

                def pair(j, J):
                    G = J + l
                    dve.wait_ge(S["gb"], G + 1)
                    dve.wait_ge(S["sw"], G + 1)
                    choose(2 * j + 2)
                    dve.wait_ge(S["th"], J + 1)
                    dve.scalar_tensor_tensor(a1[:], th[:], 1.0, ps[:, 6, 0:DE], ALU.add, ALU.mult).then_inc(S["cval"], 1)
                    dve.wait_ge(S["cval"], J + 1)
                    dve.tensor_tensor(act_[:, 0, :], a1[:], ps[:, 6, DE:2 * DE], ALU.mult).then_inc(S["a"], 1)
                    copy_first(G + 1)
                    dve.wait_ge(S["tt"], J + 1)
                    weigh(2 * j + 2, G + 1)
                    dve.wait_ge(S["y0"], J + 1)
                    dve.tensor_copy(ysb[:, 0:512], ps[:, 4, :]).then_inc(S["ya"], 1)

                dve.wait_ge(S["plan"], 2 * l + 2)
                choose(0)
                weigh(0, done + l)
                copy_first(done + l)
                with dve.Fori(0, PAIRS) as r:
                    pair(r, r + done)
                extra = dve.value_load(xpairs[0:1, 0:1], min_val=1, max_val=XP_MAX)
                with dve.Fori(0, extra) as x:
                    pair(x + PAIRS, x + (done + PAIRS))
                done, xdone = extra + (done + PAIRS), extra + xdone
                dve.wait_ge(S["added"], done)
                for c in range(KD):
                    for g in range(NG):
                        last = dve.scalar_tensor_tensor(xt[:, c, g * T:(g + 1) * T], xview[:, c, g * T:(g + 1) * T],
                                                        mod[:, 40 + c, g:g + 1], xt[:, c, g * T:(g + 1) * T],
                                                        ALU.mult, ALU.add)
                    if c % 2 == 1:
                        last.then_inc(S["x2"], 1)
                dve.wait_ge(S["x2"], 4 * l + 4)
            norm(2 * DEPTH + 1, 5)
            dve.wait_ge(S["hn"], 2 * DEPTH + 1)
            for c in range(KD):
                last = dve.tensor_scalar(ht[:, c, :], ht[:, c, :], colsl[:, 0, V_F + c:V_F + c + 1], None, ALU.mult)
            last.then_inc(S["fin"], 1)
            dve.wait_ge(S["fin_t"], 2)
            dve.tensor_copy(wide[:, 0, :].rearrange("p (a b) -> p a b", a=2), ps[:, 0:2, :]).then_inc(S["fin_c"], 1)


_INS = ["x_prompt", "x_sample", "cache_a_k", "cache_a_v", "cache_b_k", "cache_b_v", "cache_c_kv", "cache_c_krope",
        "c", "c_ctx", "norm1_g", "norm2_g", "w_ada", "b_ada", "w_in", "a_sink", "b_rpb", "c_q_norm_g", "c_w_uq",
        "c_kv_norm_g", "c_w_ukv", "w_out", "router_w", "router_bias", "exp_w_gate", "exp_w_up", "exp_w_down",
        "sh_w_gate", "sh_w_up", "sh_w_down", "final_norm_g"]
_OUTS = [(1, T, D), (1, T, D), (1, DEPTH, T, A_KV, HD), (1, DEPTH, T, A_KV, HD), (1, DEPTH, T, B_H, HD),
         (1, DEPTH, T, B_H, HD), (1, DEPTH, T, CKV), (1, DEPTH, T, CR)]


def kernel(**inputs):
    import concourse.bacc as bacc
    from concourse.bass_utils import run_bass_kernel_spmd

    nc = bacc.Bacc("TRN2", target_bir_lowering=False, num_devices=1)
    arrays, aps = {}, {}
    for name in _INS:
        a = np.ascontiguousarray(inputs[name])
        arrays[f"in_{name}"] = a
        aps[name] = nc.dram_tensor(f"in_{name}", a.shape, mybir.dt.from_np(a.dtype), kind="ExternalInput").ap()
    arrays["consts"] = constants()
    consts = nc.dram_tensor("consts", (P, C_COLS), F32, kind="ExternalInput").ap()
    skew = nc.dram_tensor("skew", (B_H, 3, BB), F32, kind="Internal").ap()
    outs = [nc.dram_tensor(f"out_{i}", s, F32, kind="ExternalOutput").ap() for i, s in enumerate(_OUTS)]
    backbone(nc, aps, consts, skew, outs)
    r = run_bass_kernel_spmd(nc, [arrays], core_ids=[0])
    return tuple(r.results[0][f"out_{i}"] for i in range(len(_OUTS)))
```
